# Optimizing a Trainium2 kernel written in Bass

```python
import jax, jax.numpy as jnp
from jax import lax
import numpy as np

D_MODEL = 1024
BATCH = 1
SEQ = 1024
DEPTH = 1

HEAD_DIM = 64
RWKV_HEADS = 8
RWKV_WIDTH = RWKV_HEADS * HEAD_DIM
DECAY_LORA = 32
AAA_LORA = 32
ATTN_HEADS = 8
ATTN_WIDTH = ATTN_HEADS * HEAD_DIM
MIX_WIDTH = RWKV_WIDTH + ATTN_WIDTH
Q_RANK = 256
KV_RANK = 128
IDX_HEADS = 4
IDX_DIM = 64
TOPK_MAX = 256
Q_BLOCK = 128
NORM_EPS = 1e-6
LN_EPS = 1e-5
GN_EPS = 64e-5

SHIFT_SIZES = [RWKV_WIDTH, RWKV_WIDTH, RWKV_WIDTH, DECAY_LORA, AAA_LORA]
SHIFT_COLS = sum(SHIFT_SIZES)
IN_SIZES = [SHIFT_COLS, RWKV_WIDTH, Q_RANK, KV_RANK, IDX_DIM, IDX_HEADS, ATTN_WIDTH]
IN_COLS = sum(IN_SIZES)
SHIFT_SPLITS = np.cumsum(SHIFT_SIZES)[:-1].tolist()
IN_SPLITS = np.cumsum(IN_SIZES)[:-1].tolist()


def rmsnorm(x, g):
    xf = x.astype(jnp.float32)
    y = xf * lax.rsqrt(jnp.mean(xf * xf, axis=-1, keepdims=True) + NORM_EPS)
    return (y * g.astype(jnp.float32)).astype(x.dtype)

def layernorm(x, g, b):
    xf = x.astype(jnp.float32)
    mu = jnp.mean(xf, axis=-1, keepdims=True)
    var = jnp.mean(jnp.square(xf - mu), axis=-1, keepdims=True)
    y = (xf - mu) * lax.rsqrt(var + LN_EPS)
    return (y * g.astype(jnp.float32) + b.astype(jnp.float32)).astype(x.dtype)

def rwkv7_scan(r, decay, k, v, kk, a):
    B, T, H, D = r.shape
    tm = lambda t: jnp.moveaxis(t, 1, 0)

    def step(S, inp):
        r_t, w_t, k_t, v_t, kk_t, a_t = inp
        sa = jnp.einsum('bhij,bhj->bhi', S, -kk_t)
        S = (S * w_t[:, :, None, :]
             + sa[..., None] * (kk_t * a_t)[:, :, None, :]
             + v_t[..., None] * k_t[:, :, None, :])
        return S, jnp.einsum('bhij,bhj->bhi', S, r_t)

    S0 = jnp.zeros((B, H, D, D), jnp.float32)
    _, y = lax.scan(step, S0, (tm(r), tm(decay), tm(k), tm(v), tm(kk), tm(a)))
    return jnp.moveaxis(y, 0, 1)

def rwkv7_branch(p_shift, gate, mu_shift, w0, w_up, a0, a_up, k_k, k_a, r_k, gn_g, gn_b):
    B, T, _ = p_shift.shape
    f32 = jnp.float32
    prev = jnp.pad(p_shift, ((0, 0), (1, 0), (0, 0)))[:, :-1]
    xs = p_shift + (prev - p_shift) * mu_shift
    r, k, v, wd, ad = jnp.split(xs, SHIFT_SPLITS, axis=-1)
    wlog = -jax.nn.softplus(-(w0 + jnp.tanh(wd) @ w_up)) - 0.5
    decay = jnp.exp(-jnp.exp(wlog.astype(f32)))
    a = jax.nn.sigmoid((a0 + ad @ a_up).astype(f32))
    heads = lambda t: t.astype(f32).reshape(B, T, RWKV_HEADS, HEAD_DIM)
    r, k, v, a, decay = heads(r), heads(k), heads(v), heads(a), heads(decay)
    kk = k * k_k.astype(f32)
    kk = kk / jnp.maximum(jnp.sqrt(jnp.sum(kk * kk, axis=-1, keepdims=True)), 1e-12)
    k = k * (1.0 + (a - 1.0) * k_a.astype(f32))
    y = rwkv7_scan(r, decay, k, v, kk, a)
    mu = jnp.mean(y, axis=-1, keepdims=True)
    var = jnp.mean(jnp.square(y - mu), axis=-1, keepdims=True)
    y = (y - mu) * lax.rsqrt(var + GN_EPS) * gn_g.astype(f32) + gn_b.astype(f32)
    y = y + jnp.sum(r * k * r_k.astype(f32), axis=-1, keepdims=True) * v
    y = y.reshape(B, T, RWKV_WIDTH).astype(gate.dtype)
    return y * jax.nn.silu(gate)

def dsa_branch(q_down, kv_down, k_idx_raw, w_idx, gate, q_norm_g, kv_norm_g,
               w_uq, w_uk, w_uv, w_qidx, kidx_g, kidx_b):
    B, T, _ = q_down.shape
    f32 = jnp.float32
    c_q = rmsnorm(q_down, q_norm_g)
    c_kv = rmsnorm(kv_down, kv_norm_g)
    q = (c_q @ w_uq).reshape(B, T, ATTN_HEADS, HEAD_DIM)
    q_abs = jnp.einsum('bthd,hrd->bthr', q, w_uk) * (HEAD_DIM ** -0.5)
    q_idx = (c_q @ w_qidx).reshape(B, T, IDX_HEADS, IDX_DIM)
    k_idx = layernorm(k_idx_raw, kidx_g, kidx_b).astype(f32)
    w_i = w_idx * (IDX_HEADS ** -0.5)
    topk = min(TOPK_MAX, T // 4)
    nb = T // Q_BLOCK
    blocks = lambda t: jnp.moveaxis(t.reshape(B, nb, Q_BLOCK, *t.shape[2:]), 1, 0)
    key_pos = jnp.arange(T)

    def attend(args):
        qa, qi, wi, t0 = args
        q_pos = t0 + jnp.arange(Q_BLOCK)
        causal = key_pos[None, :] <= q_pos[:, None]
        logits = jnp.einsum('bqhd,bsd->bqhs', qi.astype(f32), k_idx)
        score = jnp.einsum('bqh,bqhs->bqs', wi.astype(f32), jax.nn.relu(logits))
        score = jnp.where(causal[None], score, -jnp.inf)
        _, idx = lax.top_k(score, topk)
        c_sel = jax.vmap(lambda c, i: c[i])(c_kv, idx).astype(f32)
        valid = idx <= q_pos[None, :, None]
        s = jnp.einsum('bqhr,bqkr->bhqk', qa.astype(f32), c_sel)
        s = jnp.where(valid[:, None], s, -jnp.inf)
        p = jax.nn.softmax(s, axis=-1)
        return jnp.einsum('bhqk,bqkr->bqhr', p, c_sel)

    o_lat = lax.map(attend, (blocks(q_abs), blocks(q_idx), blocks(w_i), jnp.arange(nb) * Q_BLOCK))
    o_lat = jnp.moveaxis(o_lat, 0, 1).reshape(B, T, ATTN_HEADS, KV_RANK).astype(gate.dtype)
    o = jnp.einsum('bthr,hrd->bthd', o_lat, w_uv).reshape(B, T, ATTN_WIDTH)
    return o * jax.nn.silu(gate)

def hybrid_layer(x, norm_g, w_in, mu_shift, w0, w_up, a0, a_up, k_k, k_a, r_k, gn_g, gn_b,
                 q_norm_g, kv_norm_g, w_uq, w_uk, w_uv, w_qidx, kidx_g, kidx_b, w_out):
    xn = rmsnorm(x, norm_g)
    p = xn @ w_in
    p_shift, g_rwkv, q_down, kv_down, k_idx_raw, w_idx, g_attn = jnp.split(p, IN_SPLITS, axis=-1)
    y_rwkv = rwkv7_branch(p_shift, g_rwkv, mu_shift, w0, w_up, a0, a_up, k_k, k_a, r_k, gn_g, gn_b)
    y_attn = dsa_branch(q_down, kv_down, k_idx_raw, w_idx, g_attn, q_norm_g, kv_norm_g,
                        w_uq, w_uk, w_uv, w_qidx, kidx_g, kidx_b)
    y = jnp.concatenate([y_rwkv, y_attn], axis=-1) @ w_out
    return x + y

def first_inputs(seed: int = 0) -> dict:
    key = jax.random.key(seed)
    ks = jax.random.split(key, 24)
    L = DEPTH
    f32 = jnp.float32
    nrm = lambda k, shape, scale: scale * jax.random.normal(k, shape, f32)
    gain = lambda k, shape: 1.0 + 0.05 * jax.random.normal(k, shape, f32)
    hd = (L, RWKV_HEADS, HEAD_DIM)
    return {
        "x": nrm(ks[0], (BATCH, SEQ, D_MODEL), 1.0),
        "norm_g": gain(ks[1], (L, D_MODEL)),
        "w_in": nrm(ks[2], (L, D_MODEL, IN_COLS), D_MODEL ** -0.5),
        "mu_shift": jax.random.uniform(ks[3], (L, SHIFT_COLS), f32),
        "w0": jax.random.uniform(ks[4], (L, RWKV_WIDTH), f32, -2.0, 2.0),
        "w_up": nrm(ks[5], (L, DECAY_LORA, RWKV_WIDTH), 0.5 * DECAY_LORA ** -0.5),
        "a0": nrm(ks[6], (L, RWKV_WIDTH), 0.5),
        "a_up": nrm(ks[7], (L, AAA_LORA, RWKV_WIDTH), 0.5 * AAA_LORA ** -0.5),
        "k_k": 0.85 + 0.05 * jax.random.normal(ks[8], hd, f32),
        "k_a": gain(ks[9], hd),
        "r_k": nrm(ks[10], hd, 0.1),
        "gn_g": gain(ks[11], hd),
        "gn_b": nrm(ks[12], hd, 0.02),
        "q_norm_g": gain(ks[13], (L, Q_RANK)),
        "kv_norm_g": gain(ks[14], (L, KV_RANK)),
        "w_uq": nrm(ks[15], (L, Q_RANK, ATTN_WIDTH), Q_RANK ** -0.5),
        "w_uk": nrm(ks[16], (L, ATTN_HEADS, KV_RANK, HEAD_DIM), KV_RANK ** -0.5),
        "w_uv": nrm(ks[17], (L, ATTN_HEADS, KV_RANK, HEAD_DIM), KV_RANK ** -0.5),
        "w_qidx": nrm(ks[18], (L, Q_RANK, IDX_HEADS * IDX_DIM), Q_RANK ** -0.5),
        "kidx_g": gain(ks[19], (L, IDX_DIM)),
        "kidx_b": nrm(ks[20], (L, IDX_DIM), 0.02),
        "w_out": nrm(ks[21], (L, MIX_WIDTH, D_MODEL), MIX_WIDTH ** -0.5),
        "final_g": gain(ks[22], (D_MODEL,)),
    }

def first_block(x, norm_g, w_in, mu_shift, w0, w_up, a0, a_up, k_k, k_a, r_k, gn_g, gn_b,
              q_norm_g, kv_norm_g, w_uq, w_uk, w_uv, w_qidx, kidx_g, kidx_b, w_out, final_g):
    for l in range(DEPTH):
        x = hybrid_layer(x, norm_g[l], w_in[l], mu_shift[l], w0[l], w_up[l], a0[l], a_up[l],
                         k_k[l], k_a[l], r_k[l], gn_g[l], gn_b[l], q_norm_g[l], kv_norm_g[l],
                         w_uq[l], w_uk[l], w_uv[l], w_qidx[l], kidx_g[l], kidx_b[l], w_out[l])
    return rmsnorm(x, final_g)


DEPTH_2 = 2

MLA_HEADS = 4
QK_NOPE = 128
QK_ROPE = 64
V_HEAD = 128
Q_RANK_2 = 384
KV_RANK_2 = 256
ROPE_THETA = 10000.0
HG_HEADS = 4
HG_KEY = 128
HG_VAL = 128
HG_CHUNK = 64
MLA_WIDTH = MLA_HEADS * V_HEAD
HG_WIDTH = HG_HEADS * HG_VAL
HG_FDIM = HG_HEADS * HG_KEY
MIX_WIDTH_2 = MLA_WIDTH + HG_WIDTH
IN_COLS_2 = Q_RANK_2 + KV_RANK_2 + QK_ROPE + 2 * HG_FDIM + 2 * HG_WIDTH
DENSE_FF = 2816
N_EXPERTS = 8
TOP_K = 2
EXPERT_FF = 3584
N_DENSE = (DEPTH_2 + 1) // 2
N_MOE = DEPTH_2 // 2
EPS = 1e-6
F_FLOOR = 1e-30


F32 = jnp.float32
NEG_BIG = float(np.finfo(np.float32).min)

def _rmsnorm(x, gain):
    xf = x.astype(F32)
    y = xf * lax.rsqrt(jnp.mean(xf * xf, axis=-1, keepdims=True) + EPS)
    return (y * gain.astype(F32)).astype(x.dtype)

def _rope_tables(positions):
    inv = ROPE_THETA ** (-jnp.arange(0, QK_ROPE, 2, dtype=F32) / QK_ROPE)
    ang = positions.astype(F32)[..., None] * inv
    return jnp.cos(ang), jnp.sin(ang)

def _apply_rope(x, cos, sin):
    x1, x2 = jnp.split(x, 2, axis=-1)
    cos = cos.astype(x.dtype)
    sin = sin.astype(x.dtype)
    return jnp.concatenate([x1 * cos - x2 * sin, x1 * sin + x2 * cos], axis=-1)

def _mla(c_q, c_kv, k_pe, positions, q_a_norm, w_q_b, kv_a_norm, w_kv_b):
    B, S, _ = c_q.shape
    q = (_rmsnorm(c_q, q_a_norm) @ w_q_b).reshape(B, S, MLA_HEADS, QK_NOPE + QK_ROPE)
    q_nope, q_pe = q[..., :QK_NOPE], q[..., QK_NOPE:]
    cos, sin = _rope_tables(positions)
    q_pe = _apply_rope(q_pe, cos[:, :, None, :], sin[:, :, None, :])
    k_pe = _apply_rope(k_pe, cos, sin)
    kv = (_rmsnorm(c_kv, kv_a_norm) @ w_kv_b).reshape(B, S, MLA_HEADS, QK_NOPE + V_HEAD)
    k_nope, v = kv[..., :QK_NOPE], kv[..., QK_NOPE:]
    scale = (QK_NOPE + QK_ROPE) ** -0.5
    nb = S // Q_BLOCK
    qn_blk = (q_nope * scale).reshape(B, nb, Q_BLOCK, MLA_HEADS, QK_NOPE).transpose(1, 0, 2, 3, 4)
    qp_blk = (q_pe * scale).reshape(B, nb, Q_BLOCK, MLA_HEADS, QK_ROPE).transpose(1, 0, 2, 3, 4)
    starts = jnp.arange(nb, dtype=jnp.int32) * Q_BLOCK
    key_idx = jnp.arange(S, dtype=jnp.int32)

    def block(args):
        qn, qp, start = args
        s = jnp.einsum('bqhd,bkhd->bhqk', qn, k_nope, preferred_element_type=F32)
        s = s + jnp.einsum('bqhr,bkr->bhqk', qp, k_pe, preferred_element_type=F32)
        q_idx = start + jnp.arange(Q_BLOCK, dtype=jnp.int32)
        s = jnp.where(key_idx[None, :] <= q_idx[:, None], s, NEG_BIG)
        p = jax.nn.softmax(s, axis=-1).astype(v.dtype)
        return jnp.einsum('bhqk,bkhd->bqhd', p, v)

    o = lax.map(block, (qn_blk, qp_blk, starts))
    return o.transpose(1, 0, 2, 3, 4).reshape(B, S, MLA_WIDTH)

def _hgrn2(q_raw, f_raw, i_in, g_raw, lower_bound, out_norm):
    B, S, _ = q_raw.shape
    nc = S // HG_CHUNK
    q = jax.nn.silu(q_raw.astype(F32))
    z = f_raw.astype(F32)
    lb = lower_bound.astype(F32)
    f = lb + (1.0 - lb) * jax.nn.sigmoid(z)
    log_f = jnp.log(jnp.maximum(f, F_FLOOR))
    k = (1.0 - lb) * jax.nn.sigmoid(-z)

    def to_chunks(t, d):
        return t.reshape(B, nc, HG_CHUNK, HG_HEADS, d).transpose(1, 0, 3, 2, 4)

    qc = to_chunks(q, HG_KEY)
    kc = to_chunks(k, HG_KEY)
    lfc = to_chunks(log_f, HG_KEY)
    vc = to_chunks(i_in.astype(F32), HG_VAL)
    tri = jnp.tril(jnp.ones((HG_CHUNK, HG_CHUNK), dtype=bool))[:, :, None]

    def step(state, inp):
        qb, kb, vb, lfb = inp
        b = jnp.cumsum(lfb, axis=2)
        diff = b[:, :, :, None, :] - b[:, :, None, :, :]
        decay = jnp.where(tri, jnp.exp(jnp.where(tri, diff, 0.0)), 0.0)
        attn = jnp.einsum('bhtd,bhsd,bhtsd->bhts', qb, kb, decay)
        o = jnp.einsum('bhts,bhsv->bhtv', attn, vb) + jnp.einsum('bhtd,bhdv->bhtv', qb * jnp.exp(b), state)
        b_last = b[:, :, -1:, :]
        new_state = jnp.exp(b_last[:, :, 0, :])[..., None] * state + jnp.einsum('bhsd,bhsv->bhdv', kb * jnp.exp(b_last - b), vb)
        return new_state, o

    s0 = jnp.zeros((B, HG_HEADS, HG_KEY, HG_VAL), F32)
    _, o = lax.scan(step, s0, (qc, kc, vc, lfc))
    o = o.transpose(1, 0, 3, 2, 4).reshape(B, S, HG_HEADS, HG_VAL)
    o = _rmsnorm(o, out_norm) * jax.nn.silu(g_raw.astype(F32).reshape(B, S, HG_HEADS, HG_VAL))
    return o.reshape(B, S, HG_WIDTH)

def _swiglu(h, w_gate, w_up, w_down):
    return (jax.nn.silu(h @ w_gate) * (h @ w_up)) @ w_down

def _moe(h, w_router, w_gate, w_up, w_down):
    B, S, D = h.shape
    T = B * S
    xf = h.reshape(T, D)
    logits = jnp.einsum('td,de->te', xf, w_router, preferred_element_type=F32)
    top_logits, top_idx = lax.top_k(logits, TOP_K)
    gates = jax.nn.softmax(top_logits, axis=-1)
    flat_e = top_idx.reshape(-1)
    flat_tok = jnp.repeat(jnp.arange(T, dtype=jnp.int32), TOP_K)
    order = jnp.argsort(flat_e)
    tok_sorted = flat_tok[order]
    xs = xf[tok_sorted]
    group_sizes = jnp.bincount(flat_e, length=N_EXPERTS).astype(jnp.int32)
    hid = jax.nn.silu(lax.ragged_dot(xs, w_gate, group_sizes)) * lax.ragged_dot(xs, w_up, group_sizes)
    ys = lax.ragged_dot(hid, w_down, group_sizes)
    ys = ys * gates.reshape(-1)[order][:, None].astype(ys.dtype)
    out = jnp.zeros_like(xf).at[tok_sorted].add(ys)
    return out.reshape(B, S, D)

def _normal(key, shape, fan_in):
    return jax.random.normal(key, shape, F32) * (fan_in ** -0.5)

def _gain(key, shape):
    return 1.0 + 0.02 * jax.random.normal(key, shape, F32)

def second_inputs(seed: int = 0) -> dict:
    key = jax.random.key(seed)
    ks = jax.random.split(key, 24)
    x = jax.random.normal(ks[0], (BATCH, SEQ, D_MODEL), F32)
    offset = jax.random.randint(ks[1], (BATCH, 1), 0, 4096, dtype=jnp.int32)
    positions = offset + jnp.arange(SEQ, dtype=jnp.int32)[None, :]
    return {
        "x": x,
        "positions": positions,
        "mix_norm": _gain(ks[2], (DEPTH_2, D_MODEL)),
        "w_in": _normal(ks[3], (DEPTH_2, D_MODEL, IN_COLS_2), D_MODEL),
        "q_a_norm": _gain(ks[4], (DEPTH_2, Q_RANK_2)),
        "w_q_b": _normal(ks[5], (DEPTH_2, Q_RANK_2, MLA_HEADS * (QK_NOPE + QK_ROPE)), Q_RANK_2),
        "kv_a_norm": _gain(ks[6], (DEPTH_2, KV_RANK_2)),
        "w_kv_b": _normal(ks[7], (DEPTH_2, KV_RANK_2, MLA_HEADS * (QK_NOPE + V_HEAD)), KV_RANK_2),
        "hg_lower_bounds": 0.5 * jax.random.normal(ks[8], (DEPTH_2, HG_FDIM), F32),
        "hg_out_norm": _gain(ks[9], (DEPTH_2, HG_VAL)),
        "w_out": _normal(ks[10], (DEPTH_2, MIX_WIDTH_2, D_MODEL), MIX_WIDTH_2),
        "ffn_norm": _gain(ks[11], (DEPTH_2, D_MODEL)),
        "dense_w_gate": _normal(ks[12], (N_DENSE, D_MODEL, DENSE_FF), D_MODEL),
        "dense_w_up": _normal(ks[13], (N_DENSE, D_MODEL, DENSE_FF), D_MODEL),
        "dense_w_down": _normal(ks[14], (N_DENSE, DENSE_FF, D_MODEL), DENSE_FF),
        "moe_router": _normal(ks[15], (N_MOE, D_MODEL, N_EXPERTS), D_MODEL),
        "moe_w_gate": _normal(ks[16], (N_MOE, N_EXPERTS, D_MODEL, EXPERT_FF), D_MODEL),
        "moe_w_up": _normal(ks[17], (N_MOE, N_EXPERTS, D_MODEL, EXPERT_FF), D_MODEL),
        "moe_w_down": _normal(ks[18], (N_MOE, N_EXPERTS, EXPERT_FF, D_MODEL), EXPERT_FF),
        "final_norm": _gain(ks[19], (D_MODEL,)),
    }

def second_block(x, positions, mix_norm, w_in, q_a_norm, w_q_b, kv_a_norm, w_kv_b, hg_lower_bounds, hg_out_norm, w_out, ffn_norm, dense_w_gate, dense_w_up, dense_w_down, moe_router, moe_w_gate, moe_w_up, moe_w_down, final_norm):
    lb_p = jax.nn.softmax(hg_lower_bounds.astype(F32), axis=0)
    lower = jnp.cumsum(lb_p, axis=0) - lb_p[0:1]
    splits = np.cumsum([Q_RANK_2, KV_RANK_2, QK_ROPE, HG_FDIM, HG_FDIM, HG_WIDTH]).tolist()
    for l in range(DEPTH_2):
        h = _rmsnorm(x, mix_norm[l])
        proj = h @ w_in[l]
        c_q, c_kv, k_pe, hq, hf, hi, hg = jnp.split(proj, splits, axis=-1)
        a = _mla(c_q, c_kv, k_pe, positions, q_a_norm[l], w_q_b[l], kv_a_norm[l], w_kv_b[l])
        r = _hgrn2(hq, hf, hi, hg, lower[l], hg_out_norm[l]).astype(x.dtype)
        x = x + jnp.concatenate([a, r], axis=-1) @ w_out[l]
        h = _rmsnorm(x, ffn_norm[l])
        if l % 2 == 0:
            j = l // 2
            x = x + _swiglu(h, dense_w_gate[j], dense_w_up[j], dense_w_down[j])
        else:
            j = l // 2
            x = x + _moe(h, moe_router[j], moe_w_gate[j], moe_w_up[j], moe_w_down[j])
    return _rmsnorm(x, final_norm)


def setup_inputs(seed=0):
    out = dict(first_inputs(seed))
    for name, value in second_inputs(seed + 1).items():
        if name != "x":
            out[name + "_2"] = value
    return out


def reference(
    x, norm_g, w_in, mu_shift, w0, w_up, a0, a_up, k_k, k_a, r_k, gn_g, gn_b, q_norm_g,
    kv_norm_g, w_uq, w_uk, w_uv, w_qidx, kidx_g, kidx_b, w_out, final_g, positions_2,
    mix_norm_2, w_in_2, q_a_norm_2, w_q_b_2, kv_a_norm_2, w_kv_b_2, hg_lower_bounds_2,
    hg_out_norm_2, w_out_2, ffn_norm_2, dense_w_gate_2, dense_w_up_2, dense_w_down_2,
    moe_router_2, moe_w_gate_2, moe_w_up_2, moe_w_down_2, final_norm_2,
):
    x = first_block(
        x, norm_g, w_in, mu_shift, w0, w_up, a0, a_up, k_k, k_a, r_k, gn_g, gn_b, q_norm_g,
        kv_norm_g, w_uq, w_uk, w_uv, w_qidx, kidx_g, kidx_b, w_out, final_g,
    )
    return second_block(
        x, positions_2, mix_norm_2, w_in_2, q_a_norm_2, w_q_b_2, kv_a_norm_2, w_kv_b_2,
        hg_lower_bounds_2, hg_out_norm_2, w_out_2, ffn_norm_2, dense_w_gate_2, dense_w_up_2,
        dense_w_down_2, moe_router_2, moe_w_gate_2, moe_w_up_2, moe_w_down_2, final_norm_2,
    )


_drawn_inputs = setup_inputs


def setup_inputs(seed=0):
    import zlib

    import numpy as np

    out = dict(_drawn_inputs(seed))
    spreads = {}
    factors = {'k_k': 3.022,
     'kv_norm_g': 3.813,
     'kidx_g': 3.337,
     'kidx_b': 4.185,
     'q_a_norm_2': 4.445,
     'kv_a_norm_2': 3.872,
     'hg_lower_bounds_2': 6.107,
     'hg_out_norm_2': 4.143,
     'ffn_norm_2': 2.842}
    for name, (base, spread) in spreads.items():
        noise = np.random.default_rng([zlib.crc32(name.encode()), seed]).standard_normal(out[name].shape)
        drawn = base * np.exp(spread * noise) if base else spread * noise
        out[name] = __import__('jax').numpy.asarray(drawn.astype(out[name].dtype))
    for name, factor in factors.items():
        out[name] = (out[name] * factor).astype(out[name].dtype)
    return out
```

```python
import math
from contextlib import ExitStack

import numpy as np
import concourse.bass as bass
from concourse import mybir

F32 = mybir.dt.float32
F32R = mybir.dt.float32r
I32 = mybir.dt.int32
U32 = mybir.dt.uint32
ALU = mybir.AluOpType
ACT = mybir.ActivationFunctionType
AX = mybir.AxisListType.X

T = 1024
D = 1024
P = 128
NT = T // P
KD = D // P
HALF = 512
NEG = -1.0e30
TAKEN = -3.0e38
CH = 64
NCH = T // CH
LEVELS = 6
TOPK = 256
IDX_HEADS = 4
SLOTS = 256
NEXP = 8
NPASS = 2 * T // SLOTS + NEXP - 1
EFF = 3584
DFF = 2816

VEC = {}
_n = 0
for _name, _w in (("norm_g", 8), ("mu", 13), ("w0", 4), ("a0", 4), ("k_k", 4), ("k_a", 4), ("r_k", 4),
                  ("gn_g", 4), ("gn_b", 4), ("q_norm_g", 2), ("kv_norm_g", 1), ("kidx_g", 1), ("kidx_b", 1),
                  ("mix0", 8), ("mix1", 8), ("ffn0", 8), ("ffn1", 8), ("qa0", 3), ("qa1", 3),
                  ("kva0", 2), ("kva1", 2), ("hgn0", 1), ("hgn1", 1), ("lb0", 4), ("lb1", 4), ("inv", 1)):
    VEC[_name] = (_n, _w)
    _n += _w
NVEC = _n

CST = {}
_n = 0
for _name, _w in (("eye", 128), ("ones", 128), ("heads", 128), ("upto", 64), ("before", 64),
                  ("level", LEVELS * 64), ("restart", T), ("causal", T), ("decaylevel", 7 * 64),
                  ("earlier", 128), ("iota8", 8), ("tok", 8), ("below8", 8), ("pass", NPASS + 1), ("fold", 64), ("spans", 512)):
    CST[_name] = (_n, _w)
    _n += _w
NCST = _n


class Links:

    def __init__(self, eng, sem, base=0):
        self.eng, self.sem, self.base, self.n = eng, sem, base, 0

    def __call__(self, ins):
        self.n += 1
        ins.then_inc(self.sem, 1)
        self.eng.wait_ge(self.sem, self.base + self.n)


class Core:

    def __init__(self, nc, dram, ctx):
        self.nc, self.dram, self.ctx = nc, dram, ctx
        self.ps = ctx.enter_context(nc.psum_tensor("ps", [P, 8, HALF], F32))
        self.cst = ctx.enter_context(nc.sbuf_tensor("cst", [P, NCST], F32))
        self.vec = ctx.enter_context(nc.sbuf_tensor("vec", [P, NVEC], F32))

        self.passed = nc.alloc_semaphore("passed")

    def settle(self, eng):
        eng.sem_inc(self.passed, 1)

    def c(self, name, p0=0, p1=P):
        o, w = CST[name]
        return self.cst[p0:p1, o:o + w]

    def v(self, name, j, p0=0, p1=P):
        o, _ = VEC[name]
        return self.vec[p0:p1, o + j:o + j + 1]

    def vs(self, name, p0=0, p1=P):
        o, w = VEC[name]
        return self.vec[p0:p1, o:o + w]


class Stage:

    def __init__(self, core, name):
        self.nc, self.name, self.stack, self.sems = core.nc, name, ExitStack(), []

    def sem(self, name):
        s = self.nc.alloc_semaphore(f"{self.name}_{name}")
        self.sems.append(s)
        return s

    def sb(self, name, shape, dt=F32):
        return self.stack.enter_context(self.nc.sbuf_tensor(f"{self.name}_{name}", shape, dt))

    def end(self):
        self.nc.clear_and_free_semaphores(self.sems)
        self.nc.all_engine_barrier()
        self.stack.close()


def at(x, i):
    if isinstance(i, int):
        return x[:, i]
    names = " ".join(f"d{k}" for k in range(len(x.shape) - 2))
    return x[:, bass.ds(i, 1)].rearrange(f"p one {names} -> p (one d0) {names[2:]}".rstrip())


def pairs(eng, count, body, first=0):
    lo, hi = first // 2, count // 2
    if hi - lo > 1:
        with eng.Fori(lo, hi, 1) as i:
            for u in range(2):
                body(2 * i + u, u, i)
    else:
        for i in range(lo, hi):
            for u in range(2):
                body(2 * i + u, u, i)
    if count % 2 and count > first:
        body(count - 1, 0, count // 2)


def load_constants(core):
    nc, d = core.nc, core.dram
    st = Stage(core, "const")
    loaded = st.sem("loaded")
    with nc.Block("const") as block:
        @block.sync
        def _(sp):
            sp.dma_start(core.cst[:, :], d["constants"]).then_inc(loaded, 16)
            sp.dma_start(core.vec[:, :], d["vectors"]).then_inc(loaded, 16)
            sp.wait_ge(loaded, 32)
    st.end()


def norm_transpose(core, name, x, xT, gain, source=None):
    nc = core.nc
    st = Stage(core, name)
    junk = st.sb("junk", [P, D])
    stat = st.sb("stat", [P, 3, NT])
    xs = st.sb("scaled", [P, 2, D])
    loaded = [st.sem(f"loaded{i}") for i in range(NT)]
    summed, mean, root, inverse = st.sem("summed"), st.sem("mean"), st.sem("root"), st.sem("inverse")
    scaled, turned, placed = st.sem("scaled"), st.sem("turned"), st.sem("placed")
    ps4 = core.ps[:, :, :].rearrange("p (u b) (c n) -> p u (b c) n", u=4, c=4)
    with nc.Block(name) as block:
        if source is not None:
            @block.sync
            def _(sp):
                for b in range(NT):
                    sp.dma_start(x[:, b, :], source[b * P:(b + 1) * P, :]).then_inc(loaded[b], 16)

        @block.scalar
        def _(act):
            for b in range(NT):
                if source is not None:
                    act.wait_ge(loaded[b], 16)
                if b:
                    act.wait_ge(summed, b)
                nc.scalar.activation(junk[:, :], x[:, b, :], ACT.Square,
                                     accum_out=stat[:, 0, b:b + 1]).then_inc(summed, 1)
            act.wait_ge(mean, 1)
            nc.scalar.activation(stat[:, 2, :], stat[:, 1, :], ACT.Sqrt).then_inc(root, 1)

        @block.vector
        def _(dve):
            dve.wait_ge(summed, NT)
            nc.vector.tensor_scalar(stat[:, 1, :], stat[:, 0, :], 1.0 / D, 1e-6, ALU.mult, ALU.add).then_inc(mean, 1)
            dve.wait_ge(root, 1)
            nc.vector.reciprocal(stat[:, 0, :], stat[:, 2, :]).then_inc(inverse, 1)
            dve.wait_ge(inverse, 1)

            def place(b):
                dve.wait_ge(turned, b + 1)
                nc.vector.tensor_tensor(xT[:, :, b * P:(b + 1) * P], ps4[:, b % 2], 
                                        core.vs(gain).unsqueeze(2).to_broadcast([P, KD, P]),
                                        ALU.mult).then_inc(placed, 1)
            for b in range(NT):
                if b >= 2:
                    dve.wait_ge(turned, b - 1)
                nc.vector.tensor_scalar(xs[:, b % 2, :], x[:, b, :], stat[:, 0, b:b + 1], None,
                                        ALU.mult).then_inc(scaled, 1)
                if b >= 1:
                    place(b - 1)
            place(NT - 1)

        @block.tensor
        def _(pe):
            for b in range(NT):
                pe.wait_ge(scaled, b + 1)
                if b >= 2:
                    pe.wait_ge(placed, b - 1)
                for k in range(KD):
                    last = nc.tensor.transpose(ps4[:, b % 2, k, :], xs[:, b % 2, k * P:(k + 1) * P], core.c("eye"))
                last.then_inc(turned, 1)
    st.end()


def gemm_t(core, name, weights, count, kb, xT, dest, first=0, func=ACT.Copy):
    nc = core.nc
    st = Stage(core, name)
    w = st.sb("w", [P, 2, kb * P])
    loaded = [st.sem("loaded0"), st.sem("loaded1")]
    product, psum_free = st.sem("product"), st.sem("psum_free")
    with nc.Block(name) as block:
        @block.sync
        def _(sp):
            def load(n, u):
                src = weights[first + n] if isinstance(n, int) else \
                    weights[bass.ds(n + first, 1)].rearrange("a p n -> p (a n)")
                sp.dma_start(w[:, u, :], src).then_inc(loaded[u], 16)
            for n in range(min(2, count)):
                load(n, n)

            def ahead(n, u, i):
                sp.wait_ge(product, n - 1)
                load(n, u)
            pairs(sp, count, ahead, first=2)

        @block.tensor
        def _(pe):
            def one(n, u, i):
                pe.wait_ge(loaded[u], (i + 1) * 16)
                pe.wait_ge(psum_free, n + 1)
                for k in range(kb):
                    for h in range(2):
                        last = nc.tensor.matmul(core.ps[:, 2 * u + h, :], w[:, u, k * P:(k + 1) * P],
                                                xT[:, k, h * HALF:(h + 1) * HALF], start=(k == 0), stop=(k == kb - 1))
                last.then_inc(product, 1)
            pairs(pe, count, one)

        @block.scalar
        def _(act):
            act.sem_inc(psum_free, 2)

            def one(n, u, i):
                act.wait_ge(product, n + 1)
                nc.scalar.activation(dest(n), core.ps[:, 2 * u:2 * u + 2, :].rearrange("p a n -> p (a n)"),
                                     func).then_inc(psum_free, 1)
            pairs(act, count, one)
    st.end()


def shift_tokens(core, big, small, mix):
    nc = core.nc
    st = Stage(core, "shift")
    diff = st.sb("diff", [P, 2, T])
    subtracted, first_token, step = st.sem("subtracted"), st.sem("first_token"), st.sem("step")
    blocks = [big[:, 1, j] for j in range(4)] + [big[:, 3, j] for j in range(4)] + \
             [big[:, 4, j] for j in range(4)] + [small[:, :]]
    with nc.Block("shift") as block:
        @block.scalar
        def _(act):
            for n, p in enumerate(blocks):
                if n >= 2:
                    act.wait_ge(step, n - 1)
                nc.scalar.activation(diff[:, n % 2, 0:1], p[:, 0:1], ACT.Copy, scale=-1.0).then_inc(first_token, 1)

        @block.gpsimd
        def _(pool):
            for n, p in enumerate(blocks):
                if n >= 2:
                    pool.wait_ge(step, n - 1)
                nc.gpsimd.tensor_tensor(diff[:, n % 2, 1:T], p[:, 0:T - 1], p[:, 1:T], ALU.subtract).then_inc(subtracted, 1)

        @block.vector
        def _(dve):
            for n, p in enumerate(blocks):
                dve.wait_ge(subtracted, n + 1)
                dve.wait_ge(first_token, n + 1)
                nc.vector.scalar_tensor_tensor(p, diff[:, n % 2, :], core.v("mu", n), p, ALU.mult, ALU.add).then_inc(step, 1)
    st.end()


def rwkv_operands(core, big, small, decay_end, bonus, rate, cum):
    nc, d = core.nc, core.dram
    st = Stage(core, "operands")
    tmp = st.sb("tmp", [P, 4, T])
    low = st.sb("low", [64, T])
    up = st.sb("up", [64, 2, 512])
    one_ka = st.sb("one_ka", [P, 4])
    wide = lambda x: x.rearrange("p a n -> p (a n)")
    R, K, V, KK, A = big[:, 1], big[:, 3], big[:, 4], big[:, 0], big[:, 2]
    all8 = core.ps[:, :, :].rearrange("p b n -> p (b n)")
    loaded, lowr, lora, gates, heads = (st.sem(x) for x in ("loaded", "lowrank", "lora", "gates", "heads"))
    a_link, d_link, scanned, squared, rooted, products, e1, e2, e3, u1, u2, u3 = (
        st.sem(x) for x in ("a_link", "d_link", "scanned", "squared", "rooted", "products",
                            "exp_up", "exp_before", "exp_down", "used_up", "used_before", "bonus_read"))
    with nc.Block("operands") as block:
        @block.sync
        def _(sp):
            sp.dma_start(up[:, 0, :], d["w_up"]).then_inc(loaded, 16)
            sp.dma_start(up[:, 1, :], d["a_up"]).then_inc(loaded, 16)
            sp.wait_ge(loaded, 32)

        @block.scalar
        def _(act):
            nc.scalar.activation(low[0:32, :], small[0:32, :], ACT.Tanh).then_inc(lowr, 1)
            nc.scalar.activation(low[32:64, :], small[32:64, :], ACT.Copy).then_inc(lowr, 1)
            for m in range(2):
                for j in range(4):
                    n = 4 * m + j
                    act.wait_ge(lora, n + 1)
                    b = 2 * (n % 4)
                    nc.scalar.activation((rate if m == 0 else A)[:, j, :],
                                         core.ps[:, b:b + 2, :].rearrange("p a n -> p (a n)"), ACT.Sigmoid,
                                         bias=core.v("w0" if m == 0 else "a0", j)).then_inc(gates, 1)
            act.wait_ge(squared, 1)
            nc.scalar.activation(wide(tmp[:, :, :]), wide(KK), ACT.Square).then_inc(squared, 1)
            act.wait_ge(heads, 1)
            nc.scalar.activation(wide(tmp[:, :, :]), all8, ACT.Sqrt).then_inc(rooted, 1)
            act.wait_ge(scanned, 4)
            act.wait_ge(u3, 1)
            nc.scalar.activation(wide(tmp[:, :, :]), wide(cum[:, :, :]), ACT.Exp).then_inc(e1, 1)
            act.wait_ge(u1, 1)
            nc.scalar.activation(wide(rate[:, :, :]), wide(rate[:, :, :]), ACT.Exp).then_inc(e2, 1)
            nc.scalar.activation(wide(tmp[:, :, :]), wide(cum[:, :, :]), ACT.Exp, scale=-1.0).then_inc(e3, 1)

        @block.tensor
        def _(pe):
            pe.wait_ge(loaded, 32)
            pe.wait_ge(lowr, 2)
            for m in range(2):
                for j in range(4):
                    n = 4 * m + j
                    if n >= 4:
                        pe.wait_ge(gates, n - 3)
                    for h in range(2):
                        last = nc.tensor.matmul(core.ps[:, 2 * (n % 4) + h, :], up[:, m, j * P:(j + 1) * P],
                                                low[:, h * HALF:(h + 1) * HALF], start=True, stop=True)
                    last.then_inc(lora, 1)

            def head_sums():
                for j in range(4):
                    for h in range(2):
                        last = nc.tensor.matmul(core.ps[:, 2 * j + h, :], core.c("heads"),
                                                tmp[:, j, h * HALF:(h + 1) * HALF], start=True, stop=True)
                last.then_inc(heads, 1)
            pe.wait_ge(gates, 8)
            pe.wait_ge(squared, 2)
            head_sums()
            pe.wait_ge(rooted, 1)
            pe.wait_ge(products, 4)
            head_sums()

        @block.vector
        def _(dve):
            link = Links(dve, d_link)
            for j in range(4):
                last = nc.vector.tensor_scalar(KK[:, j, :], K[:, j, :], core.v("k_k", j), None, ALU.mult)
            last.then_inc(squared, 1)
            link(nc.vector.tensor_scalar(one_ka[:, :], core.vs("k_a"), -1.0, 1.0, ALU.mult, ALU.add))
            dve.wait_ge(gates, 4)
            link(nc.vector.tensor_scalar(wide(rate[:, :, :]), wide(rate[:, :, :]), -math.exp(-0.5), None, ALU.mult))
            for j in range(4):
                nc.vector.tensor_tensor_scan(cum[:, j, :], core.c("restart"), rate[:, j, :], 0.0,
                                             ALU.mult, ALU.add).then_inc(scanned, 1)
            dve.wait_ge(rooted, 1)
            link(nc.vector.tensor_scalar(wide(tmp[:, :, :]), wide(tmp[:, :, :]), 1e-12, None, ALU.max))
            link(nc.vector.reciprocal(wide(tmp[:, :, :]), wide(tmp[:, :, :])))
            link(nc.vector.tensor_tensor(wide(KK), wide(KK), wide(tmp[:, :, :]), ALU.mult))
            dve.wait_ge(gates, 8)
            for j in range(4):
                last = nc.vector.tensor_scalar(tmp[:, j, :], A[:, j, :], core.v("k_a", j), one_ka[:, j:j + 1],
                                               ALU.mult, ALU.add)
            link(last)
            link(nc.vector.tensor_tensor(wide(K), wide(K), wide(tmp[:, :, :]), ALU.mult))
            nc.vector.tensor_tensor(wide(A), wide(A), wide(KK), ALU.mult)
            for j in range(4):
                nc.vector.scalar_tensor_tensor(tmp[:, j, :], R[:, j, :], core.v("r_k", j), K[:, j, :],
                                               ALU.mult, ALU.mult).then_inc(products, 1)
            dve.wait_ge(heads, 2)
            nc.vector.tensor_tensor(wide(bonus[:, :, :]), all8, wide(V), ALU.mult).then_inc(u3, 1)
            dve.wait_ge(scanned, 4)
            nc.vector.tensor_tensor(wide(rate[:, :, :]), wide(cum[:, :, :]), wide(rate[:, :, :]), ALU.subtract)
            dve.wait_ge(e1, 1)
            nc.vector.tensor_copy(decay_end[:, :, :], tmp[:, :, CH - 1::CH])
            nc.vector.tensor_tensor(wide(R), wide(R), wide(tmp[:, :, :]), ALU.mult).then_inc(u1, 1)
            dve.wait_ge(e2, 1)
            nc.vector.tensor_tensor(wide(KK), wide(KK), wide(rate[:, :, :]), ALU.mult)
            dve.wait_ge(e3, 1)
            nc.vector.tensor_tensor(wide(A), wide(A), wide(tmp[:, :, :]), ALU.mult)
            nc.vector.tensor_tensor(wide(K), wide(K), wide(tmp[:, :, :]), ALU.mult)
    st.end()


def rwkv_chunks(core, big, decay_end, spare):
    nc = core.nc
    st = Stage(core, "chunks")
    H = 8
    x64 = st.sb("x64", [64, 4, H, CH])
    x128 = st.sb("x128", [P, 3, 4, CH])
    tok = st.sb("tok", [64, 3, H, CH])
    flat = spare[0:64, :, :].rearrange("p a n -> p (a n)")
    w = H * CH
    a_lvl = flat[:, 0:LEVELS * w].rearrange("p (l h n) -> p l h n", l=LEVELS, h=H)
    k12 = flat[:, LEVELS * w:(LEVELS + 2) * w].rearrange("p (m h n) -> p m h n", m=2, h=H)
    inv = flat[:, (LEVELS + 2) * w:(LEVELS + 4) * w].rearrange("p (m h n) -> p m h n", m=2, h=H)
    b1 = flat[:, (LEVELS + 4) * w:(LEVELS + 5) * w].rearrange("p (h n) -> p h n", h=H)
    q1 = st.sb("q1", [64, H, CH])
    nr = st.sb("nr", [64, H, CH])
    sa = st.sb("sa", [64, H, CH])
    state = st.sb("state", [64, H, CH])
    gam = st.sb("gam", [64, H])
    names = ("copied_a", "copied_d", "copied_p", "products", "turned", "masked", "tokened", "q_ready", "q_copied", "upd_ready",
             "updated", "r_ready", "r_copied", "sa_ready", "sa_copied", "yd_ready", "y_copied", "state_new", "d_link")
    s = {x: st.sem(x) for x in names}
    ps = core.ps
    bank = lambda b: ps[0:64, b, :].rearrange("p (h n) -> p h n", h=H)
    NL = LEVELS - 1

    with nc.Block("chunks") as block:
        @block.gpsimd
        def _(pool):
            nc.gpsimd.memset(state[:, :, :], 0.0).then_inc(s["state_new"], 1)
            with pool.Fori(0, NCH, 1) as c:
                pool.wait_ge(s["state_new"], c + 1)
                nc.gpsimd.tensor_copy(x128[:, :, :, :], big[:, 2:5, :, bass.ds(c * CH, CH)]).then_inc(s["copied_p"], 1)

        @block.scalar
        def _(act):
            with act.Fori(0, NCH, 1) as c:
                act.wait_ge(s["state_new"], c + 1)
                nc.scalar.activation(x64[:, :, 4:8, :], big[64:128, 0:4, :, bass.ds(c * CH, CH)], ACT.Copy).then_inc(s["copied_a"], 1)
                act.wait_ge(s["turned"], c + 1)
                for j in range(3):
                    nc.scalar.activation(tok[:, j, :, :].rearrange("p (o r) n -> p r o n", o=2),
                                         ps[0:64, 4 + j, :].rearrange("p (r o n) -> p r o n", r=4, o=2),
                                         ACT.Copy).then_inc(s["tokened"], 1)
                for l in range(1, LEVELS):
                    act.wait_ge(s["q_ready"], c * LEVELS + l + 1)
                    nc.scalar.activation(q1[:, :, :], bank(0), ACT.Copy).then_inc(s["q_copied"], 1)
                act.wait_ge(s["r_ready"], c + 1)
                nc.scalar.activation(nr[:, :, :], bank(5), ACT.Copy, scale=-1.0).then_inc(s["r_copied"], 1)
                act.wait_ge(s["yd_ready"], c + 1)
                for o in range(2):
                    nc.scalar.activation(big[64 * o:64 * o + 64, 1, :, bass.ds(c * CH, CH)],
                                         bank(6)[:, 4 * o:4 * o + 4, :], ACT.Copy).then_inc(s["y_copied"], 1)

        @block.vector
        def _(dve):
            with dve.Fori(0, NCH, 1) as c:
                link = Links(dve, s["d_link"], c * 3)
                dve.wait_ge(s["state_new"], c + 1)
                nc.vector.tensor_copy(x64[:, :, 0:4, :], big[0:64, 0:4, :, bass.ds(c * CH, CH)]).then_inc(s["copied_d"], 1)
                for o in range(2):
                    last = nc.vector.tensor_copy(gam[:, 4 * o:4 * o + 4],
                                                 decay_end[64 * o:64 * o + 64, :, bass.ds(c, 1)].rearrange("p r n -> p (r n)"))
                link(last)
                dve.wait_ge(s["products"], c + 1)
                lv = core.c("level", 0, 64).rearrange("p (l n) -> p l n", l=LEVELS)
                for l in range(LEVELS):
                    nc.vector.tensor_tensor(a_lvl[:, l, :, :], bank(3),
                                            lv[:, l].unsqueeze(1).to_broadcast([64, H, CH]), ALU.mult).then_inc(s["masked"], 1)
                nc.vector.tensor_tensor(b1[:, :, :], bank(0), core.c("upto", 0, 64).unsqueeze(1).to_broadcast([64, H, CH]),
                                        ALU.mult).then_inc(s["masked"], 1)
                for m, mask in enumerate(("before", "upto")):
                    nc.vector.tensor_tensor(k12[:, m, :, :], bank(1 + m),
                                            core.c(mask, 0, 64).unsqueeze(1).to_broadcast([64, H, CH]),
                                            ALU.mult).then_inc(s["masked"], 1)
                eye = core.c("eye", 0, 64)[:, 0:64].unsqueeze(1).to_broadcast([64, H, CH])
                dve.wait_ge(s["q_ready"], c * LEVELS + 1)
                nc.vector.scalar_tensor_tensor(inv[:, 0, :, :], bank(0), -1.0, eye, ALU.mult, ALU.add).then_inc(s["updated"], 1)
                link(nc.vector.tensor_scalar(inv[:, 1, :, :], a_lvl[:, 0, :, :], -1.0, None, ALU.mult))
                nc.vector.tensor_tensor(inv[:, 1, :, :], inv[:, 1, :, :], eye, ALU.add).then_inc(s["updated"], 1)
                for l in range(1, LEVELS):
                    dve.wait_ge(s["upd_ready"], c * NL + l)
                    dve.wait_ge(s["updated"], c * (NL + 2) + l + 1)
                    m = 2 if l < LEVELS - 1 else 1
                    nc.vector.tensor_tensor(inv[:, 0:m, :, :], inv[:, 0:m, :, :],
                                            ps[0:64, 1:1 + m, :].rearrange("p m (h n) -> p m h n", h=H),
                                            ALU.subtract).then_inc(s["updated"], 1)
                dve.wait_ge(s["sa_ready"], c + 1)
                nc.vector.tensor_copy(sa[:, :, :], bank(4)).then_inc(s["sa_copied"], 1)
                dve.wait_ge(s["yd_ready"], c + 1)
                link(nc.vector.tensor_tensor(state[:, :, :], state[:, :, :], bank(7), ALU.add))
                nc.vector.tensor_tensor(state[:, :, :], state[:, :, :], gam[:, :].unsqueeze(2).to_broadcast([64, H, CH]),
                                        ALU.mult).then_inc(s["state_new"], 1)

        @block.tensor
        def _(pe):
            mm = nc.tensor.matmul
            with pe.Fori(0, NCH, 1) as c:
                pe.wait_ge(s["copied_a"], c + 1)
                pe.wait_ge(s["copied_d"], c + 1)
                core.settle(pe)
                for h in range(H):
                    mm(bank(3)[:, h], x64[:, 0, h], x64[:, 2, h], start=True, stop=True)
                    mm(bank(0)[:, h], x64[:, 2, h], x64[:, 1, h], start=True, stop=True)
                    mm(bank(1)[:, h], x64[:, 3, h], x64[:, 0, h], start=True, stop=True)
                    last = mm(bank(2)[:, h], x64[:, 3, h], x64[:, 1, h], start=True, stop=True)
                last.then_inc(s["products"], 1)
                pe.wait_ge(s["copied_p"], c + 1)
                core.settle(pe)
                for j in range(3):
                    for r in range(4):
                        last = nc.tensor.transpose(ps[0:64, 4 + j, r * P:(r + 1) * P], x128[:, j, r, :], core.c("eye"))
                last.then_inc(s["turned"], 1)
                pe.wait_ge(s["masked"], (c + 1) * (LEVELS + 3))
                core.settle(pe)
                for h in range(H):
                    last = mm(bank(0)[:, h], a_lvl[:, 0, h], core.c("eye", 0, 64)[:, 0:64], start=True, stop=True)
                last.then_inc(s["q_ready"], 1)
                for l in range(1, LEVELS):
                    pe.wait_ge(s["updated"], c * (NL + 2) + l + 1)
                    core.settle(pe)
                    for h in range(H):
                        last = mm(bank(0)[:, h], a_lvl[:, l, h], inv[:, 0, h], start=True, stop=True)
                    last.then_inc(s["q_ready"], 1)
                    pe.wait_ge(s["q_copied"], c * NL + l)
                    core.settle(pe)
                    for h in range(H):
                        last = mm(bank(1)[:, h], inv[:, 1, h], q1[:, h], start=True, stop=True)
                        if l < LEVELS - 1:
                            last = mm(bank(2)[:, h], q1[:, h], inv[:, 1, h], start=True, stop=True)
                    last.then_inc(s["upd_ready"], 1)
                pe.wait_ge(s["tokened"], 3 * (c + 1))
                core.settle(pe)
                for h in range(H):
                    mm(bank(5)[:, h], x64[:, 0, h], state[:, h], start=True, stop=False)
                    last = mm(bank(5)[:, h], k12[:, 0, h], tok[:, 2, h], start=False, stop=True)
                last.then_inc(s["r_ready"], 1)
                pe.wait_ge(s["r_copied"], c + 1)
                pe.wait_ge(s["updated"], (c + 1) * (NL + 2))
                core.settle(pe)
                for h in range(H):
                    last = mm(bank(4)[:, h], inv[:, 0, h], nr[:, h], start=True, stop=True)
                last.then_inc(s["sa_ready"], 1)
                pe.wait_ge(s["sa_copied"], c + 1)
                core.settle(pe)
                for h in range(H):
                    mm(bank(6)[:, h], state[:, h], x64[:, 1, h], start=True, stop=False)
                    mm(bank(6)[:, h], sa[:, h], b1[:, h], start=False, stop=False)
                    mm(bank(6)[:, h], tok[:, 2, h], k12[:, 1, h], start=False, stop=True)
                    mm(bank(7)[:, h], tok[:, 0, h], sa[:, h], start=True, stop=False)
                    last = mm(bank(7)[:, h], tok[:, 1, h], tok[:, 2, h], start=False, stop=True)
                last.then_inc(s["yd_ready"], 1)
                pe.wait_ge(s["y_copied"], 2 * (c + 1))
                pe.wait_ge(s["state_new"], c + 2)
    st.end()


def rwkv_output(core, big, gate, bonus, mixT):
    nc = core.nc
    st = Stage(core, "rwkv_out")
    dev, var = big[:, 2], big[:, 3]
    wide = lambda x: x.rearrange("p a n -> p (a n)")
    Y = big[:, 1]
    all8 = core.ps[:, :, :].rearrange("p b n -> p (b n)")
    sums, centred, squared, meanvar, rooted, d_link = (
        st.sem(x) for x in ("sums", "centred", "squared", "meanvar", "rooted", "d_link"))
    with nc.Block("rwkv_out") as block:
        @block.tensor
        def _(pe):
            for m, x in enumerate((Y, var)):
                if m:
                    pe.wait_ge(squared, 1)
                for j in range(4):
                    for h in range(2):
                        last = nc.tensor.matmul(core.ps[:, 2 * j + h, :], core.c("heads"),
                                                x[:, j, h * HALF:(h + 1) * HALF], start=True, stop=True)
                last.then_inc(sums, 1)

        @block.scalar
        def _(act):
            act.wait_ge(centred, 1)
            nc.scalar.activation(wide(var), wide(dev), ACT.Square).then_inc(squared, 1)
            act.wait_ge(meanvar, 1)
            nc.scalar.activation(wide(var), wide(var), ACT.Sqrt).then_inc(rooted, 1)

        @block.vector
        def _(dve):
            link = Links(dve, d_link)
            dve.wait_ge(sums, 1)
            nc.vector.scalar_tensor_tensor(wide(dev), all8, -1.0 / 64, wide(Y), ALU.mult, ALU.add).then_inc(centred, 1)
            dve.wait_ge(sums, 2)
            nc.vector.tensor_scalar(wide(var), all8, 1.0 / 64, 64e-5, ALU.mult, ALU.add).then_inc(meanvar, 1)
            dve.wait_ge(rooted, 1)
            link(nc.vector.reciprocal(wide(var), wide(var)))
            link(nc.vector.tensor_tensor(wide(dev), wide(dev), wide(var), ALU.mult))
            for j in range(4):
                last = nc.vector.tensor_scalar(dev[:, j, :], dev[:, j, :], core.v("gn_g", j), core.v("gn_b", j), ALU.mult, ALU.add)
            link(last)
            link(nc.vector.tensor_tensor(wide(dev), wide(dev), wide(bonus[:, :, :]), ALU.add))
            nc.vector.tensor_tensor(wide(mixT[:, 0:4, :]), wide(gate[:, :, :]), wide(dev), ALU.mult)
    st.end()


def channel_norms(core, name, x, groups):
    nc = core.nc
    st = Stage(core, name)
    n_blocks = max(max(g[0]) for g in groups) + 1
    sq = st.sb("sq", [P, n_blocks, T])
    inv = st.sb("inv", [P, len(groups), T])
    mean_ready, centred_done, squared, sums, meansq, rooted, d_link = (
        st.sem(x) for x in ("mean_ready", "centred", "squared", "sums", "meansq", "rooted", "d_link"))
    two = lambda b: core.ps[:, b:b + 2, :].rearrange("p a n -> p (a n)")
    halves = lambda y, h: y[:, h * HALF:(h + 1) * HALF]
    centred = [(i, g) for i, g in enumerate(groups) if g[4]]
    with nc.Block(name) as block:
        @block.tensor
        def _(pe):
            for i, g in centred:
                for h in range(2):
                    last = nc.tensor.matmul(core.ps[:, 6 + h, :], core.c("heads"), halves(x[:, g[0][0], :], h), start=True, stop=True)
                last.then_inc(mean_ready, 1)
            done = 0
            for i, g in enumerate(groups):
                done += len(g[0])
                pe.wait_ge(squared, done)
                for h in range(2):
                    for m, b in enumerate(g[0]):
                        last = nc.tensor.matmul(core.ps[:, 2 * i + h, :], core.c("heads" if g[4] else "ones"),
                                                halves(sq[:, b, :], h), start=(m == 0), stop=(m == len(g[0]) - 1))
                last.then_inc(sums, 1)

        @block.scalar
        def _(act):
            for i, g in enumerate(groups):
                if g[4]:
                    act.wait_ge(centred_done, 1)
                for b in g[0]:
                    nc.scalar.activation(sq[:, b, :], x[:, b, :], ACT.Square).then_inc(squared, 1)
            for i, g in enumerate(groups):
                act.wait_ge(meansq, i + 1)
                nc.scalar.activation(inv[:, i, :], inv[:, i, :], ACT.Sqrt).then_inc(rooted, 1)

        @block.vector
        def _(dve):
            link = Links(dve, d_link)
            for i, g in centred:
                dve.wait_ge(mean_ready, 1)
                nc.vector.scalar_tensor_tensor(x[:, g[0][0], :], two(6), -1.0 / 64, x[:, g[0][0], :],
                                               ALU.mult, ALU.add).then_inc(centred_done, 1)
            for i, g in enumerate(groups):
                dve.wait_ge(sums, i + 1)
                nc.vector.tensor_scalar(inv[:, i, :], two(2 * i), 1.0 / g[1], g[2], ALU.mult, ALU.add).then_inc(meansq, 1)
            for i, g in enumerate(groups):
                dve.wait_ge(rooted, i + 1)
                link(nc.vector.reciprocal(inv[:, i, :], inv[:, i, :]))
                for m, b in enumerate(g[0]):
                    last = nc.vector.scalar_tensor_tensor(x[:, b, :], x[:, b, :], core.v(g[3], m), inv[:, i, :],
                                                          ALU.mult, ALU.mult)
                if g[4]:
                    link(last)
                    nc.vector.tensor_scalar(x[:, g[0][0], :], x[:, g[0][0], :], core.v(g[4], 0), None, ALU.add)
    st.end()


def transposed_blocks(core, name, pairs_of):
    nc = core.nc
    st = Stage(core, name)
    turned, free = st.sem("turned"), st.sem("free")
    groups = [pairs_of[i:i + 4] for i in range(0, len(pairs_of), 4)]
    with nc.Block(name) as block:
        @block.tensor
        def _(pe):
            for n, g in enumerate(groups):
                if n >= 2:
                    pe.wait_ge(free, n - 1)
                for m, (_, src) in enumerate(g):
                    last = nc.tensor.transpose(core.ps[:, n % 2, m * P:(m + 1) * P], src, core.c("eye"))
                last.then_inc(turned, 1)

        @block.scalar
        def _(act):
            for n, g in enumerate(groups):
                act.wait_ge(turned, n + 1)
                for m, (dst, _) in enumerate(g):
                    last = nc.scalar.activation(dst, core.ps[:, n % 2, m * P:m * P + dst.shape[1]], ACT.Copy)
                last.then_inc(free, 1)
    st.end()


def offset(b):
    return P * b * (b + 1) // 2


def index_masks(core, idxT, keysT, weight, masks):
    nc = core.nc
    st = Stage(core, "index")
    relu = st.sb("relu", [P, 2, T])
    score = st.sb("score", [P, 2, T])
    top = st.sb("top", [P, 8])
    logits, rectified, added, d_link, found = (st.sem(x) for x in ("logits", "rectified", "added", "d_link", "found"))
    blocks = list(range(TOPK // P, NT))
    units = [(b, h) for b in blocks for h in range(IDX_HEADS)]
    two = lambda b, w: core.ps[:, b:b + 2, :].rearrange("p a n -> p (a n)")[:, 0:w]
    with nc.Block("index") as block:
        @block.tensor
        def _(pe):
            for n, (b, h) in enumerate(units):
                w = (b + 1) * P
                if n >= 4:
                    pe.wait_ge(rectified, n - 3)
                p0 = 64 * (h % 2)
                for c in range(0, w, HALF):
                    e = min(w, c + HALF)
                    last = nc.tensor.matmul(core.ps[:, 2 * (n % 4) + c // HALF, 0:e - c],
                                            idxT[p0:p0 + 64, h // 2, b * P:(b + 1) * P], keysT[p0:p0 + 64, c:e],
                                            start=True, stop=True)
                last.then_inc(logits, 1)

        @block.scalar
        def _(act):
            for n, (b, h) in enumerate(units):
                w = (b + 1) * P
                act.wait_ge(logits, n + 1)
                if n >= 2:
                    act.wait_ge(added, n - 1)
                nc.scalar.activation(relu[:, n % 2, 0:w], two(2 * (n % 4), w), ACT.Relu).then_inc(rectified, 1)

        @block.vector
        def _(dve):
            link = Links(dve, d_link)
            rounds = 0
            for m, b in enumerate(blocks):
                w = (b + 1) * P
                s = score[:, m % 2, 0:w]
                for h in range(IDX_HEADS):
                    n = IDX_HEADS * m + h
                    dve.wait_ge(rectified, n + 1)
                    if h == 0:
                        nc.vector.tensor_scalar(s, relu[:, n % 2, 0:w], weight[:, b, 0:1], None, ALU.mult).then_inc(added, 1)
                    else:
                        dve.wait_ge(added, n)
                        nc.vector.scalar_tensor_tensor(s, relu[:, n % 2, 0:w], weight[:, b, h:h + 1], s,
                                                       ALU.mult, ALU.add).then_inc(added, 1)
                dve.wait_ge(added, IDX_HEADS * (m + 1))
                link(nc.vector.tensor_tensor(s, s, core.c("causal")[:, T - w:T], ALU.add))
                base = 2 * rounds
                with dve.Fori(0, TOPK // 8, 1) as r:
                    nc.vector.max(top[:, :], s).then_inc(found, 1)
                    dve.wait_ge(found, 2 * r + base + 1)
                    core.settle(dve)
                    nc.vector.match_replace(s, top[:, :], s, TAKEN).then_inc(found, 1)
                    dve.wait_ge(found, 2 * r + base + 2)
                rounds += TOPK // 8
                nc.vector.tensor_scalar(masks[:, offset(b):offset(b) + w], s, TAKEN / 2, NEG, ALU.is_gt, ALU.mult)
    st.end()


def attention(core, name, heads, copies, scores, values, masks, scale, outT):
    nc = core.nc
    st = Stage(core, name)
    masked_s = st.sb("masked", [P, 2, T])
    probs = st.sb("probs", [P, 2, T])
    probsT = st.sb("probsT", [P, 2, T])
    stat = st.sb("stat", [P, 2, 4])
    names = ("fetched", "scored", "masked", "peak", "exps", "total", "scaled", "turned", "placed", "pv", "stored", "drained")
    s = {x: st.sem(x) for x in names}
    units = [(u, b) for u in range(2) for b in range(NT)]
    U = len(units)
    n_copies = len(copies(0, 0)) * 2
    wide = lambda b, w: core.ps[:, b:b + 2, :].rearrange("p a n -> p (a n)")[:, 0:w]
    with nc.Block(name) as block:
        @block.gpsimd
        def _(pool):
            with pool.Fori(0, heads // 2, 1) as i:
                pool.wait_ge(s["drained"], i + 1)
                for u in range(2):
                    for dst, src in copies(2 * i + u, u):
                        nc.gpsimd.tensor_copy(dst, src).then_inc(s["fetched"], 1)

        @block.tensor
        def _(pe):
            pe.sem_inc(s["drained"], 1)
            with pe.Fori(0, heads // 2, 1) as i:
                pe.wait_ge(s["fetched"], (i + 1) * n_copies)
                for k in range(U + 2):
                    if k < U:
                        u, b = units[k]
                        w = (b + 1) * P
                        if k >= 2:
                            pe.wait_ge(s["masked"], i * U + k - 1)
                        ops = scores(u, b, 2 * i + u)
                        for c in range(0, w, HALF):
                            e = min(w, c + HALF)
                            for m, (q, keys) in enumerate(ops):
                                last = nc.tensor.matmul(core.ps[:, 2 * (k % 2) + c // HALF, 0:e - c], q, keys[:, c:e],
                                                        start=(m == 0), stop=(m == len(ops) - 1))
                        last.then_inc(s["scored"], 1)
                    if 1 <= k <= U:
                        u, b = units[k - 1]
                        pe.wait_ge(s["scaled"], i * U + k)
                        if k >= 2:
                            pe.wait_ge(s["placed"], i * U + k - 1)
                        for j in range(b + 1):
                            last = nc.tensor.transpose(wide(4, T)[:, j * P:(j + 1) * P],
                                                       probs[:, (k - 1) % 2, j * P:(j + 1) * P], core.c("eye"))
                        last.then_inc(s["turned"], 1)
                    if k >= 2:
                        u, b = units[k - 2]
                        pe.wait_ge(s["placed"], i * U + k - 1)
                        if k >= 4:
                            pe.wait_ge(s["stored"], i * U + k - 3)
                        for j in range(b + 1):
                            last = nc.tensor.matmul(core.ps[:, 6 + k % 2, 0:P], values(u, j),
                                                    probsT[:, (k - 2) % 2, j * P:(j + 1) * P], start=(j == 0), stop=(j == b))
                        last.then_inc(s["pv"], 1)
                pe.wait_ge(s["stored"], (i + 1) * U)
                pe.sem_inc(s["drained"], 1)

        @block.vector
        def _(dve):
            with dve.Fori(0, heads // 2, 1) as i:
                for k in range(U + 1):
                    if k < U:
                        u, b = units[k]
                        w = (b + 1) * P
                        o = i * U + k
                        dve.wait_ge(s["scored"], o + 1)
                        if k >= 2:
                            dve.wait_ge(s["exps"], o - 1)
                        core.settle(dve)
                        st_k = stat[:, k % 2, :]
                        nc.vector.tensor_tensor_reduce(masked_s[:, k % 2, 0:w], wide(2 * (k % 2), w), masks(b), 1.0, -3.4e38,
                                                       ALU.add, ALU.max, st_k[:, 0:1]).then_inc(s["masked"], 1)
                        dve.wait_ge(s["masked"], o + 1)
                        nc.vector.tensor_scalar(st_k[:, 1:2], st_k[:, 0:1], -scale, None, ALU.mult).then_inc(s["peak"], 1)
                    if k >= 1:
                        u, b = units[k - 1]
                        w = (b + 1) * P
                        o = i * U + k - 1
                        st_k = stat[:, (k - 1) % 2, :]
                        dve.wait_ge(s["exps"], o + 1)
                        nc.vector.reciprocal(st_k[:, 3:4], st_k[:, 2:3]).then_inc(s["total"], 1)
                        dve.wait_ge(s["total"], o + 1)
                        p = probs[:, (k - 1) % 2, 0:w]
                        nc.vector.tensor_scalar(p, p, st_k[:, 3:4], None, ALU.mult).then_inc(s["scaled"], 1)

        @block.scalar
        def _(act):
            with act.Fori(0, heads // 2, 1) as i:
                for k in range(U + 2):
                    if k < U:
                        u, b = units[k]
                        w = (b + 1) * P
                        o = i * U + k
                        act.wait_ge(s["peak"], o + 1)
                        if k >= 2:
                            act.wait_ge(s["turned"], o - 1)
                        nc.scalar.activation(probs[:, k % 2, 0:w], masked_s[:, k % 2, 0:w], ACT.Exp, bias=stat[:, k % 2, 1:2],
                                             scale=scale, accum_out=stat[:, k % 2, 2:3]).then_inc(s["exps"], 1)
                    if 1 <= k <= U:
                        u, b = units[k - 1]
                        w = (b + 1) * P
                        o = i * U + k - 1
                        act.wait_ge(s["turned"], o + 1)
                        if k >= 3:
                            act.wait_ge(s["pv"], o - 1)
                        nc.scalar.activation(probsT[:, (k - 1) % 2, 0:w], wide(4, w), ACT.Copy).then_inc(s["placed"], 1)
                    if k >= 2:
                        u, b = units[k - 2]
                        o = i * U + k - 2
                        act.wait_ge(s["pv"], o + 1)
                        nc.scalar.activation(at(outT, 2 * i + u)[:, b * P:(b + 1) * P], core.ps[:, 6 + k % 2, 0:P],
                                             ACT.Copy).then_inc(s["stored"], 1)
    st.end()


def pair_products(core, name, dst, units, gate=None, scale=1.0, rows=P):
    nc = core.nc
    st = Stage(core, name)
    product, free = st.sem("product"), st.sem("free")
    with nc.Block(name) as block:
        @block.tensor
        def _(pe):
            for n, parts in enumerate(units):
                if n >= 4:
                    pe.wait_ge(free, n - 3)
                for h in range(2):
                    for m, (w, x) in enumerate(parts):
                        last = nc.tensor.matmul(core.ps[0:rows, 2 * (n % 4) + h, :], w, x[:, h * HALF:(h + 1) * HALF],
                                                start=(m == 0), stop=(m == len(parts) - 1))
                last.then_inc(product, 1)

        def ps(n):
            return core.ps[0:rows, 2 * (n % 4):2 * (n % 4) + 2, :].rearrange("p a n -> p (a n)")
        if gate is None:
            @block.scalar
            def _(act):
                for n in range(len(units)):
                    act.wait_ge(product, n + 1)
                    nc.scalar.activation(dst(n), ps(n), ACT.Copy, scale=scale).then_inc(free, 1)
        else:
            @block.vector
            def _(dve):
                for n in range(len(units)):
                    dve.wait_ge(product, n + 1)
                    nc.vector.tensor_tensor(dst(n), ps(n), gate(n), ALU.mult).then_inc(free, 1)
    st.end()


def load(core, name, moves):
    nc = core.nc
    st = Stage(core, name)
    loaded = st.sem("loaded")
    with nc.Block(name) as block:
        @block.sync
        def _(sp):
            for dst, src in moves:
                sp.dma_start(dst, src).then_inc(loaded, 16)
            sp.wait_ge(loaded, 16 * len(moves))
    st.end()


def product_rows(core, name, lhsT, kb, weights, x, source=None, out=None, cols=HALF):
    nc = core.nc
    st = Stage(core, name)
    w = st.sb("w", [P, 2, kb, cols])
    n_cols = D // cols
    loaded = [st.sem(f"loaded{i}") for i in range(2)]
    xin = [st.sem(f"xin{i}") for i in range(n_cols)]
    product, added, written = st.sem("product"), st.sem("added"), st.sem("written")
    wv = weights.rearrange("(k p) n -> p k n", p=P)
    xv = None if source is None else source.rearrange("(b p) n -> p b n", p=P)
    with nc.Block(name) as block:
        @block.sync
        def _(sp):
            for h in range(n_cols):
                c = slice(h * cols, (h + 1) * cols)
                if source is not None:
                    sp.dma_start(x[:, :, c], xv[:, :, c]).then_inc(xin[h], 16)
                if h >= 2:
                    sp.wait_ge(product, (h - 1) * NT)
                sp.dma_start(w[:, h % 2, :, :], wv[:, :, c]).then_inc(loaded[h % 2], 16)
            if out is not None:
                for b in range(NT):
                    sp.wait_ge(added, (n_cols - 1) * NT + b + 1)
                    sp.dma_start(out[b * P:(b + 1) * P, :], x[:, b, :]).then_inc(written, 16)
                sp.wait_ge(written, 16 * NT)

        @block.tensor
        def _(pe):
            for n in range(n_cols * NT):
                h, b = divmod(n, NT)
                if b == 0:
                    pe.wait_ge(loaded[h % 2], 16 * (h // 2 + 1))
                if n >= 8:
                    pe.wait_ge(added, n - 7)
                for k in range(kb):
                    last = nc.tensor.matmul(core.ps[:, n % 8, 0:cols], lhsT[:, k, b * P:(b + 1) * P],
                                            w[:, h % 2, k, :], start=(k == 0), stop=(k == kb - 1))
                last.then_inc(product, 1)

        @block.vector
        def _(dve):
            for n in range(n_cols * NT):
                h, b = divmod(n, NT)
                if source is not None and b == 0:
                    dve.wait_ge(xin[h], 16)
                dve.wait_ge(product, n + 1)
                xs = x[:, b, h * cols:(h + 1) * cols]
                nc.vector.tensor_tensor(xs, xs, core.ps[:, n % 8, 0:cols], ALU.add).then_inc(added, 1)
    st.end()


def norm_rows(core, name, x, gain_row, out=None, keep=True):
    nc = core.nc
    st = Stage(core, name)
    junk = st.sb("junk", [P, D])
    stat = st.sb("stat", [P, 3, NT])
    gain = st.sb("gain", [P, D])
    loaded, summed, mean, root, inverse, normed, written = (
        st.sem(n) for n in ("loaded", "summed", "mean", "root", "inverse", "normed", "written"))
    with nc.Block(name) as block:
        @block.sync
        def _(sp):
            sp.dma_start(gain[:, :], gain_row.to_broadcast([P, D])).then_inc(loaded, 16)
            if out is not None:
                for b in range(NT):
                    sp.wait_ge(normed, b + 1)
                    sp.dma_start(out[b * P:(b + 1) * P, :], x[:, b, :]).then_inc(written, 16)
                sp.wait_ge(written, 16 * NT)

        @block.scalar
        def _(act):
            for b in range(NT):
                if b:
                    act.wait_ge(summed, b)
                nc.scalar.activation(junk[:, :], x[:, b, :], ACT.Square,
                                     accum_out=stat[:, 0, b:b + 1]).then_inc(summed, 1)
            act.wait_ge(mean, 1)
            nc.scalar.activation(stat[:, 2, :], stat[:, 1, :], ACT.Sqrt).then_inc(root, 1)

        @block.vector
        def _(dve):
            dve.wait_ge(summed, NT)
            nc.vector.tensor_scalar(stat[:, 1, :], stat[:, 0, :], 1.0 / D, 1e-6, ALU.mult, ALU.add).then_inc(mean, 1)
            dve.wait_ge(root, 1)
            nc.vector.reciprocal(stat[:, 0, :], stat[:, 2, :]).then_inc(inverse, 1)
            dve.wait_ge(inverse, 1)
            dve.wait_ge(loaded, 16)
            for b in range(NT):
                nc.vector.scalar_tensor_tensor(x[:, b, :], x[:, b, :], stat[:, 0, b:b + 1], gain[:, :],
                                               ALU.mult, ALU.mult).then_inc(normed, 1)
    st.end()


def rope_tables(core, table):
    nc = core.nc
    st = Stage(core, "rope")
    pos_i = st.sb("pos_i", [P, T], I32)
    ang = st.sb("ang", [P, T])
    turns = st.sb("turns", [P, T])
    loaded, d_link, reduced, sines = (st.sem(x) for x in ("loaded", "d_link", "reduced", "sines"))
    c1, c2 = 6.28125, 4059.0 / 2 ** 21
    c3 = 2 * math.pi - c1 - c2
    magic = 12582912.0
    with nc.Block("rope") as block:
        @block.sync
        def _(sp):
            sp.dma_start(pos_i[:, :], core.dram["positions"].to_broadcast([P, T])).then_inc(loaded, 16)

        @block.vector
        def _(dve):
            link = Links(dve, d_link)
            ts = nc.vector.tensor_scalar
            dve.wait_ge(loaded, 16)
            link(nc.vector.tensor_copy(ang[:, :], pos_i[:, :]))
            link(ts(ang[:, :], ang[:, :], core.v("inv", 0), None, ALU.mult))
            link(ts(turns[0:64, :], ang[0:64, :], 1 / (2 * math.pi), 0.25, ALU.mult, ALU.add))
            link(ts(turns[64:P, :], ang[64:P, :], 1 / (2 * math.pi), None, ALU.mult))
            link(ts(turns[:, :], turns[:, :], magic, None, ALU.add))
            link(ts(turns[:, :], turns[:, :], magic, None, ALU.subtract))
            for c in (c1, c2, c3):
                link(nc.vector.scalar_tensor_tensor(ang[:, :], turns[:, :], -c, ang[:, :], ALU.mult, ALU.add))
            link(ts(ang[0:64, :], ang[0:64, :], math.pi / 2, None, ALU.add))
            ts(ang[:, :], ang[:, :], 3.1415925, -3.1415925, ALU.min, ALU.max).then_inc(reduced, 1)
            dve.wait_ge(sines, 1)
            ts(table[64:96, :], table[64:96, :], -1.0, None, ALU.mult)

        @block.scalar
        def _(act):
            act.wait_ge(reduced, 1)
            nc.scalar.activation(table[:, :], ang[:, :], ACT.Sin).then_inc(sines, 1)
    st.end()


def rows_t(core, name, lhsT, kb, weights, dst):
    nc = core.nc
    st = Stage(core, name)
    w = st.sb("w", [P, kb, HALF])
    loaded, product, free = st.sem("loaded"), st.sem("product"), st.sem("free")
    with nc.Block(name) as block:
        @block.sync
        def _(sp):
            sp.dma_start(w[:, :, :], weights).then_inc(loaded, 16)

        @block.tensor
        def _(pe):
            pe.wait_ge(loaded, 16)
            for b in range(NT):
                for k in range(kb):
                    last = nc.tensor.matmul(core.ps[:, b, :], lhsT[:, k, b * P:(b + 1) * P], w[:, k, :],
                                            start=(k == 0), stop=(k == kb - 1))
                last.then_inc(product, 1)

        @block.scalar
        def _(act):
            for b in range(NT):
                act.wait_ge(product, b + 1)
                nc.scalar.activation(dst[:, b, :], core.ps[:, b, :], ACT.Copy)
    st.end()


def rotate(core, name, blocks, table, dst):
    nc = core.nc
    st = Stage(core, name)
    scaled, product, free = st.sem("scaled"), st.sem("product"), st.sem("free")
    with nc.Block(name) as block:
        @block.vector
        def _(dve):
            for n, x in enumerate(blocks):
                nc.vector.tensor_tensor(x, x, table[:, :], ALU.mult).then_inc(scaled, 1)

        @block.tensor
        def _(pe):
            for n, x in enumerate(blocks):
                pe.wait_ge(scaled, n + 1)
                if n >= 4:
                    pe.wait_ge(free, n - 3)
                for h in range(2):
                    last = nc.tensor.matmul(core.ps[0:64, 2 * (n % 4) + h, :], core.c("fold"), x[:, h * HALF:(h + 1) * HALF],
                                            start=True, stop=True)
                last.then_inc(product, 1)

        @block.scalar
        def _(act):
            for n, x in enumerate(blocks):
                act.wait_ge(product, n + 1)
                nc.scalar.activation(dst[0:64, n, :], core.ps[0:64, 2 * (n % 4):2 * (n % 4) + 2, :].rearrange("p a n -> p (a n)"),
                                     ACT.Copy).then_inc(free, 1)
    st.end()


def gates_of_layer(core, name, l, qk, z):
    nc = core.nc
    st = Stage(core, name)
    low = st.sb("low", [P, 8, 4])
    small = st.sb("small", [P, 4, T])
    wide = lambda x: x.rearrange("p a n -> p (a n)")
    shifted, exps, sig, ready, logs, d_link = (st.sem(x) for x in ("shifted", "exps", "sigmoids", "ready", "logs", "d_link"))
    tiny = 2.0 ** -60
    with nc.Block(name) as block:
        @block.scalar
        def _(act):
            act.wait_ge(shifted, 2)
            nc.scalar.activation(low[:, 2:4, :], low[:, 0:2, :], ACT.Exp).then_inc(exps, 1)
            nc.scalar.activation(wide(qk[:, 1]), wide(z), ACT.Sigmoid, scale=-1.0).then_inc(sig, 1)
            act.wait_ge(sig, 1)
            nc.scalar.activation(wide(z), wide(z), ACT.Sigmoid).then_inc(sig, 1)
            act.wait_ge(ready, 2)
            nc.scalar.activation(wide(z), wide(z), ACT.Ln).then_inc(logs, 1)
            nc.scalar.activation(wide(small[:, :, :]), wide(small[:, :, :]), ACT.Ln).then_inc(logs, 1)

        @block.vector
        def _(dve):
            link = Links(dve, d_link)
            tt, ts = nc.vector.tensor_tensor, nc.vector.tensor_scalar
            link(tt(low[:, 4, :], core.vs("lb0"), core.vs("lb1"), ALU.max))
            tt(low[:, 0, :], core.vs("lb0"), low[:, 4, :], ALU.subtract).then_inc(shifted, 1)
            tt(low[:, 1, :], core.vs("lb1"), low[:, 4, :], ALU.subtract).then_inc(shifted, 1)
            dve.wait_ge(exps, 1)
            link(tt(low[:, 4, :], low[:, 2, :], low[:, 3, :], ALU.add))
            link(nc.vector.reciprocal(low[:, 5, :], low[:, 4, :]))
            link(tt(low[:, 2, :], low[:, 2, :], low[:, 5, :], ALU.mult))
            link(tt(low[:, 3, :], low[:, 3, :], low[:, 5, :], ALU.mult))
            if l == 1:
                link(tt(low[:, 6, :], low[:, 2, :], low[:, 3, :], ALU.add))
                link(tt(low[:, 6, :], low[:, 6, :], low[:, 2, :], ALU.subtract))
            else:
                link(tt(low[:, 6, :], low[:, 2, :], low[:, 2, :], ALU.subtract))
            link(ts(low[:, 7, :], low[:, 6, :], -1.0, 1.0, ALU.mult, ALU.add))
            dve.wait_ge(sig, 2)
            for j in range(4):
                ts(qk[:, 1, j, :], qk[:, 1, j, :], low[:, 7, j:j + 1], None, ALU.mult)
                last = ts(z[:, j, :], z[:, j, :], low[:, 7, j:j + 1], low[:, 6, j:j + 1], ALU.mult, ALU.add)
            link(last)
            link(ts(wide(z), wide(z), 1e-30, None, ALU.max))
            ts(wide(small[:, :, :]), wide(z), tiny, 1 / tiny, ALU.min, ALU.mult).then_inc(ready, 1)
            dve.wait_ge(ready, 1)
            ts(wide(z), wide(z), tiny, None, ALU.max).then_inc(ready, 1)
            dve.wait_ge(logs, 2)
            tt(wide(z), wide(z), wide(small[:, :, :]), ALU.add)
    st.end()


def gated_chunks(core, name, qk, rows, oT):
    nc = core.nc
    st = Stage(core, name)
    H = 4
    lv = st.sb("lv", [64, 2, HALF])
    span = st.sb("span", [P, H, 8, CH])
    qs = st.sb("qs", [P, H, 8, CH])
    ks = st.sb("ks", [P, H, 8, CH])
    prod = st.sb("prod", [64, H, 7, CH])
    attn = st.sb("attn", [64, H, CH])
    kt = st.sb("kt", [64, H, P])
    state = st.sb("state", [P, H, P])
    names = ("fetched", "state_new", "summed", "span_exp", "q_ready", "k_ready", "raw", "k_end", "products", "masked", "attn_ready",
             "turned", "k_rows", "o_ready", "o_stored")
    s = {x: st.sem(x) for x in names}
    ps = core.ps
    last_cum = span[:, :, 6, CH - 1:CH]
    with nc.Block(name) as block:
        @block.gpsimd
        def _(pool):
            nc.gpsimd.memset(state[:, :, :], 0.0).then_inc(s["state_new"], H)

            def one(n, u, i):
                pool.wait_ge(s["state_new"], (n + 1) * H)
                nc.gpsimd.tensor_copy(lv[:, :, :], rows[64 * u:64 * u + 64, :, bass.ds(i, 1), :].rearrange("p a b n -> p a (b n)"))                    .then_inc(s["fetched"], 1)
                pool.wait_ge(s["fetched"], n + 1)
                cols = bass.ds(n * CH, CH)
                nc.gpsimd.tensor_copy(ks[:, :, 6, :], qk[:, 1, :, cols]).then_inc(s["raw"], 1)
                nc.gpsimd.tensor_copy(qs[:, :, 7, :], qk[:, 0, :, cols]).then_inc(s["raw"], 1)
                pool.wait_ge(s["span_exp"], n + 1)
                core.settle(pool)
                nc.gpsimd.tensor_tensor(ks[:, :, 7, :], span[:, :, 7, :], qk[:, 1, :, cols], ALU.mult).then_inc(s["k_end"], 1)
            pairs(pool, NCH, one)

        @block.scalar
        def _(act):
            def one(n, u, i):
                act.wait_ge(s["summed"], n + 1)
                nc.scalar.activation(span[:, :, :, :].rearrange("p h l n -> p (h l n)"),
                                     ps[:, 0:4, :].rearrange("p a n -> p (a n)"), ACT.Exp).then_inc(s["span_exp"], 1)
                act.wait_ge(s["turned"], n + 1)
                nc.scalar.activation(kt[:, :, :], ps[0:64, 4, :].rearrange("p (h n) -> p h n", h=H), ACT.Copy).then_inc(s["k_rows"], 1)
                act.wait_ge(s["o_ready"], n + 1)
                nc.scalar.activation(oT[:, :, bass.ds(n * CH, CH)], ps[:, 5, 0:256].rearrange("p (h n) -> p h n", h=H),
                                     ACT.Copy).then_inc(s["o_stored"], 1)
            pairs(act, NCH, one)

        @block.vector
        def _(dve):
            def one(n, u, i):
                cols = bass.ds(n * CH, CH)
                dve.wait_ge(s["span_exp"], n + 1)
                for h in range(H):
                    q = qk[:, 0, h:h + 1, cols].to_broadcast([P, 7, CH])
                    last = nc.vector.tensor_tensor(qs[:, h, 0:7, :], span[:, h, 0:7, :], q, ALU.mult)
                last.then_inc(s["q_ready"], 1)
                for h in range(H):
                    k = qk[:, 1, h:h + 1, cols].to_broadcast([P, 6, CH])
                    last = nc.vector.tensor_tensor(ks[:, h, 0:6, :], span[:, h, 0:6, :], k, ALU.mult)
                last.then_inc(s["k_ready"], 1)
                dve.wait_ge(s["products"], n + 1)
                nc.vector.tensor_tensor(prod[:, :, :, :], ps[0:64, 0:4, :].rearrange("p h (l n) -> p h l n", l=8)[:, :, 0:7],
                                        core.c("decaylevel", 0, 64).rearrange("p (l n) -> p l n", l=7).unsqueeze(1)
                                        .to_broadcast([64, H, 7, CH]), ALU.mult).then_inc(s["masked"], 1)
                dve.wait_ge(s["masked"], n + 1)
                nc.vector.tensor_reduce(attn[:, :, :], prod[:, :, :, :].rearrange("p h l n -> p h n l"), AX, ALU.add)                    .then_inc(s["attn_ready"], 1)
                dve.wait_ge(s["o_ready"], n + 1)
                for h in range(H):
                    nc.vector.scalar_tensor_tensor(state[:, h, :], state[:, h, :], last_cum[:, h, :],
                                                   ps[:, 6, h * P:(h + 1) * P], ALU.mult, ALU.add).then_inc(s["state_new"], 1)
            pairs(dve, NCH, one)

        @block.tensor
        def _(pe):
            mm = nc.tensor.matmul

            def one(n, u, i):
                pe.wait_ge(s["fetched"], n + 1)
                core.settle(pe)
                for h in range(H):
                    last = mm(ps[:, h, :], lv[:, 0, h * P:(h + 1) * P], core.c("spans", 0, 64), start=True, stop=True)
                last.then_inc(s["summed"], 1)
                pe.wait_ge(s["q_ready"], n + 1)
                pe.wait_ge(s["k_ready"], n + 1)
                pe.wait_ge(s["raw"], 2 * (n + 1))
                pe.wait_ge(s["k_end"], n + 1)
                core.settle(pe)
                for h in range(H):
                    for l in range(7):
                        last = mm(ps[0:64, h, l * CH:(l + 1) * CH], ks[:, h, l, :], qs[:, h, l if l < 6 else 7, :], start=True, stop=True)
                last.then_inc(s["products"], 1)
                for h in range(H):
                    last = nc.tensor.transpose(ps[0:64, 4, h * P:(h + 1) * P], ks[:, h, 7, :], core.c("eye"))
                last.then_inc(s["turned"], 1)
                pe.wait_ge(s["k_rows"], n + 1)
                core.settle(pe)
                for h in range(H):
                    last = mm(ps[:, 6, h * P:(h + 1) * P], kt[:, h, :], lv[:, 1, h * P:(h + 1) * P], start=True, stop=True)
                pe.wait_ge(s["attn_ready"], n + 1)
                core.settle(pe)
                for h in range(H):
                    mm(ps[:, 5, h * CH:(h + 1) * CH], state[:, h, :], qs[:, h, 6, :], start=True, stop=False)
                    last = mm(ps[:, 5, h * CH:(h + 1) * CH], lv[:, 1, h * P:(h + 1) * P], attn[:, h, :], start=False, stop=True)
                last.then_inc(s["o_ready"], 1)
                pe.wait_ge(s["o_stored"], n + 1)
                pe.wait_ge(s["state_new"], (n + 2) * H)
            pairs(pe, NCH, one)
    st.end()


def head_norm_gate(core, name, oT, gain, dst):
    nc = core.nc
    st = Stage(core, name)
    sq = st.sb("sq", [P, 4, T])
    wide = lambda x: x.rearrange("p a n -> p (a n)")
    all8 = core.ps[:, :, :].rearrange("p b n -> p (b n)")
    squared, sums, meansq, rooted, d_link = (st.sem(x) for x in ("squared", "sums", "meansq", "rooted", "d_link"))
    with nc.Block(name) as block:
        @block.scalar
        def _(act):
            nc.scalar.activation(wide(sq[:, :, :]), wide(oT), ACT.Square).then_inc(squared, 1)
            act.wait_ge(meansq, 1)
            nc.scalar.activation(wide(sq[:, :, :]), wide(sq[:, :, :]), ACT.Sqrt).then_inc(rooted, 1)

        @block.tensor
        def _(pe):
            pe.wait_ge(squared, 1)
            for j in range(4):
                for h in range(2):
                    last = nc.tensor.matmul(core.ps[:, 2 * j + h, :], core.c("ones"), sq[:, j, h * HALF:(h + 1) * HALF],
                                            start=True, stop=True)
            last.then_inc(sums, 1)

        @block.vector
        def _(dve):
            link = Links(dve, d_link)
            dve.wait_ge(sums, 1)
            nc.vector.tensor_scalar(wide(sq[:, :, :]), all8, 1.0 / P, 1e-6, ALU.mult, ALU.add).then_inc(meansq, 1)
            link(nc.vector.tensor_tensor(wide(dst), wide(dst), wide(oT), ALU.mult))
            dve.wait_ge(rooted, 1)
            link(nc.vector.reciprocal(wide(sq[:, :, :]), wide(sq[:, :, :])))
            nc.vector.scalar_tensor_tensor(wide(dst), wide(dst), gain, wide(sq[:, :, :]), ALU.mult, ALU.mult)
    st.end()


def gated_hidden(core, name, weights, count, xT, hidden):
    nc = core.nc
    st = Stage(core, name)
    w = st.sb("w", [P, 2, 2, KD * P])
    act_out = st.sb("silu", [P, 2, T])
    loaded = [st.sem("loaded0"), st.sem("loaded1")]
    product, silu, done = st.sem("product"), st.sem("silu"), st.sem("done")
    two = lambda b: core.ps[:, b:b + 2, :].rearrange("p a n -> p (a n)")
    with nc.Block(name) as block:
        @block.sync
        def _(sp):
            def fetch(n, u):
                src = weights[n] if isinstance(n, int) else weights[bass.ds(n, 1)].rearrange("a p n -> p (a n)")
                sp.dma_start(w[:, u, :, :].rearrange("p a n -> p (a n)"), src).then_inc(loaded[u], 16)
            fetch(0, 0)
            fetch(1, 1)

            def ahead(n, u, i):
                sp.wait_ge(product, n - 1)
                fetch(n, u)
            pairs(sp, count, ahead, first=2)

        @block.tensor
        def _(pe):
            def one(n, u, i):
                pe.wait_ge(loaded[u], (i + 1) * 16)
                pe.wait_ge(done, n + 1)
                for m in range(2):
                    for k in range(KD):
                        for h in range(2):
                            last = nc.tensor.matmul(core.ps[:, 4 * u + 2 * m + h, :], w[:, u, m, k * P:(k + 1) * P],
                                                    xT[:, k, h * HALF:(h + 1) * HALF], start=(k == 0), stop=(k == KD - 1))
                last.then_inc(product, 1)
            pairs(pe, count, one)

        @block.scalar
        def _(act):
            def one(n, u, i):
                act.wait_ge(product, n + 1)
                act.wait_ge(done, n + 1)
                nc.scalar.activation(act_out[:, u, :], two(4 * u), ACT.Silu).then_inc(silu, 1)
            pairs(act, count, one)

        @block.vector
        def _(dve):
            dve.sem_inc(done, 2)

            def one(n, u, i):
                dve.wait_ge(silu, n + 1)
                nc.vector.tensor_tensor(at(hidden, n), act_out[:, u, :], two(4 * u + 2), ALU.mult).then_inc(done, 1)
            pairs(dve, count, one)
    st.end()


def route(core, xT, gates, slots, experts, tiles):
    nc, d = core.nc, core.dram
    st = Stage(core, "route")
    rw = st.sb("rw", [P, KD, NEXP])
    logits = st.sb("logits", [P, NT, NEXP])
    top = st.sb("top", [P, NT, 8])
    which = st.sb("which", [P, NT, 8], U32)
    whichf = st.sb("whichf", [P, NT, 8])
    hot = st.sb("hot", [P, 2, NT, NEXP])
    both = st.sb("both", [P, NT, NEXP])
    g = st.sb("g", [P, 4, NT])
    rank = st.sb("rank", [P, NT, NEXP])
    ex = st.sb("ex", [P, 6, NEXP])
    over = st.sb("over", [P, NPASS + 1, NEXP])
    left = st.sb("left", [P, NPASS + 1, NEXP])
    ef = st.sb("ef", [P, NPASS + 1])
    first = st.sb("first", [P, NPASS + 1])
    slotf = st.sb("slotf", [P, 2, NT])
    token = st.sb("token", [P, NT], U32)
    zero = st.sb("zero", [P, (NPASS + 1) * SLOTS // P], U32)
    loaded, product, d_link, e_done, counted, ready, cleared, scattered, ranked, diffed = (
        st.sem(x) for x in ("loaded", "product", "d_link", "exp", "counted", "ready", "cleared", "scattered", "ranked", "diffed"))
    with nc.Block("route") as block:
        @block.sync
        def _(sp):
            sp.dma_start(rw[:, :, :], d["router"]).then_inc(loaded, 16)

        @block.tensor
        def _(pe):
            pe.wait_ge(loaded, 16)
            for b in range(NT):
                for k in range(KD):
                    last = nc.tensor.matmul(core.ps[:, 0, b * 8:b * 8 + 8], xT[:, k, b * P:(b + 1) * P], rw[:, k, :],
                                            start=(k == 0), stop=(k == KD - 1))
            last.then_inc(product, 1)
            pe.wait_ge(counted, 1)
            for b in range(NT):
                for e in range(b):
                    nc.tensor.matmul(core.ps[:, 1, b * 8:b * 8 + 8], core.c("ones"), both[:, e, :], start=(e == 0), stop=False)
                nc.tensor.matmul(core.ps[:, 1, b * 8:b * 8 + 8], core.c("earlier"), both[:, b, :], start=(b == 0), stop=True)
            for b in range(NT):
                last = nc.tensor.matmul(core.ps[:, 2, 0:8], core.c("ones"), both[:, b, :], start=(b == 0), stop=(b == NT - 1))
            last.then_inc(ranked, 1)

        @block.scalar
        def _(act):
            act.wait_ge(diffed, 1)
            nc.scalar.activation(g[:, 1, :], g[:, 0, :], ACT.Exp).then_inc(e_done, 1)

        @block.vector
        def _(dve):
            link = Links(dve, d_link)
            tt, ts = nc.vector.tensor_tensor, nc.vector.tensor_scalar
            dve.wait_ge(product, 1)
            link(nc.vector.tensor_copy(logits[:, :, :].rearrange("p a n -> p (a n)"), core.ps[:, 0, 0:64]))
            for b in range(NT):
                link(nc.vector.max(top[:, b, :], logits[:, b, :]))
                link(nc.vector.max_index(which[:, b, :], top[:, b, :], logits[:, b, :]))
            link(nc.vector.tensor_copy(whichf[:, :, :], which[:, :, :]))
            for k in range(2):
                link(tt(hot[:, k, :, :], core.c("iota8").unsqueeze(1).to_broadcast([P, NT, NEXP]),
                        whichf[:, :, k:k + 1].to_broadcast([P, NT, NEXP]), ALU.is_equal))
            tt(both[:, :, :], hot[:, 0, :, :], hot[:, 1, :, :], ALU.add).then_inc(counted, 1)
            tt(g[:, 0, :], top[:, :, 1], top[:, :, 0], ALU.subtract).then_inc(diffed, 1)
            dve.wait_ge(e_done, 1)
            link(ts(g[:, 2, :], g[:, 1, :], 1.0, None, ALU.add))
            link(nc.vector.reciprocal(gates[:, 0, :], g[:, 2, :]))
            link(tt(gates[:, 1, :], gates[:, 0, :], g[:, 1, :], ALU.mult))
            dve.wait_ge(ranked, 1)
            link(nc.vector.tensor_copy(ex[:, 0, :], core.ps[:, 2, 0:8]))
            link(ts(ex[:, 1, :], ex[:, 0, :], 0.0, None, ALU.is_gt))
            for j in range(1, T // SLOTS):
                link(ts(ex[:, 2, :], ex[:, 0, :], float(j * SLOTS), None, ALU.is_gt))
                link(tt(ex[:, 1, :], ex[:, 1, :], ex[:, 2, :], ALU.add))
            link(nc.vector.tensor_tensor_scan(ex[:, 3, :], core.c("ones")[:, 0:NEXP], ex[:, 1, :], 0.0, ALU.mult, ALU.add))
            link(tt(ex[:, 4, :], ex[:, 3, :], ex[:, 1, :], ALU.subtract))
            link(ts(ex[:, 4, :], ex[:, 4, :], float(SLOTS), None, ALU.mult))
            link(tt(rank[:, :, :], core.ps[:, 1, 0:64].rearrange("p (b e) -> p b e", b=NT),
                    ex[:, 4, :].unsqueeze(1).to_broadcast([P, NT, NEXP]), ALU.add))
            for k in range(2):
                link(tt(hot[:, k, :, :], hot[:, k, :, :], rank[:, :, :], ALU.mult))
                link(nc.vector.tensor_reduce(slotf[:, k, :], hot[:, k, :, :], AX, ALU.add))
            link(nc.vector.tensor_copy(slots[:, :, :], slotf[:, :, :]))
            each = [P, NPASS + 1, NEXP]
            by_pass, by_expert = (lambda x: x.unsqueeze(2).to_broadcast(each)), (lambda x: x.unsqueeze(1).to_broadcast(each))
            link(tt(over[:, :, :], by_expert(ex[:, 3, :]), by_pass(core.c("pass")), ALU.is_le))
            link(nc.vector.tensor_reduce(ef[:, :], over[:, :, :], AX, ALU.add))
            link(ts(ef[:, :], ef[:, :], float(NEXP - 1), None, ALU.min))
            link(nc.vector.tensor_copy(experts[:, :], ef[:, :]))
            link(ts(first[:, :], core.c("pass"), float(SLOTS), None, ALU.mult))
            link(tt(left[:, :, :], by_expert(ex[:, 4, :]), by_pass(first[:, :]), ALU.is_le))
            link(tt(over[:, :, :], left[:, :, :], over[:, :, :], ALU.subtract))
            link(tt(ex[:, 5, :], ex[:, 4, :], ex[:, 0, :], ALU.add))
            link(tt(left[:, :, :], by_expert(ex[:, 5, :]), by_pass(first[:, :]), ALU.subtract))
            link(tt(left[:, :, :], left[:, :, :], over[:, :, :], ALU.mult))
            link(nc.vector.tensor_reduce(ef[:, :], left[:, :, :], AX, ALU.add))
            link(ts(first[:, :], ef[:, :], float(P), None, ALU.is_gt))
            link(ts(ef[:, :], ef[:, :], 0.0, None, ALU.is_gt))
            link(tt(ef[:, :], ef[:, :], first[:, :], ALU.add))
            link(nc.vector.tensor_copy(tiles[:, :], ef[:, :]))
            nc.vector.tensor_copy(token[:, :], core.c("tok")).then_inc(ready, 1)

        @block.gpsimd
        def _(pool):
            nc.gpsimd.memset(zero[:, :], 0).then_inc(cleared, 1)
            pool.wait_ge(cleared, 1)
            nc.gpsimd.dma_start(d["slot_token"].rearrange("(p n) one -> p (n one)", p=P), zero[:, :]).then_inc(scattered, 16)
            pool.wait_ge(scattered, 16)
            pool.wait_ge(ready, 1)
            for k in range(2):
                for b in range(NT):
                    nc.gpsimd.indirect_dma_start(
                        d["slot_token"], bass.IndirectOffsetOnAxis(ap=slots[:, k, b:b + 1], axis=0),
                        token[:, b:b + 1], None).then_inc(scattered, 16)
            pool.wait_ge(scattered, 16 * (2 * NT + 1))
    st.end()


def expert_passes(core, experts, tiles):
    nc, d = core.nc, core.dram
    st = Stage(core, "experts")
    NC, NB, AHEAD = EFF // P, 4, 2
    raw = st.sb("raw", [P, NB, 3, D])
    high = st.sb("high", [P, NB, 3, D], F32R)
    low = st.sb("low", [P, NB, 3, D], F32R)
    index = st.sb("index", [P, 2], U32)
    xs = st.sb("xs", [P, 2, D])
    xs_high = st.sb("xs_high", [P, KD, SLOTS], F32R)
    xs_low = st.sb("xs_low", [P, KD, SLOTS], F32R)
    silu = st.sb("silu", [P, 2, SLOTS])
    hid = st.sb("hid", [P, 2, SLOTS])
    hid_high = st.sb("hid_high", [P, 2, SLOTS], F32R)
    hid_low = st.sb("hid_low", [P, 2, SLOTS], F32R)
    y = st.sb("y", [P, 2, D])
    loaded = [st.sem(f"loaded{i}") for i in range(NB)]
    (indexed, gathered, turned, x_high, x_low, rounded, split, product, silu_done, hid_made, hid_rounded, hid_split, down,
     y_copied_a, y_copied_v, written) = (
        st.sem(x) for x in ("indexed", "gathered", "turned", "x_high", "x_low", "rounded", "split", "product", "silu", "hid_made",
                            "hid_rounded", "hid_split", "down", "y_scalar", "y_vector", "written"))
    ps = core.ps
    SPLIT0 = 3 * NB
    bank = lambda u, m, width: ps[:, u % 2, m * SLOTS:m * SLOTS + width]
    rows_psum = ps[:, 2:4, :].rearrange("p b (k n) -> p (b k) n", k=4)

    def chunks(eng, body):
        G = NC // NB
        for u in range(NB):
            body(u, u)
        with eng.Fori(1, G - 1, 1) as g:
            for u in range(NB):
                body(g * NB + u, u)
        for u in range(NB):
            body((G - 1) * NB + u, u)

    def passes(eng, body, otherwise=None):
        with eng.Fori(0, NPASS, 1) as j:
            n = eng.value_load(tiles[0:1, bass.ds(j, 1)], min_val=0, max_val=2)
            with eng.If(n > 1):
                body(j, SLOTS)
            with eng.If(n == 1):
                body(j, P)
            if otherwise is not None:
                with eng.If(n == 0):
                    otherwise(j)

    with nc.Block("experts") as block:
        @block.sync
        def _(sp):
            def fetch(e, f, v):
                row = e * NC + f
                sp.dma_start(raw[:, v, :, :].rearrange("p a n -> p (a n)"), d["experts"][bass.ds(row, 1)].rearrange("a p n -> p (a n)"))\
                    .then_inc(loaded[v], 16)
            first = sp.value_load(experts[0:1, 0:1], min_val=0, max_val=NEXP - 1)
            for f in range(AHEAD):
                fetch(first, f, f)
            with sp.Fori(0, NPASS, 1) as j:
                n = sp.value_load(tiles[0:1, bass.ds(j, 1)], min_val=0, max_val=2)
                with sp.If(n > 0):
                    e = sp.value_load(experts[0:1, bass.ds(j, 1)], min_val=0, max_val=NEXP - 1)
                    e_next = sp.value_load(experts[0:1, bass.ds(j + 1, 1)], min_val=0, max_val=NEXP - 1)

                    def one(f, u):
                        sp.wait_ge(split, 3 * (j * NC + f - 1) + SPLIT0)
                        if isinstance(f, int) and f + AHEAD >= NC:
                            fetch(e_next, f + AHEAD - NC, (u + AHEAD) % NB)
                        else:
                            fetch(e, f + AHEAD, (u + AHEAD) % NB)
                    chunks(sp, one)

        @block.gpsimd
        def _(pool):
            def gather(j):
                for a in range(2):
                    src = d["slot_token"][j * SLOTS + a * P:j * SLOTS + (a + 1) * P, :] if isinstance(j, int) \
                        else d["slot_token"][bass.ds(j * SLOTS + a * P, P), :]
                    nc.gpsimd.dma_start(index[:, a:a + 1], src).then_inc(indexed, 16)
                pool.wait_ge(indexed, 32 * (j + 1))
                core.settle(pool)
                for a in range(2):
                    nc.gpsimd.indirect_dma_start(xs[:, a, :], None, d["h_rows"],
                                                 bass.IndirectOffsetOnAxis(ap=index[:, a:a + 1], axis=0)).then_inc(gathered, 16)
                pool.wait_ge(gathered, 32 * (j + 1))
            gather(0)
            with pool.Fori(0, NPASS, 1) as j:
                n = pool.value_load(tiles[0:1, bass.ds(j, 1)], min_val=0, max_val=2)
                with pool.If(n > 0):
                    pool.wait_ge(turned, 2 * (j + 1))
                    gather(j + 1)

        @block.tensor
        def _(pe):
            pe.sem_inc(down, 2)

            def turn(a):
                for k in range(KD):
                    last = nc.tensor.transpose(rows_psum[:, k, :], xs[:, a, k * P:(k + 1) * P], core.c("eye"))
                last.then_inc(turned, 1)
            pe.wait_ge(gathered, 32)
            turn(0)
            pe.wait_ge(x_low, 1)
            turn(1)

            def one_pass(j, width):
                pe.wait_ge(x_low, 2 * (j + 1))
                core.settle(pe)

                def down_part(f, v, first, last_one):
                    pe.wait_ge(hid_split, j * NC + f + 1)
                    core.settle(pe)
                    for a in range(width // P):
                        for h in range(2):
                            for i, (x, w) in enumerate(((hid_high, high), (hid_high, low), (hid_low, high))):
                                last = nc.tensor.matmul(ps[:, 4 + 2 * a + h, :], x[:, v % 2, a * P:(a + 1) * P],
                                                        w[:, v, 2, h * HALF:(h + 1) * HALF],
                                                        start=first and i == 0, stop=last_one and i == 2)
                    last.then_inc(down, 1)

                def one(f, u):
                    pe.wait_ge(split, 3 * (j * NC + f + 1) + SPLIT0)
                    pe.wait_ge(hid_made, j * NC + f + 1)
                    core.settle(pe)
                    for m in range(2):
                        for k in range(KD):
                            for i, (w, x) in enumerate(((high, xs_high), (high, xs_low), (low, xs_high))):
                                last = nc.tensor.matmul(bank(u, m, width), w[:, u, m, k * P:(k + 1) * P], x[:, k, 0:width],
                                                        start=(k == 0 and i == 0), stop=(k == KD - 1 and i == 2))
                    last.then_inc(product, 1)
                    is_last = isinstance(f, int) and f == NC - 1
                    if is_last:
                        pe.wait_ge(gathered, 32 * (j + 2))
                        core.settle(pe)
                        turn(0)
                    if isinstance(f, int) and f == 1:
                        pe.wait_ge(y_copied_a, 2 * j + 2)
                        pe.wait_ge(y_copied_v, 2 * j + 2)
                    if not (isinstance(f, int) and f == 0):
                        down_part(f - 1, (u - 1) % NB, isinstance(f, int) and f == 1, False)
                    if is_last:
                        pe.wait_ge(x_low, 2 * (j + 1) + 1)
                        core.settle(pe)
                        turn(1)
                        down_part(f, u, False, True)
                chunks(pe, one)
            passes(pe, one_pass)

        @block.scalar
        def _(act):
            act.sem_inc(y_copied_a, 2)

            def round_chunk(n, v):
                act.wait_ge(loaded[v], n)
                for t in range(3):
                    nc.scalar.activation(high[:, v, t, :], raw[:, v, t, :], ACT.Copy).then_inc(rounded, 1)

            def place(a, n):
                act.wait_ge(turned, n)
                nc.scalar.activation(xs_high[:, :, a * P:(a + 1) * P], rows_psum, ACT.Copy).then_inc(x_high, 1)

            def write(j):
                act.dma_start(d["y_slot"][bass.ds(j * SLOTS, SLOTS), :].rearrange("(a p) n -> p a n", p=P), y[:, :, :]).then_inc(written, 16)
            for v in range(AHEAD):
                round_chunk(16, v)
            for a in range(2):
                place(a, a + 1)

            def one_pass(j, width):
                def one(f, u):
                    act.wait_ge(product, j * NC + f + 1)
                    nc.scalar.activation(silu[:, u % 2, 0:width], bank(u, 0, width), ACT.Silu).then_inc(silu_done, 1)
                    if isinstance(f, int) and f == NC - 1:
                        place(0, 2 * (j + 1) + 1)
                    act.wait_ge(down, j * NC + f + 1)
                    act.wait_ge(hid_made, j * NC + f + 3)
                    nc.scalar.activation(hid_high[:, u % 2, 0:width], hid[:, u % 2, 0:width], ACT.Copy).then_inc(hid_rounded, 1)
                    v = (u + AHEAD) % NB
                    round_chunk((j * NC + f + AHEAD - v) * (16 // NB) + 16, v)
                chunks(act, one)
                place(1, 2 * (j + 1) + 2)
                act.wait_ge(down, (j + 1) * NC + 2)
                act.wait_ge(written, 16 * (j + 1))
                for h in range(2 if width > P else 1):
                    nc.scalar.activation(y[:, 0, h * HALF:(h + 1) * HALF], ps[:, 4 + h, :], ACT.Copy)\
                        .then_inc(y_copied_a, 1 if width > P else 2)
                act.wait_ge(y_copied_a, 2 * (j + 2))
                act.wait_ge(y_copied_v, 2 * (j + 2))
                write(j)
            passes(act, one_pass, lambda j: write(j))
            act.wait_ge(written, 16 * (NPASS + 1))

        @block.vector
        def _(dve):
            nc.vector.memset(y[:, :, :], 0.0).then_inc(y_copied_v, 2)
            dve.wait_ge(y_copied_v, 2)
            dve.sem_inc(hid_made, 2)
            dve.sem_inc(written, 16)
            dve.sem_inc(split, SPLIT0)

            def place(a, n):
                dve.wait_ge(x_high, n)
                part = slice(a * P, (a + 1) * P)
                nc.vector.tensor_tensor(xs_low[:, :, part], rows_psum, xs_high[:, :, part].bitcast(F32), ALU.subtract).then_inc(x_low, 1)

            def split_chunk(v, n):
                for t in range(3):
                    dve.wait_ge(rounded, 3 * n + t + 1)
                    nc.vector.tensor_tensor(low[:, v, t, :], raw[:, v, t, :], high[:, v, t, :].bitcast(F32), ALU.subtract).then_inc(split, 1)
            for v in range(AHEAD):
                split_chunk(v, v)
            for a in range(2):
                place(a, a + 1)

            def one_pass(j, width):
                def one(f, u):
                    h = slice(0, width)
                    dve.wait_ge(silu_done, j * NC + f + 1)
                    nc.vector.tensor_tensor(hid[:, u % 2, h], silu[:, u % 2, h], bank(u, 1, width), ALU.mult).then_inc(hid_made, 1)
                    if isinstance(f, int) and f == NC - 1:
                        place(0, 2 * (j + 1) + 1)
                    dve.wait_ge(hid_rounded, j * NC + f + 1)
                    nc.vector.tensor_tensor(hid_low[:, u % 2, h], hid[:, u % 2, h], hid_high[:, u % 2, h].bitcast(F32),
                                            ALU.subtract).then_inc(hid_split, 1)
                    split_chunk((u + AHEAD) % NB, j * NC + f + AHEAD)
                chunks(dve, one)
                place(1, 2 * (j + 1) + 2)
                dve.wait_ge(down, (j + 1) * NC + 2)
                dve.wait_ge(written, 16 * (j + 1))
                if width > P:
                    for h in range(2):
                        nc.vector.tensor_copy(y[:, 1, h * HALF:(h + 1) * HALF], ps[:, 6 + h, :]).then_inc(y_copied_v, 1)
                else:
                    nc.vector.tensor_copy(y[:, 0, HALF:D], ps[:, 5, :]).then_inc(y_copied_v, 2)
            passes(dve, one_pass)
    st.end()


def combine(core, x, source, gates, slots):
    nc, d = core.nc, core.dram
    st = Stage(core, "combine")
    rows = st.sb("rows", [P, 4, D])
    loaded = [st.sem(f"loaded{b}") for b in range(NT)]
    gathered = [st.sem(f"gathered{i}") for i in range(4)]
    added = st.sem("added")
    with nc.Block("combine") as block:
        @block.sync
        def _(sp):
            for b in range(NT):
                sp.dma_start(x[:, b, :], source[b * P:(b + 1) * P, :]).then_inc(loaded[b], 16)

        @block.gpsimd
        def _(pool):
            for n in range(2 * NT):
                b, k = divmod(n, 2)
                if n >= 4:
                    pool.wait_ge(added, n - 3)
                nc.gpsimd.indirect_dma_start(rows[:, n % 4, :], None, d["y_slot"],
                                             bass.IndirectOffsetOnAxis(ap=slots[:, k, b:b + 1], axis=0)).then_inc(gathered[n % 4], 16)

        @block.vector
        def _(dve):
            for n in range(2 * NT):
                b, k = divmod(n, 2)
                if k == 0:
                    dve.wait_ge(loaded[b], 16)
                else:
                    dve.wait_ge(added, n)
                dve.wait_ge(gathered[n % 4], 16 * (n // 4 + 1))
                nc.vector.scalar_tensor_tensor(x[:, b, :], rows[:, n % 4, :], gates[:, k, b:b + 1], x[:, b, :],
                                               ALU.mult, ALU.add).then_inc(added, 1)
    st.end()


def build(nc, dram, dump=None, until=None):
    with ExitStack() as ctx:
        core = Core(nc, dram, ctx)
        load_constants(core)
        first_block(core, dump)
        with nc.sbuf_tensor("rope_table", [P, T], F32) as table:
            rope_tables(core, table)
            source = dram["x_block"]
            for l in range(2):
                mix_layer(core, l, table, source, dram[f"x_mixed{l}"], dump)
                source = dram[f"x_mixed{l}"]
                if l == 0:
                    dense_ffn(core, source, dram["x_ffn"])
                    source = dram["x_ffn"]
            expert_ffn(core, source, dram["out"])


def dense_ffn(core, source, out):
    nc, d = core.nc, core.dram
    nf = DFF // P
    with nc.sbuf_tensor("hidden", [P, nf, T], F32) as hidden:
        with nc.sbuf_tensor("ffn_xT", [P, KD, T], F32) as xT:
            with nc.sbuf_tensor("ffn_x", [P, NT, D], F32) as x:
                norm_transpose(core, "ffn_norm", x, xT, "ffn0", source)
            gated_hidden(core, "dense_up", d["dense_gu"], nf, xT, hidden)
        with nc.sbuf_tensor("ffn_x2", [P, NT, D], F32) as x:
            product_rows(core, "dense_down", hidden, nf, d["dense_down"], x, source, out, cols=256)


def expert_ffn(core, source, out):
    nc, d = core.nc, core.dram
    with nc.sbuf_tensor("gates", [P, 2, NT], F32) as gates, nc.sbuf_tensor("slots", [P, 2, NT], U32) as slots, \
            nc.sbuf_tensor("experts_of", [P, NPASS + 1], U32) as experts, nc.sbuf_tensor("tiles", [P, NPASS + 1], U32) as tiles:
        with nc.sbuf_tensor("moe_xT", [P, KD, T], F32) as xT, nc.sbuf_tensor("moe_x", [P, NT, D], F32) as x:
            norm_transpose(core, "moe_norm", x, xT, "ffn1", source)
            norm_rows(core, "moe_rows", x, d["ffn_g"], d["h_rows"])
            route(core, xT, gates, slots, experts, tiles)
        expert_passes(core, experts, tiles)
        with nc.sbuf_tensor("moe_y", [P, NT, D], F32) as x:
            combine(core, x, source, gates, slots)
            norm_rows(core, "final_norm", x, d["final_norm"], out)


def mix_layer(core, l, table, source, out, dump):
    nc, d = core.nc, core.dram
    with ExitStack() as s1:
        sb = lambda name, shape: s1.enter_context(nc.sbuf_tensor(f"{name}{l}", shape, F32))
        mixT = sb("mixT", [P, 8, T])
        xT = sb("xT", [P, KD, T])
        w_in = d[f"w_in{l}"]
        with nc.sbuf_tensor(f"x{l}", [P, NT, D], F32) as x:
            norm_transpose(core, f"mix_norm{l}", x, xT, f"mix{l}", source)
        with ExitStack() as s2:
            sb2 = lambda name, shape: s2.enter_context(nc.sbuf_tensor(f"{name}{l}", shape, F32))
            turned = sb2("turned", [64, 5, T])
            down = sb2("down", [P, 6, T])
            values = mixT[:, 4:8, :].rearrange("p a n -> p (a n)").rearrange("p (b n) -> p b n", b=NT)
            nope = sb2("nope", [P, 4, T])
            keys = sb2("keys", [P, 4, T])
            gemm_t(core, f"proj_down{l}", w_in, 6, KD, xT, lambda n: at(down, n))
            channel_norms(core, f"mla_norms{l}", down, [((0, 1, 2), 384, 1e-6, f"qa{l}", None),
                                                        ((3, 4), 256, 1e-6, f"kva{l}", None)])
            gemm_t(core, f"up_nope{l}", d[f"w_q{l}"], 4, 3, down, lambda n: at(nope, n))
            with nc.sbuf_tensor(f"pe{l}", [P, 4, T], F32) as pe_blocks:
                gemm_t(core, f"up_pe{l}", d[f"w_q{l}"], 4, 3, down, lambda n: at(pe_blocks, n), first=4)
                rotate(core, f"rotate{l}", [pe_blocks[:, j, :] for j in range(4)] + [down[:, 5, :]], table, turned)
            gemm_t(core, f"up_k{l}", d[f"w_k{l}"], 4, 2, down[:, 3:5], lambda n: at(keys, n))
            rows_t(core, f"up_v{l}", down[:, 3:5], 2, d[f"w_v{l}"], values)
            qbuf = down[:, 0:2, :]
            vbuf = down[:, 2:4, :].rearrange("p u (b n) -> p u b n", b=NT)
            rbuf = down[0:64, 4:6, :]
            attention(core, f"mla{l}", 4,
                      lambda n, u: [(qbuf[:, u, :], at(nope, n)), (rbuf[:, u, :], at(turned, n)),
                                    (vbuf[:, u, :, :], values[:, :, bass.ds(n * P, P)])],
                      lambda u, b, n: [(qbuf[:, u, b * P:(b + 1) * P], at(keys, n)),
                                       (rbuf[:, u, b * P:(b + 1) * P], turned[:, 4, :])],
                      lambda u, j: vbuf[:, u, j, :],
                      lambda b: core.c("causal")[:, T - (b + 1) * P:T], 192 ** -0.5, mixT[:, 0:4, :])
        with ExitStack() as s2:
            sb2 = lambda name, shape: s2.enter_context(nc.sbuf_tensor(f"{name}{l}", shape, F32))
            z = sb2("z", [P, 4, T])
            qk = sb2("qk", [P, 2, 4, T])
            gemm_t(core, f"proj_hq{l}", w_in, 4, KD, xT, lambda n: at(qk[:, 0], n), first=6, func=ACT.Silu)
            gemm_t(core, f"proj_hf{l}", w_in, 4, KD, xT, lambda n: at(z, n), first=10)
            gemm_t(core, f"proj_hg{l}", w_in, 4, KD, xT, lambda n: at(mixT[:, 4:8], n), first=14, func=ACT.Silu)
            gates_of_layer(core, f"gates{l}", l, qk, z)
            rows = sb2("rows", [P, 2, NT, HALF])
            rows_t(core, f"inputs{l}", xT, KD, d[f"w_hi{l}"], rows[:, 1])
            transposed_blocks(core, f"decay_rows{l}", [(rows[:, 0, b, j * P:(j + 1) * P], z[:, j, b * P:(b + 1) * P])
                                                       for b in range(NT) for j in range(4)])
            gated_chunks(core, f"gated{l}", qk, rows, z)
            head_norm_gate(core, f"gated_norm{l}", z[:, :, :], core.v(f"hgn{l}", 0), mixT[:, 4:8, :])
        if dump:
            dump(core, f"mix{l}", mixT[:, :, :].rearrange("p a n -> p (a n)"))
        x = xT[:, :, :].rearrange("p a n -> p (a n)").rearrange("p (b n) -> p b n", b=NT)
        product_rows(core, f"out_proj{l}", mixT, 8, d[f"w_out{l}"], x, source, out)


def first_block(core, dump):
    nc = core.nc
    with ExitStack() as s1:
        sb = lambda name, shape: s1.enter_context(nc.sbuf_tensor(name, shape, F32))
        xT = sb("xT", [P, KD, T])
        mixT = sb("mixT", [P, 8, T])
        weight = sb("index_weight", [P, NT, IDX_HEADS])
        with nc.sbuf_tensor("x_in", [P, NT, D], F32) as x:
            norm_transpose(core, "norm_in", x, xT, "norm_g", core.dram["x"])
        with nc.sbuf_tensor("big", [P, 5, 4, T], F32) as big, nc.sbuf_tensor("bonus", [P, 4, T], F32) as bonus, \
                nc.sbuf_tensor("small", [P, T], F32) as small, \
                nc.sbuf_tensor("decay_end", [P, 4, NCH], F32) as decay_end:
            flat = big[:, :, :, :].rearrange("p a j n -> p (a j) n")
            gemm_t(core, "proj_r", core.dram["w_in"], 4, KD, xT, lambda n: at(flat, n + 4))
            gemm_t(core, "proj_kv", core.dram["w_in"], 8, KD, xT, lambda n: at(flat, n + 12), first=4)
            gemm_t(core, "proj_small", core.dram["w_in"], 1, KD, xT, lambda n: small[:, :], first=12)
            index_weights(core, small, weight)
            shift_tokens(core, big, small, None)
            rwkv_operands(core, big, small, decay_end, bonus, mixT[:, 0:4], mixT[:, 4:8])
            rwkv_chunks(core, big, decay_end, mixT)
            gate = big[:, 0]
            gemm_t(core, "proj_gate", core.dram["w_in"], 4, KD, xT, lambda n: at(gate, n), first=13, func=ACT.Silu)
            rwkv_output(core, big, gate, bonus, mixT)
        index_attention(core, xT, weight, mixT)
        if dump:
            dump(core, "mixT", mixT[:, :, :].rearrange("p a n -> p (a n)"))
        with nc.sbuf_tensor("x_res", [P, NT, D], F32) as x:
            product_rows(core, "out_proj", mixT, 8, core.dram["w_out"], x, core.dram["x"])
            norm_rows(core, "block_norm", x, core.dram["final_g"], core.dram["x_block"])
            if dump:
                dump(core, "x1", x[:, :, :].rearrange("p a n -> p (a n)"))


def index_attention(core, xT, weight, mixT):
    nc, d = core.nc, core.dram
    with ExitStack() as s:
        sb = lambda name, shape: s.enter_context(nc.sbuf_tensor(name, shape, F32))
        down = sb("down", [P, 4, T])
        gate = mixT[:, 4:8, :]
        gemm_t(core, "proj_down", d["w_in"], 4, KD, xT, lambda n: at(down, n), first=17)
        gemm_t(core, "proj_gate2", d["w_in"], 4, KD, xT, lambda n: at(gate, n), first=21, func=ACT.Silu)
        channel_norms(core, "latent_norms", down, [((0, 1), 256, 1e-6, "q_norm_g", None),
                                                   ((2,), 128, 1e-6, "kv_norm_g", None),
                                                   ((3,), 64, 1e-5, "kidx_g", "kidx_b")])
        queries = sb("queries", [P, 6, T])
        gemm_t(core, "up_q", d["w_uq"], 6, 2, down, lambda n: at(queries, n))
        latent = sb("latent", [P, NT, P])
        blk = lambda x, b: x[:, b * P:(b + 1) * P]
        transposed_blocks(core, "latent_rows", [(latent[:, b, :], blk(down[:, 2, :], b)) for b in range(NT)])
        masks = sb("masks", [P, offset(NT)])
        index_masks(core, queries[:, 4:6, :], down[:, 3, :], weight, masks)
        w_uk = sb("uk", [P, 4, P])
        w_uv = sb("uv", [P, 8, P])
        load(core, "absorb_w", [(w_uk[:, :, :], d["w_uk"]), (w_uv[:, :, :], d["w_uv"])])
        q_abs = xT
        half = lambda x, h: x[64 * (h % 2):64 * (h % 2) + 64, h // 2, :]
        pair_products(core, "absorb", lambda n: q_abs[:, n, :], [[(half(w_uk, h), half(queries, h))] for h in range(8)],
                      scale=0.125)
        o_lat = sb("o_lat", [P, 8, T])
        qbuf = queries[:, 0:2, :]
        attention(core, "dsa", 8, lambda n, u: [(qbuf[:, u, :], at(q_abs, n))],
                  lambda u, b, n: [(qbuf[:, u, b * P:(b + 1) * P], down[:, 2, :])],
                  lambda u, j: latent[:, j, :],
                  lambda b: masks[:, offset(b):offset(b + 1)] if b * P >= TOPK else core.c("causal")[:, T - (b + 1) * P:T],
                  1.0, o_lat)
        pair_products(core, "values_up", lambda n: mixT[:, 4 + n, :],
                      [[(w_uv[:, 2 * r, :], o_lat[:, 2 * r, :]), (w_uv[:, 2 * r + 1, :], o_lat[:, 2 * r + 1, :])]
                       for r in range(4)], gate=lambda n: gate[:, n, :])


def index_weights(core, small, weight):
    nc = core.nc
    st = Stage(core, "index_w")
    turned = st.sem("turned")
    with nc.Block("index_w") as block:
        @block.tensor
        def _(pe):
            for b in range(NT):
                last = nc.tensor.transpose(core.ps[:, b // 4, (b % 4) * P:(b % 4 + 1) * P], small[:, b * P:(b + 1) * P], core.c("eye"))
            last.then_inc(turned, 1)

        @block.scalar
        def _(act):
            act.wait_ge(turned, 1)
            for b in range(NT):
                o = (b % 4) * P + 64
                nc.scalar.activation(weight[:, b, :], core.ps[:, b // 4, o:o + IDX_HEADS], ACT.Copy, scale=IDX_HEADS ** -0.5)
    st.end()


def blocks_of(w, cols=P):
    k, n = w.shape
    return np.ascontiguousarray(w.reshape(k // P, P, n // cols, cols).transpose(2, 1, 0, 3).reshape(n // cols, P, (k // P) * cols))


def rows_of(w):
    k, n = w.shape
    return np.ascontiguousarray(w.reshape(k // P, P, n).transpose(1, 0, 2))


def padded(w):
    return np.concatenate([w, np.zeros((w.shape[0], -w.shape[1] % P), w.dtype)], 1)


def constants():
    c = np.zeros((P, NCST), np.float32)
    p = np.arange(P)[:, None]
    q = np.arange(64)[:, None]

    def put(name, value):
        o, w = CST[name]
        value = np.asarray(value, np.float32)
        c[:value.shape[0], o:o + w] = value
    put("eye", np.eye(P))
    put("ones", np.ones((P, P)))
    put("heads", (p // 64) == (np.arange(P)[None] // 64))
    n = np.arange(64)[None]
    put("upto", q <= n)
    put("before", q < n)
    lev = [((q >> (l + 1)) == (n >> (l + 1))) & (((q >> l) & 1) == 1) & (((n >> l) & 1) == 0) for l in range(LEVELS)]
    put("level", np.concatenate(lev, 1))
    put("restart", np.broadcast_to((np.arange(T) % CH != 0), (P, T)))
    put("causal", np.where(np.arange(T)[None] - (T - P) <= p, 0.0, NEG))
    put("decaylevel", np.concatenate([x.T for x in lev] + [q == n], 1))
    put("earlier", p < np.arange(P)[None])
    put("iota8", np.broadcast_to(np.arange(8), (P, 8)))
    put("tok", p + P * np.arange(8)[None])
    put("below8", np.arange(8)[:, None] < np.arange(8)[None])
    put("fold", (p % 64) == n)
    u, t = np.arange(64)[:, None], np.arange(64)[None]
    groups = []
    for l in range(LEVELS):
        mid = (t >> (l + 1) << (l + 1)) + (1 << l) - 1
        groups.append(((u > mid) & (u <= t)) | ((u > t) & (u <= mid)))
    put("spans", np.concatenate(groups + [u <= t, u > t], 1))
    put("pass", np.broadcast_to(np.arange(NPASS + 1), (P, NPASS + 1)))
    return c


def laid_out(a):
    out = {"x": a["x"][0], "constants": constants()}
    w = a["w_in"][0]
    s, g = 1600, 2112
    w_in = np.concatenate([w[:, 0:1536], padded(np.concatenate([w[:, 1536:1600], w[:, 2560:2564]], 1)), w[:, 1600:2112],
                           w[:, 2112:2368], w[:, 2368:2496], w[:, 2496:2560], w[:, 2496:2560], w[:, 2564:3076]], 1)
    out["w_in"] = blocks_of(w_in)
    z = np.zeros((32, 512), np.float32)
    out["w_up"] = np.concatenate([a["w_up"][0], z], 0)
    out["a_up"] = np.concatenate([z, a["a_up"][0]], 0)
    vec = np.zeros((P, NVEC), np.float32)

    def put(name, value):
        o, wd = VEC[name]
        value = np.asarray(value).reshape(-1)
        value = np.concatenate([value, np.zeros(wd * P - value.size, value.dtype)])
        vec[:, o:o + wd] = value.reshape(wd, P).T
    for name in ("norm_g", "w0", "a0", "k_k", "k_a", "r_k", "gn_g", "gn_b", "q_norm_g", "kv_norm_g"):
        put(name, a[name][0])
    put("mu", a["mu_shift"][0])
    put("kidx_g", np.concatenate([a["kidx_g"][0]] * 2))
    put("kidx_b", np.concatenate([a["kidx_b"][0]] * 2))
    for l in range(2):
        put(f"mix{l}", a["mix_norm_2"][l])
        put(f"ffn{l}", a["ffn_norm_2"][l])
        put(f"qa{l}", a["q_a_norm_2"][l])
        put(f"kva{l}", a["kv_a_norm_2"][l])
        put(f"hgn{l}", a["hg_out_norm_2"][l])
        put(f"lb{l}", a["hg_lower_bounds_2"][l])
    inv = (10000.0 ** (-np.arange(0, 64, 2) / 64.0)).astype(np.float32)
    put("inv", np.concatenate([inv] * 4))
    out["vectors"] = vec
    out["positions"] = a["positions_2"]
    for l in range(2):
        w = a["w_in_2"][l]
        pe = w[:, 640:704]
        swap = lambda x: np.concatenate([x[:, 32:], x[:, :32]], 1)
        out[f"w_in{l}"] = blocks_of(np.concatenate([w[:, 0:640], pe, swap(pe), w[:, 704:1728], w[:, 2240:2752]], 1))
        out[f"w_hi{l}"] = rows_of(w[:, 1728:2240])
        wq = a["w_q_b_2"][l].reshape(384, 4, 192)
        out[f"w_q{l}"] = blocks_of(np.concatenate([wq[:, h, 0:128] for h in range(4)] +
                                                  [x for h in range(4) for x in (wq[:, h, 128:], swap(wq[:, h, 128:]))], 1))
        wkv = a["w_kv_b_2"][l].reshape(256, 4, 2, 128)
        out[f"w_k{l}"] = blocks_of(np.ascontiguousarray(wkv[:, :, 0]).reshape(256, 512))
        out[f"w_v{l}"] = rows_of(np.ascontiguousarray(wkv[:, :, 1]).reshape(256, 512))
        out[f"w_out{l}"] = a["w_out_2"][l]
    out["w_uq"] = blocks_of(np.concatenate([a["w_uq"][0], a["w_qidx"][0]], 1))
    out["w_uk"] = np.ascontiguousarray(a["w_uk"][0].transpose(2, 0, 1).reshape(64, 4, 2, P).transpose(2, 0, 1, 3).reshape(P, 4, P))
    uv = np.zeros((P, 8, P), np.float32)
    for h in range(8):
        uv[:, h, 64 * (h % 2):64 * (h % 2) + 64] = a["w_uv"][0][h]
    out["w_uv"] = uv
    out["w_out"] = a["w_out"][0]
    out["final_g"] = a["final_g"][None]
    out["final_norm"] = a["final_norm_2"][None]
    out["ffn_g"] = a["ffn_norm_2"][1:2]
    out["dense_gu"] = np.concatenate([blocks_of(a["dense_w_gate_2"][0]), blocks_of(a["dense_w_up_2"][0])], 2)
    out["dense_down"] = a["dense_w_down_2"][0]
    out["router"] = rows_of(a["moe_router_2"][0])
    nf = EFF // P
    ex = np.empty((NEXP * nf, P, 2 * KD * P + D), np.float32)
    for e in range(NEXP):
        s = slice(e * nf, (e + 1) * nf)
        ex[s, :, 0:D] = blocks_of(a["moe_w_gate_2"][0, e])
        ex[s, :, D:2 * D] = blocks_of(a["moe_w_up_2"][0, e])
        ex[s, :, 2 * D:] = a["moe_w_down_2"][0, e].reshape(nf, P, D)
    out["experts"] = ex
    return out


def kernel(**inputs):
    import concourse.bacc as bacc
    from concourse.bass_utils import run_bass_kernel_spmd

    arrays = laid_out({name: np.asarray(value) for name, value in inputs.items()})
    nc = bacc.Bacc("TRN2", target_bir_lowering=False, num_devices=1)
    dram = {name: nc.dram_tensor(name, a.shape, mybir.dt.from_np(a.dtype), kind="ExternalInput").ap()
            for name, a in arrays.items()}
    for name in ("x_block", "x_mixed0", "x_ffn", "x_mixed1", "h_rows"):
        dram[name] = nc.dram_tensor(name, (T, D), F32).ap()
    dram["y_slot"] = nc.dram_tensor("y_slot", (NPASS * SLOTS, D), F32).ap()
    dram["slot_token"] = nc.dram_tensor("slot_token", ((NPASS + 1) * SLOTS, 1), U32).ap()
    dram["out"] = nc.dram_tensor("out", (T, D), F32, kind="ExternalOutput").ap()
    build(nc, dram)
    result = run_bass_kernel_spmd(nc, [arrays], core_ids=[0])
    return result.results[0]["out"].reshape(1, T, D)
```

```python
import math
from contextlib import ExitStack

import numpy as np
import concourse.bass as bass
from concourse import mybir

F32 = mybir.dt.float32
F32R = mybir.dt.float32r
I32 = mybir.dt.int32
U32 = mybir.dt.uint32
ALU = mybir.AluOpType
ACT = mybir.ActivationFunctionType
AX = mybir.AxisListType.X

T = 1024
D = 1024
P = 128
NT = T // P
KD = D // P
HALF = 512
NEG = -1.0e30
TAKEN = -3.0e38
CH = 64
NCH = T // CH
LEVELS = 6
TOPK = 256
IDX_HEADS = 4
SLOTS = 256
NEXP = 8
NPASS = 2 * T // SLOTS + NEXP - 1
EFF = 3584
DFF = 2816

VEC = {}
_n = 0
for _name, _w in (("norm_g", 8), ("mu", 13), ("w0", 4), ("a0", 4), ("k_k", 4), ("k_a", 4), ("r_k", 4),
                  ("gn_g", 4), ("gn_b", 4), ("q_norm_g", 2), ("kv_norm_g", 1), ("kidx_g", 1), ("kidx_b", 1),
                  ("mix0", 8), ("mix1", 8), ("ffn0", 8), ("ffn1", 8), ("qa0", 3), ("qa1", 3),
                  ("kva0", 2), ("kva1", 2), ("hgn0", 1), ("hgn1", 1), ("lb0", 4), ("lb1", 4), ("inv", 1)):
    VEC[_name] = (_n, _w)
    _n += _w
NVEC = _n

CST = {}
_n = 0
for _name, _w in (("eye", 128), ("ones", 128), ("heads", 128), ("upto", 64), ("before", 64),
                  ("restart", T), ("causal", T), ("decaylevel", 7 * 64),
                  ("earlier", 128), ("iota8", 8), ("tok", 8), ("pass", NPASS + 1), ("fold", 64), ("spans", 512)):
    CST[_name] = (_n, _w)
    _n += _w
NCST = _n


class Links:

    def __init__(self, eng, sem, base=0):
        self.eng, self.sem, self.base, self.n = eng, sem, base, 0

    def __call__(self, ins):
        self.n += 1
        ins.then_inc(self.sem, 1)
        self.eng.wait_ge(self.sem, self.base + self.n)


class Core:

    def __init__(self, nc, dram, ctx):
        self.nc, self.dram, self.ctx = nc, dram, ctx
        self.ps = ctx.enter_context(nc.psum_tensor("ps", [P, 8, HALF], F32))
        self.cst = ctx.enter_context(nc.sbuf_tensor("cst", [P, NCST], F32))
        self.vec = ctx.enter_context(nc.sbuf_tensor("vec", [P, NVEC], F32))

        self.passed = nc.alloc_semaphore("passed")

    def settle(self, eng):
        eng.sem_inc(self.passed, 1)

    def c(self, name, p0=0, p1=P):
        o, w = CST[name]
        return self.cst[p0:p1, o:o + w]

    def v(self, name, j, p0=0, p1=P):
        o, _ = VEC[name]
        return self.vec[p0:p1, o + j:o + j + 1]

    def vs(self, name, p0=0, p1=P):
        o, w = VEC[name]
        return self.vec[p0:p1, o:o + w]


class Stage:

    def __init__(self, core, name):
        self.nc, self.name, self.stack, self.sems = core.nc, name, ExitStack(), []

    def sem(self, name):
        s = self.nc.alloc_semaphore(f"{self.name}_{name}")
        self.sems.append(s)
        return s

    def sb(self, name, shape, dt=F32):
        return self.stack.enter_context(self.nc.sbuf_tensor(f"{self.name}_{name}", shape, dt))

    def end(self):
        self.nc.clear_and_free_semaphores(self.sems)
        self.nc.all_engine_barrier()
        self.stack.close()


def at(x, i):
    if isinstance(i, int):
        return x[:, i]
    names = " ".join(f"d{k}" for k in range(len(x.shape) - 2))
    return x[:, bass.ds(i, 1)].rearrange(f"p one {names} -> p (one d0) {names[2:]}".rstrip())


def pairs(eng, count, body, first=0):
    lo, hi = first // 2, count // 2
    if hi - lo > 1:
        with eng.Fori(lo, hi, 1) as i:
            for u in range(2):
                body(2 * i + u, u, i)
    else:
        for i in range(lo, hi):
            for u in range(2):
                body(2 * i + u, u, i)
    if count % 2 and count > first:
        body(count - 1, 0, count // 2)


def load_constants(core):
    nc, d = core.nc, core.dram
    st = Stage(core, "const")
    loaded = st.sem("loaded")
    with nc.Block("const") as block:
        @block.sync
        def _(sp):
            sp.dma_start(core.cst[:, :], d["constants"]).then_inc(loaded, 16)
            sp.dma_start(core.vec[:, :], d["vectors"]).then_inc(loaded, 16)
            sp.wait_ge(loaded, 32)
    st.end()


def norm_transpose(core, name, x, xT, gain, source=None):
    nc = core.nc
    st = Stage(core, name)
    parts = xT if isinstance(xT, tuple) else None
    whole = st.sb("whole", [P, 2, KD, P]) if parts else None
    made, rounded, rested = st.sem("made"), st.sem("rounded"), st.sem("rested")
    place_at = lambda b: whole[:, b % 2, :, :] if parts else xT[:, :, b * P:(b + 1) * P]
    junk = st.sb("junk", [P, D])
    stat = st.sb("stat", [P, 3, NT])
    xs = st.sb("scaled", [P, 2, D])
    loaded = [st.sem(f"loaded{i}") for i in range(NT)]
    summed, mean, root, inverse = st.sem("summed"), st.sem("mean"), st.sem("root"), st.sem("inverse")
    scaled, turned, placed = st.sem("scaled"), st.sem("turned"), st.sem("placed")
    ps4 = core.ps[:, :, :].rearrange("p (u b) (c n) -> p u (b c) n", u=4, c=4)
    with nc.Block(name) as block:
        if source is not None:
            @block.sync
            def _(sp):
                for b in range(NT):
                    sp.dma_start(x[:, b, :], source[b * P:(b + 1) * P, :]).then_inc(loaded[b], 16)

        @block.scalar
        def _(act):
            for b in range(NT):
                if source is not None:
                    act.wait_ge(loaded[b], 16)
                if b:
                    act.wait_ge(summed, b)
                nc.scalar.activation(junk[:, :], x[:, b, :], ACT.Square,
                                     accum_out=stat[:, 0, b:b + 1]).then_inc(summed, 1)
            act.wait_ge(mean, 1)
            nc.scalar.activation(stat[:, 2, :], stat[:, 1, :], ACT.Sqrt).then_inc(root, 1)
            if parts:
                for b in range(NT):
                    act.wait_ge(made, b + 1)
                    nc.scalar.activation(parts[0][:, :, b * P:(b + 1) * P], whole[:, b % 2, :, :], ACT.Copy).then_inc(rounded, 1)

        @block.vector
        def _(dve):
            dve.wait_ge(summed, NT)
            nc.vector.tensor_scalar(stat[:, 1, :], stat[:, 0, :], 1.0 / D, 1e-6, ALU.mult, ALU.add).then_inc(mean, 1)
            dve.wait_ge(root, 1)
            nc.vector.reciprocal(stat[:, 0, :], stat[:, 2, :]).then_inc(inverse, 1)
            dve.wait_ge(inverse, 1)

            def place(b):
                dve.wait_ge(turned, b + 1)
                if parts and b >= 2:
                    dve.wait_ge(rested, b - 1)
                nc.vector.tensor_tensor(place_at(b), ps4[:, b % 2],
                                        core.vs(gain).unsqueeze(2).to_broadcast([P, KD, P]),
                                        ALU.mult).then_inc(placed, 1)
                if parts:
                    dve.wait_ge(placed, b + 1)
                    dve.sem_inc(made, 1)

            def rest(b):
                dve.wait_ge(rounded, b + 1)
                nc.vector.tensor_tensor(parts[1][:, :, b * P:(b + 1) * P], whole[:, b % 2, :, :],
                                        parts[0][:, :, b * P:(b + 1) * P].bitcast(F32), ALU.subtract).then_inc(rested, 1)
            for b in range(NT):
                if b >= 2:
                    dve.wait_ge(turned, b - 1)
                nc.vector.tensor_scalar(xs[:, b % 2, :], x[:, b, :], stat[:, 0, b:b + 1], None,
                                        ALU.mult).then_inc(scaled, 1)
                if b >= 1:
                    place(b - 1)
                if parts and b >= 2:
                    rest(b - 2)
            place(NT - 1)
            if parts:
                rest(NT - 2)
                rest(NT - 1)

        @block.tensor
        def _(pe):
            for b in range(NT):
                pe.wait_ge(scaled, b + 1)
                if b >= 2:
                    pe.wait_ge(placed, b - 1)
                for k in range(KD):
                    last = nc.tensor.transpose(ps4[:, b % 2, k, :], xs[:, b % 2, k * P:(k + 1) * P], core.c("eye"))
                last.then_inc(turned, 1)
    st.end()


def gemm_t(core, name, weights, count, kb, xT, dest, first=0, func=ACT.Copy):
    nc = core.nc
    st = Stage(core, name)
    w = st.sb("w", [P, 2, kb * P])
    loaded = [st.sem("loaded0"), st.sem("loaded1")]
    product, psum_free = st.sem("product"), st.sem("psum_free")
    with nc.Block(name) as block:
        @block.sync
        def _(sp):
            def load(n, u):
                src = weights[first + n] if isinstance(n, int) else \
                    weights[bass.ds(n + first, 1)].rearrange("a p n -> p (a n)")
                sp.dma_start(w[:, u, :], src).then_inc(loaded[u], 16)
            for n in range(min(2, count)):
                load(n, n)

            def ahead(n, u, i):
                sp.wait_ge(product, n - 1)
                load(n, u)
            pairs(sp, count, ahead, first=2)

        @block.tensor
        def _(pe):
            def one(n, u, i):
                pe.wait_ge(loaded[u], (i + 1) * 16)
                pe.wait_ge(psum_free, n + 1)
                for k in range(kb):
                    for h in range(2):
                        last = nc.tensor.matmul(core.ps[:, 2 * u + h, :], w[:, u, k * P:(k + 1) * P],
                                                xT[:, k, h * HALF:(h + 1) * HALF], start=(k == 0), stop=(k == kb - 1))
                last.then_inc(product, 1)
            pairs(pe, count, one)

        @block.scalar
        def _(act):
            act.sem_inc(psum_free, 2)

            def one(n, u, i):
                act.wait_ge(product, n + 1)
                nc.scalar.activation(dest(n), core.ps[:, 2 * u:2 * u + 2, :].rearrange("p a n -> p (a n)"),
                                     func).then_inc(psum_free, 1)
            pairs(act, count, one)
    st.end()


def projections(core, name, weights, xT, segments):
    nc = core.nc
    st = Stage(core, name)
    raw = st.sb("raw", [P, 2, KD * P])
    high = st.sb("high", [P, 2, KD * P], F32R)
    low = st.sb("low", [P, 2, KD * P], F32R)
    buf = st.sb("buf", [P, 2, T])
    x_high, x_low = xT
    loaded = [st.sem(f"loaded{i}") for i in range(2)]
    stored = [st.sem(f"stored{i}") for i in range(2)]
    rounded, split, product, psum_free = (st.sem(x) for x in ("rounded", "split", "product", "psum_free"))
    total = sum(seg[0] for seg in segments)
    spills = sum(seg[0] for seg in segments if seg[3] is not None)

    def blocks(eng, body):
        base = spilled = 0
        for seg in segments:
            peeled = 2 if base + seg[0] == total and seg[0] % 2 == 0 else 0
            pairs(eng, seg[0] - peeled, lambda n, u, i: body(base + n, u, seg, n, i, spilled))
            for n in range(seg[0] - peeled, seg[0]):
                if peeled:
                    body(base + n, n % 2, seg, n, n // 2, spilled)
            base += seg[0]
            spilled += seg[0] if seg[3] is not None else 0
            assert base % 2 == 0 or base == total

    with nc.Block(name) as block:
        @block.sync
        def _(sp):
            def load(n, u):
                src = weights[n] if isinstance(n, int) else weights[bass.ds(n, 1)].rearrange("a p n -> p (a n)")
                sp.dma_start(raw[:, u, :], src).then_inc(loaded[u], 16)
            for n in range(min(2, total)):
                load(n, n)

            def ahead(n, u, i):
                sp.wait_ge(split, n - 1)
                load(n, u)
            pairs(sp, total, ahead, first=2)

        @block.tensor
        def _(pe):
            def one(n, u, seg, m, i, spilled):
                pe.wait_ge(split, n + 1)
                pe.wait_ge(psum_free, n + 1)
                core.settle(pe)
                for k in range(KD):
                    for j, (w, x) in enumerate(((high, x_high), (high, x_low), (low, x_high))):
                        for h in range(2):
                            last = nc.tensor.matmul(core.ps[:, 2 * u + h, :], w[:, u, k * P:(k + 1) * P],
                                                    x[:, k, h * HALF:(h + 1) * HALF],
                                                    start=(k == 0 and j == 0), stop=(k == KD - 1 and j == 2))
                last.then_inc(product, 1)
            blocks(pe, one)

        @block.scalar
        def _(act):
            act.sem_inc(psum_free, 2)
            for u in range(2):
                act.sem_inc(stored[u], 16)

            def round_block(n_loads, u):
                act.wait_ge(loaded[u], n_loads)
                nc.scalar.activation(high[:, u, :], raw[:, u, :], ACT.Copy).then_inc(rounded, 1)
            round_block(16, 0)

            def one(n, u, seg, m, i, spilled):
                _, func, dest, spill = seg
                if not isinstance(n, int) or n + 1 < total:
                    if not isinstance(n, int) or n >= 1:
                        act.wait_ge(product, n)
                    round_block((n + 1 - (1 - u)) * 8 + 16, 1 - u)
                act.wait_ge(product, n + 1)
                out = dest(m) if spill is None else buf[:, u, :]
                if spill is not None:
                    act.wait_ge(stored[u], 16 * (spilled // 2 + i + 1))
                nc.scalar.activation(out, core.ps[:, 2 * u:2 * u + 2, :].rearrange("p a n -> p (a n)"),
                                     func).then_inc(psum_free, 1)
                if spill is not None:
                    act.wait_ge(psum_free, n + 3)
                    act.dma_start(spill[:, m, :] if isinstance(m, int) else at(spill, m), buf[:, u, :]).then_inc(stored[u], 16)
            blocks(act, one)
            for u in range(2):
                act.wait_ge(stored[u], 16 * (spills // 2 + 1))

        @block.vector
        def _(dve):
            def split_block(n, u):
                dve.wait_ge(rounded, n + 1)
                nc.vector.tensor_tensor(low[:, u, :], raw[:, u, :], high[:, u, :].bitcast(F32), ALU.subtract).then_inc(split, 1)
            pairs(dve, total, lambda n, u, i: split_block(n, u))
    st.end()


def shift_tokens(core, big, small):
    nc = core.nc
    st = Stage(core, "shift")
    diff = st.sb("diff", [P, 2, T])
    subtracted, first_token, step = st.sem("subtracted"), st.sem("first_token"), st.sem("step")
    blocks = [big[:, 1, j] for j in range(4)] + [big[:, 3, j] for j in range(4)] + \
             [big[:, 4, j] for j in range(4)] + [small[:, :]]
    with nc.Block("shift") as block:
        @block.scalar
        def _(act):
            for n, p in enumerate(blocks):
                if n >= 2:
                    act.wait_ge(step, n - 1)
                nc.scalar.activation(diff[:, n % 2, 0:1], p[:, 0:1], ACT.Copy, scale=-1.0).then_inc(first_token, 1)

        @block.gpsimd
        def _(pool):
            for n, p in enumerate(blocks):
                if n >= 2:
                    pool.wait_ge(step, n - 1)
                nc.gpsimd.tensor_tensor(diff[:, n % 2, 1:T], p[:, 0:T - 1], p[:, 1:T], ALU.subtract).then_inc(subtracted, 1)

        @block.vector
        def _(dve):
            for n, p in enumerate(blocks):
                dve.wait_ge(subtracted, n + 1)
                dve.wait_ge(first_token, n + 1)
                nc.vector.scalar_tensor_tensor(p, diff[:, n % 2, :], core.v("mu", n), p, ALU.mult, ALU.add).then_inc(step, 1)
    st.end()


def rwkv_operands(core, big, small, decay_end, bonus, rate, cum):
    nc, d = core.nc, core.dram
    st = Stage(core, "operands")
    tmp = st.sb("tmp", [P, 4, T])
    low = st.sb("low", [64, T])
    up = st.sb("up", [64, 2, 512])
    one_ka = st.sb("one_ka", [P, 4])
    wide = lambda x: x.rearrange("p a n -> p (a n)")
    R, K, V, KK, A = big[:, 1], big[:, 3], big[:, 4], big[:, 0], big[:, 2]
    two = lambda j: core.ps[:, 2 * j:2 * j + 2, :].rearrange("p b n -> p (b n)")
    loaded, lowr, lora, gates, heads = (st.sem(x) for x in ("loaded", "lowrank", "lora", "gates", "heads"))
    d_link, scanned, keyed, squared, rooted, bounded, inverse, unit, eased, keys, removed, products, before, e1, e2, e3, u1 = (
        st.sem(x) for x in ("d_link", "scanned", "keyed", "squared", "rooted", "bounded", "inverse", "unit", "eased", "keys",
                            "removed", "products", "before", "exp_up", "exp_before", "exp_down", "used_up"))
    with nc.Block("operands") as block:
        @block.sync
        def _(sp):
            sp.dma_start(up[:, 0, :], d["w_up"]).then_inc(loaded, 16)
            sp.dma_start(up[:, 1, :], d["a_up"]).then_inc(loaded, 16)
            sp.wait_ge(loaded, 32)

        @block.scalar
        def _(act):
            nc.scalar.activation(low[0:32, :], small[0:32, :], ACT.Tanh).then_inc(lowr, 1)
            nc.scalar.activation(low[32:64, :], small[32:64, :], ACT.Copy).then_inc(lowr, 1)
            for m in range(2):
                for j in range(4):
                    n = 4 * m + j
                    act.wait_ge(lora, n + 1)
                    b = 2 * (n % 4)
                    nc.scalar.activation((rate if m == 0 else A)[:, j, :],
                                         core.ps[:, b:b + 2, :].rearrange("p a n -> p (a n)"), ACT.Sigmoid,
                                         bias=core.v("w0" if m == 0 else "a0", j)).then_inc(gates, 1)
            for j in range(4):
                act.wait_ge(keyed, j + 1)
                nc.scalar.activation(tmp[:, j, :], KK[:, j, :], ACT.Square).then_inc(squared, 1)
            for j in range(4):
                act.wait_ge(heads, j + 1)
                nc.scalar.activation(tmp[:, j, :], two(j), ACT.Sqrt).then_inc(rooted, 1)
            act.wait_ge(scanned, 4)
            for j in range(4):
                act.wait_ge(heads, 4 + j + 1)
                nc.scalar.activation(tmp[:, j, :], cum[:, j, :], ACT.Exp).then_inc(e1, 1)
            for j in range(4):
                act.wait_ge(before, j + 1)
                nc.scalar.activation(rate[:, j, :], rate[:, j, :], ACT.Exp).then_inc(e2, 1)
            for j in range(4):
                act.wait_ge(u1, j + 1)
                nc.scalar.activation(tmp[:, j, :], cum[:, j, :], ACT.Exp, scale=-1.0).then_inc(e3, 1)

        @block.tensor
        def _(pe):
            pe.wait_ge(loaded, 32)
            pe.wait_ge(lowr, 2)
            for m in range(2):
                for j in range(4):
                    n = 4 * m + j
                    if n >= 4:
                        pe.wait_ge(gates, n - 3)
                    for h in range(2):
                        last = nc.tensor.matmul(core.ps[:, 2 * (n % 4) + h, :], up[:, m, j * P:(j + 1) * P],
                                                low[:, h * HALF:(h + 1) * HALF], start=True, stop=True)
                    last.then_inc(lora, 1)

            def head_sums(sem, count):
                for j in range(4):
                    pe.wait_ge(sem, count + j)
                    for h in range(2):
                        last = nc.tensor.matmul(core.ps[:, 2 * j + h, :], core.c("heads"),
                                                tmp[:, j, h * HALF:(h + 1) * HALF], start=True, stop=True)
                    last.then_inc(heads, 1)
            pe.wait_ge(gates, 8)
            head_sums(squared, 1)
            pe.wait_ge(rooted, 4)
            head_sums(products, 1)

        @block.vector
        def _(dve):
            link = Links(dve, d_link)
            for j in range(4):
                nc.vector.tensor_scalar(KK[:, j, :], K[:, j, :], core.v("k_k", j), None, ALU.mult).then_inc(keyed, 1)
            link(nc.vector.tensor_scalar(one_ka[:, :], core.vs("k_a"), -1.0, 1.0, ALU.mult, ALU.add))
            dve.wait_ge(gates, 4)
            link(nc.vector.tensor_scalar(wide(rate[:, :, :]), wide(rate[:, :, :]), -math.exp(-0.5), None, ALU.mult))
            for j in range(4):
                nc.vector.tensor_tensor_scan(cum[:, j, :], core.c("restart"), rate[:, j, :], 0.0,
                                             ALU.mult, ALU.add).then_inc(scanned, 1)
            steps = range(4)
            for j in steps:
                dve.wait_ge(rooted, j + 1)
                nc.vector.tensor_scalar(tmp[:, j, :], tmp[:, j, :], 1e-12, None, ALU.max).then_inc(bounded, 1)
            for j in steps:
                dve.wait_ge(bounded, j + 1)
                nc.vector.reciprocal(tmp[:, j, :], tmp[:, j, :]).then_inc(inverse, 1)
            for j in steps:
                dve.wait_ge(inverse, j + 1)
                nc.vector.tensor_tensor(KK[:, j, :], KK[:, j, :], tmp[:, j, :], ALU.mult).then_inc(unit, 1)
            dve.wait_ge(gates, 8)
            for j in steps:
                dve.wait_ge(unit, j + 1)
                nc.vector.tensor_scalar(tmp[:, j, :], A[:, j, :], core.v("k_a", j), one_ka[:, j:j + 1], ALU.mult, ALU.add).then_inc(eased, 1)
            for j in steps:
                dve.wait_ge(eased, j + 1)
                nc.vector.tensor_tensor(K[:, j, :], K[:, j, :], tmp[:, j, :], ALU.mult).then_inc(keys, 1)
            for j in steps:
                dve.wait_ge(keys, j + 1)
                nc.vector.scalar_tensor_tensor(tmp[:, j, :], R[:, j, :], core.v("r_k", j), K[:, j, :],
                                               ALU.mult, ALU.mult).then_inc(products, 1)
            for j in steps:
                nc.vector.tensor_tensor(A[:, j, :], A[:, j, :], KK[:, j, :], ALU.mult).then_inc(removed, 1)
            dve.wait_ge(scanned, 4)
            for j in steps:
                nc.vector.tensor_tensor(rate[:, j, :], cum[:, j, :], rate[:, j, :], ALU.subtract).then_inc(before, 1)
            for j in steps:
                dve.wait_ge(heads, 4 + j + 1)
                nc.vector.tensor_tensor(bonus[:, j, :], two(j), V[:, j, :], ALU.mult)
            dve.wait_ge(removed, 4)
            for j in steps:
                dve.wait_ge(e1, j + 1)
                nc.vector.tensor_copy(decay_end[:, j, :], tmp[:, j, CH - 1::CH])
                nc.vector.tensor_tensor(R[:, j, :], R[:, j, :], tmp[:, j, :], ALU.mult).then_inc(u1, 1)
            for j in steps:
                dve.wait_ge(e2, j + 1)
                nc.vector.tensor_tensor(KK[:, j, :], KK[:, j, :], rate[:, j, :], ALU.mult)
            for j in steps:
                dve.wait_ge(e3, j + 1)
                nc.vector.tensor_tensor(A[:, j, :], A[:, j, :], tmp[:, j, :], ALU.mult)
                nc.vector.tensor_tensor(K[:, j, :], K[:, j, :], tmp[:, j, :], ALU.mult)
    st.end()


def rwkv_chunks(core, big, decay_end, space):
    nc = core.nc
    st = Stage(core, "chunks")
    R4 = 4
    flat = space[:, :, :].rearrange("p a n -> p (a n)")
    lvl_bd = flat[:, 0:6144].rearrange("p (u l r n) -> p u l r n", u=2, l=LEVELS, r=R4)
    xt_bd = flat[:, 6144:7168].rearrange("p (u r n) -> p u r n", u=2, r=R4)
    k0_bd = flat[:, 7168:8192].rearrange("p (u r n) -> p u r n", u=2, r=R4)
    in_bd = st.sb("in_bd", [P, 2, 4, R4, P])
    tok_bd = st.sb("tok_bd", [P, 2, 3, R4, P])
    tok_v = st.sb("tok_v", [P, 2, R4, CH])
    k1 = st.sb("k1", [P, 2, R4, CH])
    b1 = st.sb("b1", [P, 2, R4, CH])
    xx = st.sb("xx", [P, 2, R4, CH])
    q_bd = st.sb("q_bd", [P, R4, P])
    q = st.sb("q", [P, R4, CH])
    nr = st.sb("nr", [P, R4, CH])
    sa = st.sb("sa", [P, R4, CH])
    sa_bd = st.sb("sa_bd", [P, R4, P])
    state = st.sb("state", [P, R4, CH])
    state_bd = st.sb("state_bd", [P, R4, P])
    names = ("cleared", "fetched", "products", "masked", "turned", "tokened", "q_ready", "q_copied", "q_bd_copied", "upd_ready",
             "updated", "xt_copied", "r_ready", "r_copied", "sa_ready", "sa_copied", "sa_bd_copied", "y_ready", "d_ready", "y_copied",
             "state_sum", "state_new", "state_bd_new")
    s = {x: st.sem(x) for x in names}
    ps = core.ps
    wide = lambda b: ps[:, b, 0:256].rearrange("p (r n) -> p r n", r=R4)
    pair_psum = lambda b: ps[:, b, :].rearrange("p (r m n) -> p r m n", r=R4, m=2)
    halves = [(slice(0, 64), slice(0, 64)), (slice(64, 128), slice(64, 128))]
    L = LEVELS
    fold = core.c("fold")
    later = lambda n, k: not isinstance(n, int) or n >= k

    def steps(eng, body):
        body(0, None, None, 0)
        body(1, 0, None, 1)
        pairs(eng, NCH, lambda p, u, i: body(p, p - 1, p - 2, u), first=2)
        body(None, NCH - 1, NCH - 2, 0)
        body(None, None, NCH - 1, 1)

    MASKS = 10

    with nc.Block("chunks") as block:
        @block.gpsimd
        def _(pool):
            clears = [flat, tok_bd[:, :, :, :, :], in_bd[:, :, :, :, :], q_bd[:, :, :], sa_bd[:, :, :], state_bd[:, :, :], state[:, :, :]]
            for k, x in enumerate(clears):
                nc.gpsimd.memset(x, 0.0).then_inc(s["cleared"], 1)
                pool.wait_ge(s["cleared"], k + 1)
            pool.sem_inc(s["state_new"], 1)

            def fetch(n, u, i):
                cols = bass.ds(n * CH, CH)
                for k, (first, source, sem, count) in enumerate(((1, slice(2, 5), "turned", 3), (0, slice(0, 1), "r_ready", 1))):
                    if later(n, 2):
                        pool.wait_ge(s[sem], count * (n - 1))
                        core.settle(pool)
                    for m, (rows, c) in enumerate(halves):
                        out = in_bd[rows, u, first:first + source.stop - source.start, :, c]
                        nc.gpsimd.tensor_copy(out, big[rows, source, :, cols]).then_inc(s["fetched"], 1)
                        pool.wait_ge(s["fetched"], 4 * n + 2 * k + m + 1)
                        core.settle(pool)
            fetch(0, 0, 0)
            fetch(1, 1, 0)
            pairs(pool, NCH, fetch, first=2)

        @block.tensor
        def _(pe):
            def mm(out, two_heads, moving, start, stop):
                for c in range(2):
                    half = slice(64 * c, 64 * c + 64)
                    last = nc.tensor.matmul(out[half], two_heads[:, half], moving, start=start, stop=stop)
                return last

            pe.wait_ge(s["cleared"], 7)

            def body(p, n, m, u):
                w = 1 - u

                def turn(j):
                    if later(n, 1) or j:
                        pe.wait_ge(s["tokened"], 3 * n + j)
                    core.settle(pe)
                    for r in range(R4):
                        last = nc.tensor.transpose(ps[:, 4, r * P:(r + 1) * P], in_bd[:, w, 1 + j, r, :], core.c("eye"))
                    last.then_inc(s["turned"], 1)

                def q_step(l):
                    pe.wait_ge(*((s["masked"], MASKS * (n + 1)) if l == 0 else (s["updated"], L * n + l)))
                    core.settle(pe)
                    for r in range(R4):
                        last = mm(wide(2)[:, r], lvl_bd[:, w, l, r, :], xx[:, 0, r, :] if l else fold, start=True, stop=True)
                    last.then_inc(s["q_ready"], 1)

                def update_step(l):
                    pe.wait_ge(s["q_copied"], L * n + l + 1)
                    if l:
                        pe.wait_ge(s["xt_copied"], L * n + l)
                    elif later(n, 1):
                        pe.wait_ge(s["updated"], L * n)
                    core.settle(pe)
                    if l < L - 1:
                        for r in range(R4):
                            mm(ps[:, 3, r * CH:(r + 1) * CH], xt_bd[:, w, r, :] if l else core.c("eye"), q[:, r, :], start=True, stop=True)
                    pe.wait_ge(s["q_bd_copied"], L * n + l + 1)
                    core.settle(pe)
                    for r in range(R4):
                        last = mm(ps[:, 3, 256 + r * CH:256 + (r + 1) * CH], q_bd[:, r, :], xx[:, 1, r, :] if l else fold,
                                  start=True, stop=True)
                    last.then_inc(s["upd_ready"], 1)

                def products():
                    pe.wait_ge(s["fetched"], 4 * p + 2)
                    if later(p, 1):
                        pe.wait_ge(s["masked"], MASKS * p)
                    core.settle(pe)
                    for r in range(R4):
                        for a, b in ((1, 0), (2, 1)):
                            last = nc.tensor.matmul(pair_psum(b)[:, r], in_bd[:, u, a, r, :], big[:, 0:2, r, bass.ds(p * CH, CH)],
                                                    start=True, stop=True)
                    last.then_inc(s["products"], 1)

                def removals_start():
                    pe.wait_ge(s["fetched"], 4 * (m + 1))
                    pe.wait_ge(s["tokened"], 3 * (m + 1))
                    pe.wait_ge(s["state_new"], m + 1)
                    core.settle(pe)
                    for r in range(R4):
                        mm(wide(5)[:, r], in_bd[:, u, 0, r, :], state[:, r, :], start=True, stop=False)
                        last = mm(wide(5)[:, r], k0_bd[:, u, r, :], tok_v[:, u, r, :], start=False, stop=True)
                    last.then_inc(s["r_ready"], 1)

                def removals():
                    pe.wait_ge(s["r_copied"], m + 1)
                    pe.wait_ge(s["xt_copied"], L * (m + 1))
                    core.settle(pe)
                    for r in range(R4):
                        last = mm(wide(5)[:, r], xt_bd[:, u, r, :], nr[:, r, :], start=True, stop=True)
                    last.then_inc(s["sa_ready"], 1)

                def outputs():
                    pe.wait_ge(s["sa_bd_copied"], m + 1)
                    if later(m, 1):
                        pe.wait_ge(s["state_bd_new"], m)
                        pe.wait_ge(s["y_copied"], m)
                    core.settle(pe)
                    for r in range(R4):
                        nc.tensor.matmul(wide(6)[:, r], state_bd[:, r, :], big[:, 1, r, bass.ds(m * CH, CH)], start=True, stop=False)
                        mm(wide(6)[:, r], sa_bd[:, r, :], b1[:, u, r, :], start=False, stop=False)
                        last = mm(wide(6)[:, r], tok_bd[:, u, 2, r, :], k1[:, u, r, :], start=False, stop=True)
                    last.then_inc(s["y_ready"], 1)

                def state_change():
                    pe.wait_ge(s["sa_copied"], m + 1)
                    core.settle(pe)
                    for r in range(R4):
                        mm(wide(7)[:, r], tok_bd[:, u, 0, r, :], sa[:, r, :], start=True, stop=False)
                        last = mm(wide(7)[:, r], tok_bd[:, u, 1, r, :], tok_v[:, u, r, :], start=False, stop=True)
                    last.then_inc(s["d_ready"], 1)

                seq = (lambda step: step()) if m is not None else (lambda step: None)
                if n is None and m is None:
                    products()
                elif n is None:
                    for step in (removals_start, removals, outputs, state_change):
                        step()
                else:
                    q_step(0)
                    seq(removals_start)
                    update_step(0)
                    q_step(1)
                    seq(removals)
                    update_step(1)
                    if p is not None:
                        products()
                    q_step(2)
                    seq(outputs)
                    update_step(2)
                    seq(state_change)
                    for l in range(3, L):
                        q_step(l)
                        turn(l - 3)
                        update_step(l)
            steps(pe, body)

        @block.scalar
        def _(act):
            copy = lambda out, x, **k: nc.scalar.activation(out, x, ACT.Copy, **k)

            def both(out, x):
                for rows, c in halves:
                    last = copy(out[rows, :, c], x[rows])
                return last

            def body(p, n, m, u):
                w = 1 - u

                def token(j):
                    act.wait_ge(s["turned"], 3 * n + j + 1)
                    if later(n, 2):
                        act.wait_ge(s["d_ready"], n - 1)
                    x = ps[:, 4, :].rearrange("p (r n) -> p r n", r=R4)
                    last = copy(tok_bd[:, w, j, :, :], x)
                    if j == 2:
                        for rows, c in halves:
                            last = copy(tok_v[rows, w, :, :], x[rows, :, c])
                    last.then_inc(s["tokened"], 1)

                def q_copy(l):
                    act.wait_ge(s["q_copied"], L * n + l + 1)
                    both(q_bd, q).then_inc(s["q_bd_copied"], 1)

                def xt_copy(l):
                    act.wait_ge(s["updated"], L * n + l + 1)
                    if l == 0 and later(n, 2):
                        act.wait_ge(s["sa_ready"], n - 1)
                    both(xt_bd[:, w], xx[:, 1]).then_inc(s["xt_copied"], 1)

                def negate():
                    act.wait_ge(s["r_ready"], m + 1)
                    copy(nr[:, :, :], wide(5), scale=-1.0).then_inc(s["r_copied"], 1)

                def sa_blocks():
                    act.wait_ge(s["sa_copied"], m + 1)
                    both(sa_bd, sa).then_inc(s["sa_bd_copied"], 1)

                def store():
                    act.wait_ge(s["y_ready"], m + 1)
                    copy(big[:, 1, :, bass.ds(m * CH, CH)], wide(6)).then_inc(s["y_copied"], 1)

                def state_blocks():
                    act.wait_ge(s["state_new"], m + 2)
                    both(state_bd, state).then_inc(s["state_bd_new"], 1)

                if n is None:
                    for step in (negate, sa_blocks, store, state_blocks) if m is not None else ():
                        step()
                    return
                with_state = {0: negate, 1: sa_blocks}
                for l in range(L):
                    q_copy(l)
                    if l in with_state and m is not None:
                        with_state[l]()
                    if l == 3 and m is not None:
                        store()
                    xt_copy(l)
                    if l == 3 and m is not None:
                        state_blocks()
                    if l >= 3:
                        token(l - 3)
            act.wait_ge(s["cleared"], 7)
            steps(act, body)

        @block.vector
        def _(dve):
            tt = nc.vector.tensor_tensor

            def body(p, n, m, u):
                small = lambda name, rows: core.c(name)[rows, :].unsqueeze(1).to_broadcast([64, R4, CH])
                full = lambda x: x.unsqueeze(1).to_broadcast([P, R4, CH])

                def q_copy(l):
                    dve.wait_ge(s["q_ready"], L * n + l + 1)
                    nc.vector.tensor_copy(q[:, :, :], wide(2)).then_inc(s["q_copied"], 1)

                def update(l):
                    dve.wait_ge(s["upd_ready"], L * n + l + 1)
                    if l:
                        dve.wait_ge(s["updated"], L * n + l)
                    elif later(n, 1):
                        dve.wait_ge(s["xt_copied"], L * n)
                    k = 0 if l < L - 1 else 1
                    before = xx[:, k:2] if l else fold.unsqueeze(1).unsqueeze(1).to_broadcast([P, 2, R4, CH])
                    tt(xx[:, k:2], before, ps[:, 3, 256 * k:512].rearrange("p (m r n) -> p m r n", m=2 - k, r=R4), ALU.subtract)\
                        .then_inc(s["updated"], 1)

                def mask(k):
                    if k == 0:
                        dve.wait_ge(s["products"], p + 1)
                    if k == 6 and later(p, 2):
                        dve.wait_ge(s["d_ready"], p - 1)
                    if k < 6:
                        l, (rows, c) = 2 * (k // 2), halves[k % 2]
                        tt(lvl_bd[rows, u, l:l + 2, :, c], pair_psum(0)[rows, :, 0, :].unsqueeze(1).to_broadcast([64, 2, R4, CH]),
                           core.c("decaylevel")[rows, l * CH:(l + 2) * CH].rearrange("p (l n) -> p l n", l=2).unsqueeze(2)
                           .to_broadcast([64, 2, R4, CH]), ALU.mult).then_inc(s["masked"], 1)
                    elif k < 8:
                        rows, c = halves[k % 2]
                        tt(k0_bd[rows, u, :, c], pair_psum(1)[rows, :, 0, :], small("before", rows), ALU.mult).then_inc(s["masked"], 1)
                    else:
                        tt((k1, b1)[k - 8][:, u], pair_psum((1, 0)[k - 8])[:, :, 1, :], full(core.c("upto")), ALU.mult)\
                            .then_inc(s["masked"], 1)

                def sa_copy():
                    dve.wait_ge(s["sa_ready"], m + 1)
                    nc.vector.tensor_copy(sa[:, :, :], wide(5)).then_inc(s["sa_copied"], 1)

                def new_state():
                    dve.wait_ge(s["d_ready"], m + 1)
                    tt(state[:, :, :], state[:, :, :], wide(7), ALU.add).then_inc(s["state_sum"], 1)
                    dve.wait_ge(s["state_sum"], m + 1)
                    tt(state[:, :, :], state[:, :, :], decay_end[:, :, bass.ds(m, 1)].to_broadcast([P, R4, CH]), ALU.mult)\
                        .then_inc(s["state_new"], 1)

                if n is None:
                    if m is not None:
                        sa_copy()
                        new_state()
                    else:
                        for k in range(MASKS):
                            mask(k)
                    return
                for l in range(L):
                    q_copy(l)
                    if l == 1 and m is not None:
                        sa_copy()
                    if l == 3 and m is not None:
                        new_state()
                    update(l)
                    if p is not None:
                        for k in {2: (0, 1, 2), 3: (3, 4, 5), 4: (6, 7), 5: (8, 9)}.get(l, ()):
                            mask(k)
            dve.wait_ge(s["cleared"], 7)
            steps(dve, body)
    st.end()


def rwkv_output(core, big, gate, bonus, mixT):
    nc = core.nc
    st = Stage(core, "rwkv_out")
    dev, var = big[:, 2], big[:, 3]
    Y = big[:, 1]
    two = lambda j: core.ps[:, 2 * j:2 * j + 2, :].rearrange("p b n -> p (b n)")
    sums, centred, squared, meanvar, rooted, inverse, normed, scaled, added = (
        st.sem(x) for x in ("sums", "centred", "squared", "meanvar", "rooted", "inverse", "normed", "scaled", "added"))
    with nc.Block("rwkv_out") as block:
        @block.tensor
        def _(pe):
            for m, x in enumerate((Y, var)):
                for j in range(4):
                    if m:
                        pe.wait_ge(squared, j + 1)
                    for h in range(2):
                        last = nc.tensor.matmul(core.ps[:, 2 * j + h, :], core.c("heads"),
                                                x[:, j, h * HALF:(h + 1) * HALF], start=True, stop=True)
                    last.then_inc(sums, 1)

        @block.scalar
        def _(act):
            for j in range(4):
                act.wait_ge(centred, j + 1)
                nc.scalar.activation(var[:, j, :], dev[:, j, :], ACT.Square).then_inc(squared, 1)
            for j in range(4):
                act.wait_ge(meanvar, j + 1)
                nc.scalar.activation(var[:, j, :], var[:, j, :], ACT.Sqrt).then_inc(rooted, 1)

        @block.vector
        def _(dve):
            for j in range(4):
                dve.wait_ge(sums, j + 1)
                nc.vector.scalar_tensor_tensor(dev[:, j, :], two(j), -1.0 / 64, Y[:, j, :], ALU.mult, ALU.add).then_inc(centred, 1)
            for j in range(4):
                dve.wait_ge(sums, 4 + j + 1)
                nc.vector.tensor_scalar(var[:, j, :], two(j), 1.0 / 64, 64e-5, ALU.mult, ALU.add).then_inc(meanvar, 1)
            for j in range(4):
                dve.wait_ge(rooted, j + 1)
                nc.vector.reciprocal(var[:, j, :], var[:, j, :]).then_inc(inverse, 1)
            for j in range(4):
                dve.wait_ge(inverse, j + 1)
                nc.vector.tensor_tensor(dev[:, j, :], dev[:, j, :], var[:, j, :], ALU.mult).then_inc(normed, 1)
            for j in range(4):
                dve.wait_ge(normed, j + 1)
                nc.vector.tensor_scalar(dev[:, j, :], dev[:, j, :], core.v("gn_g", j), core.v("gn_b", j), ALU.mult, ALU.add)\
                    .then_inc(scaled, 1)
            for j in range(4):
                dve.wait_ge(scaled, j + 1)
                nc.vector.tensor_tensor(dev[:, j, :], dev[:, j, :], bonus[:, j, :], ALU.add).then_inc(added, 1)
            for j in range(4):
                dve.wait_ge(added, j + 1)
                nc.vector.tensor_tensor(mixT[:, j, :], gate[:, j, :], dev[:, j, :], ALU.mult)
    st.end()


def channel_norms(core, name, x, groups):
    nc = core.nc
    st = Stage(core, name)
    n_blocks = max(max(g[0]) for g in groups) + 1
    sq = st.sb("sq", [P, n_blocks, T])
    inv = st.sb("inv", [P, len(groups), T])
    mean_ready, centred_done, squared, sums, meansq, rooted, d_link = (
        st.sem(x) for x in ("mean_ready", "centred", "squared", "sums", "meansq", "rooted", "d_link"))
    two = lambda b: core.ps[:, b:b + 2, :].rearrange("p a n -> p (a n)")
    halves = lambda y, h: y[:, h * HALF:(h + 1) * HALF]
    centred = [(i, g) for i, g in enumerate(groups) if g[4]]
    with nc.Block(name) as block:
        @block.tensor
        def _(pe):
            for i, g in centred:
                for h in range(2):
                    last = nc.tensor.matmul(core.ps[:, 6 + h, :], core.c("heads"), halves(x[:, g[0][0], :], h), start=True, stop=True)
                last.then_inc(mean_ready, 1)
            done = 0
            for i, g in enumerate(groups):
                done += len(g[0])
                pe.wait_ge(squared, done)
                for h in range(2):
                    for m, b in enumerate(g[0]):
                        last = nc.tensor.matmul(core.ps[:, 2 * i + h, :], core.c("heads" if g[4] else "ones"),
                                                halves(sq[:, b, :], h), start=(m == 0), stop=(m == len(g[0]) - 1))
                last.then_inc(sums, 1)

        @block.scalar
        def _(act):
            for i, g in enumerate(groups):
                if g[4]:
                    act.wait_ge(centred_done, 1)
                for b in g[0]:
                    nc.scalar.activation(sq[:, b, :], x[:, b, :], ACT.Square).then_inc(squared, 1)
            for i, g in enumerate(groups):
                act.wait_ge(meansq, i + 1)
                nc.scalar.activation(inv[:, i, :], inv[:, i, :], ACT.Sqrt).then_inc(rooted, 1)

        @block.vector
        def _(dve):
            link = Links(dve, d_link)
            for i, g in centred:
                dve.wait_ge(mean_ready, 1)
                nc.vector.scalar_tensor_tensor(x[:, g[0][0], :], two(6), -1.0 / 64, x[:, g[0][0], :],
                                               ALU.mult, ALU.add).then_inc(centred_done, 1)
            for i, g in enumerate(groups):
                dve.wait_ge(sums, i + 1)
                nc.vector.tensor_scalar(inv[:, i, :], two(2 * i), 1.0 / g[1], g[2], ALU.mult, ALU.add).then_inc(meansq, 1)
            for i, g in enumerate(groups):
                dve.wait_ge(rooted, i + 1)
                link(nc.vector.reciprocal(inv[:, i, :], inv[:, i, :]))
                for m, b in enumerate(g[0]):
                    last = nc.vector.scalar_tensor_tensor(x[:, b, :], x[:, b, :], core.v(g[3], m), inv[:, i, :],
                                                          ALU.mult, ALU.mult)
                if g[4]:
                    link(last)
                    nc.vector.tensor_scalar(x[:, g[0][0], :], x[:, g[0][0], :], core.v(g[4], 0), None, ALU.add)
    st.end()


def transposed_blocks(core, name, pairs_of):
    nc = core.nc
    st = Stage(core, name)
    turned, free = st.sem("turned"), st.sem("free")
    groups = [pairs_of[i:i + 4] for i in range(0, len(pairs_of), 4)]
    with nc.Block(name) as block:
        @block.tensor
        def _(pe):
            for n, g in enumerate(groups):
                if n >= 2:
                    pe.wait_ge(free, n - 1)
                for m, (_, src) in enumerate(g):
                    last = nc.tensor.transpose(core.ps[:, n % 2, m * P:(m + 1) * P], src, core.c("eye"))
                last.then_inc(turned, 1)

        @block.scalar
        def _(act):
            for n, g in enumerate(groups):
                act.wait_ge(turned, n + 1)
                for m, (dst, _) in enumerate(g):
                    last = nc.scalar.activation(dst, core.ps[:, n % 2, m * P:m * P + dst.shape[1]], ACT.Copy)
                last.then_inc(free, 1)
    st.end()


def offset(b):
    return P * b * (b + 1) // 2


def index_masks(core, idxT, keysT, weight, masks):
    nc = core.nc
    st = Stage(core, "index")
    relu = st.sb("relu", [P, 2, T])
    blocks = list(range(TOPK // P, NT))
    top = st.sb("top", [P, len(blocks), 8])
    logits, rectified, added, d_link = (st.sem(x) for x in ("logits", "rectified", "added", "d_link"))
    found = [st.sem(f"found{b}") for b in blocks]
    units = [(b, h) for b in blocks for h in range(IDX_HEADS)]
    two = lambda b, w: core.ps[:, b:b + 2, :].rearrange("p a n -> p (a n)")[:, 0:w]
    with nc.Block("index") as block:
        @block.tensor
        def _(pe):
            for n, (b, h) in enumerate(units):
                w = (b + 1) * P
                if n >= 4:
                    pe.wait_ge(rectified, n - 3)
                p0 = 64 * (h % 2)
                for c in range(0, w, HALF):
                    e = min(w, c + HALF)
                    last = nc.tensor.matmul(core.ps[:, 2 * (n % 4) + c // HALF, 0:e - c],
                                            idxT[p0:p0 + 64, h // 2, b * P:(b + 1) * P], keysT[p0:p0 + 64, c:e],
                                            start=True, stop=True)
                last.then_inc(logits, 1)

        @block.scalar
        def _(act):
            for n, (b, h) in enumerate(units):
                w = (b + 1) * P
                act.wait_ge(logits, n + 1)
                if n >= 2:
                    act.wait_ge(added, n - 1)
                nc.scalar.activation(relu[:, n % 2, 0:w], two(2 * (n % 4), w), ACT.Relu).then_inc(rectified, 1)

        @block.vector
        def _(dve):
            link = Links(dve, d_link)
            scores = [masks[:, offset(b):offset(b + 1)] for b in blocks]
            for m, b in enumerate(blocks):
                w = (b + 1) * P
                for h in range(IDX_HEADS):
                    n = IDX_HEADS * m + h
                    dve.wait_ge(rectified, n + 1)
                    if h == 0:
                        nc.vector.tensor_scalar(scores[m], relu[:, n % 2, 0:w], weight[:, b, 0:1], None, ALU.mult).then_inc(added, 1)
                    else:
                        dve.wait_ge(added, n)
                        nc.vector.scalar_tensor_tensor(scores[m], relu[:, n % 2, 0:w], weight[:, b, h:h + 1], scores[m],
                                                       ALU.mult, ALU.add).then_inc(added, 1)
                dve.wait_ge(added, IDX_HEADS * (m + 1))
                link(nc.vector.tensor_tensor(scores[m], scores[m], core.c("causal")[:, T - w:T], ALU.add))
            with dve.Fori(0, TOPK // 8, 1) as r:
                for m, x in enumerate(scores):
                    nc.vector.max(top[:, m, :], x).then_inc(found[m], 1)
                for m, x in enumerate(scores):
                    dve.wait_ge(found[m], 2 * r + 1)
                    core.settle(dve)
                    nc.vector.match_replace(x, top[:, m, :], x, TAKEN).then_inc(found[m], 1)
                for m in range(len(scores)):
                    dve.wait_ge(found[m], 2 * r + 2)
            x = masks[:, offset(blocks[0]):offset(NT)]
            nc.vector.tensor_scalar(x, x, TAKEN / 2, NEG, ALU.is_gt, ALU.mult)
    st.end()


def attention(core, name, heads, copies, scores, values, masks, scale, outT):
    nc = core.nc
    st = Stage(core, name)
    masked_s = st.sb("masked", [P, 2, T])
    probs = st.sb("probs", [P, 2, T])
    probsT = st.sb("probsT", [P, 2, T])
    stat = st.sb("stat", [P, 2, 4])
    names = ("fetched_a", "fetched_v", "scored", "masked", "peak", "exps", "total", "scaled", "turned", "placed", "pv", "stored", "drained")
    s = {x: st.sem(x) for x in names}
    units = [(u, b) for u in range(2) for b in range(NT)]
    U = len(units)
    n_copies = len(copies(0, 0))
    wide = lambda b, w: core.ps[:, b:b + 2, :].rearrange("p a n -> p (a n)")[:, 0:w]
    with nc.Block(name) as block:
        @block.tensor
        def _(pe):
            pe.sem_inc(s["drained"], 1)
            with pe.Fori(0, heads // 2, 1) as i:
                pe.wait_ge(s["fetched_a"], (i + 1) * n_copies)
                pe.wait_ge(s["fetched_v"], (i + 1) * n_copies)
                core.settle(pe)
                for k in range(U + 3):
                    if k < U:
                        u, b = units[k]
                        w = (b + 1) * P
                        if k >= 2:
                            pe.wait_ge(s["masked"], i * U + k - 1)
                        ops = scores(u, b, 2 * i + u)
                        for c in range(0, w, HALF):
                            e = min(w, c + HALF)
                            for m, (q, keys) in enumerate(ops):
                                last = nc.tensor.matmul(core.ps[:, 2 * (k % 2) + c // HALF, 0:e - c], q, keys[:, c:e],
                                                        start=(m == 0), stop=(m == len(ops) - 1))
                        last.then_inc(s["scored"], 1)
                    if 0 <= k - 2 < U:
                        u, b = units[k - 2]
                        pe.wait_ge(s["scaled"], i * U + k - 1)
                        if k >= 3:
                            pe.wait_ge(s["placed"], i * U + k - 2)
                        for j in range(b + 1):
                            last = nc.tensor.transpose(wide(4, T)[:, j * P:(j + 1) * P],
                                                       probs[:, k % 2, j * P:(j + 1) * P], core.c("eye"))
                        last.then_inc(s["turned"], 1)
                    if k >= 3:
                        u, b = units[k - 3]
                        pe.wait_ge(s["placed"], i * U + k - 2)
                        if k >= 5:
                            pe.wait_ge(s["stored"], i * U + k - 4)
                        for j in range(b + 1):
                            last = nc.tensor.matmul(core.ps[:, 6 + (k - 3) % 2, 0:P], values(u, j),
                                                    probsT[:, (k - 3) % 2, j * P:(j + 1) * P], start=(j == 0), stop=(j == b))
                        last.then_inc(s["pv"], 1)
                pe.wait_ge(s["stored"], (i + 1) * U)
                pe.sem_inc(s["drained"], 1)

        @block.vector
        def _(dve):
            with dve.Fori(0, heads // 2, 1) as i:
                dve.wait_ge(s["drained"], i + 1)
                core.settle(dve)
                for dst, src in copies(2 * i + 1, 1):
                    nc.vector.tensor_copy(dst, src).then_inc(s["fetched_v"], 1)
                for k in range(U + 1):
                    if k < U:
                        u, b = units[k]
                        w = (b + 1) * P
                        o = i * U + k
                        dve.wait_ge(s["scored"], o + 1)
                        if k >= 2:
                            dve.wait_ge(s["exps"], o - 1)
                        core.settle(dve)
                        st_k = stat[:, k % 2, :]
                        nc.vector.tensor_tensor_reduce(masked_s[:, k % 2, 0:w], wide(2 * (k % 2), w), masks(b), 1.0, -3.4e38,
                                                       ALU.add, ALU.max, st_k[:, 0:1]).then_inc(s["masked"], 1)
                        dve.wait_ge(s["masked"], o + 1)
                        nc.vector.tensor_scalar(st_k[:, 1:2], st_k[:, 0:1], -scale, None, ALU.mult).then_inc(s["peak"], 1)
                    if k >= 1:
                        u, b = units[k - 1]
                        w = (b + 1) * P
                        o = i * U + k - 1
                        st_k = stat[:, (k - 1) % 2, :]
                        dve.wait_ge(s["exps"], o + 1)
                        nc.vector.reciprocal(st_k[:, 3:4], st_k[:, 2:3]).then_inc(s["total"], 1)
                        dve.wait_ge(s["total"], o + 1)
                        p = probs[:, (k - 1) % 2, 0:w]
                        nc.vector.tensor_scalar(p, p, st_k[:, 3:4], None, ALU.mult).then_inc(s["scaled"], 1)

        @block.scalar
        def _(act):
            with act.Fori(0, heads // 2, 1) as i:
                act.wait_ge(s["drained"], i + 1)
                core.settle(act)
                for dst, src in copies(2 * i, 0):
                    nc.scalar.activation(dst, src, ACT.Copy).then_inc(s["fetched_a"], 1)
                for k in range(U + 3):
                    if 0 <= k - 2 < U:
                        b = units[k - 2][1]
                        w = (b + 1) * P
                        act.wait_ge(s["turned"], i * U + k - 1)
                        if k >= 4:
                            act.wait_ge(s["pv"], i * U + k - 3)
                        nc.scalar.activation(probsT[:, k % 2, 0:w], wide(4, w), ACT.Copy).then_inc(s["placed"], 1)
                    if k < U:
                        w = (units[k][1] + 1) * P
                        act.wait_ge(s["peak"], i * U + k + 1)
                        nc.scalar.activation(probs[:, k % 2, 0:w], masked_s[:, k % 2, 0:w], ACT.Exp, bias=stat[:, k % 2, 1:2],
                                             scale=scale, accum_out=stat[:, k % 2, 2:3]).then_inc(s["exps"], 1)
                    if k >= 3:
                        u, b = units[k - 3]
                        act.wait_ge(s["pv"], i * U + k - 2)
                        nc.scalar.activation(at(outT, 2 * i + u)[:, b * P:(b + 1) * P], core.ps[:, 6 + (k - 3) % 2, 0:P],
                                             ACT.Copy).then_inc(s["stored"], 1)
    st.end()


def pair_products(core, name, dst, units, gate=None, scale=1.0, rows=P):
    nc = core.nc
    st = Stage(core, name)
    product, free = st.sem("product"), st.sem("free")
    with nc.Block(name) as block:
        @block.tensor
        def _(pe):
            for n, parts in enumerate(units):
                if n >= 4:
                    pe.wait_ge(free, n - 3)
                for h in range(2):
                    for m, (w, x) in enumerate(parts):
                        last = nc.tensor.matmul(core.ps[0:rows, 2 * (n % 4) + h, :], w, x[:, h * HALF:(h + 1) * HALF],
                                                start=(m == 0), stop=(m == len(parts) - 1))
                last.then_inc(product, 1)

        def ps(n):
            return core.ps[0:rows, 2 * (n % 4):2 * (n % 4) + 2, :].rearrange("p a n -> p (a n)")
        if gate is None:
            @block.scalar
            def _(act):
                for n in range(len(units)):
                    act.wait_ge(product, n + 1)
                    nc.scalar.activation(dst(n), ps(n), ACT.Copy, scale=scale).then_inc(free, 1)
        else:
            @block.vector
            def _(dve):
                for n in range(len(units)):
                    dve.wait_ge(product, n + 1)
                    nc.vector.tensor_tensor(dst(n), ps(n), gate(n), ALU.mult).then_inc(free, 1)
    st.end()


def load(core, name, moves):
    nc = core.nc
    st = Stage(core, name)
    loaded = st.sem("loaded")
    with nc.Block(name) as block:
        @block.sync
        def _(sp):
            for dst, src in moves:
                sp.dma_start(dst, src).then_inc(loaded, 16)
            sp.wait_ge(loaded, 16 * len(moves))
    st.end()


def product_rows(core, name, lhsT, kb, weights, n_half, dst, source=None, out=None):
    nc = core.nc
    st = Stage(core, name)
    whole = not isinstance(lhsT, tuple)
    N = n_half * kb
    raw = st.sb("raw", [P, 2, HALF])
    high = st.sb("high", [P, 2, HALF], F32R)
    low = st.sb("low", [P, 2, HALF], F32R)
    x_high = st.sb("x_high", [P, 2, T], F32R) if whole else None
    x_low = st.sb("x_low", [P, 2, T], F32R) if whole else None
    loaded = [st.sem(f"loaded{i}") for i in range(2)]
    xin = [st.sem(f"xin{i}") for i in range(n_half)]
    rounded, split, used, product, added, written = (st.sem(x) for x in ("rounded", "split", "used", "product", "added", "written"))
    with nc.Block(name) as block:
        @block.sync
        def _(sp):
            for n in range(N):
                h, k = divmod(n, kb)
                if n >= 2:
                    sp.wait_ge(split, n - 1)
                sp.dma_start(raw[:, n % 2, :], weights[k * P:(k + 1) * P, h * HALF:(h + 1) * HALF]).then_inc(loaded[n % 2], 16)
                if k == 0 and source is not None:
                    c = slice(h * HALF, (h + 1) * HALF)
                    sp.dma_start(dst[:, :, c], source.rearrange("(b p) n -> p b n", p=P)[:, :, c]).then_inc(xin[h], 16)
            if out is not None:
                for b in range(NT):
                    sp.wait_ge(added, (n_half - 1) * NT + b + 1)
                    sp.dma_start(out[b * P:(b + 1) * P, :], dst[:, b, :]).then_inc(written, 16)
                sp.wait_ge(written, 16 * NT)

        @block.tensor
        def _(pe):
            for n in range(N):
                h, k = divmod(n, kb)
                pe.wait_ge(split, n + 1)
                for b in range(NT):
                    if k == 0 and h > 0:
                        pe.wait_ge(added, (h - 1) * NT + b + 1)
                    c = slice(b * P, (b + 1) * P)
                    xh, xl = (x_high[:, n % 2, c], x_low[:, n % 2, c]) if whole else (lhsT[0][:, k, c], lhsT[1][:, k, c])
                    for j, (x, w) in enumerate(((xh, high), (xh, low), (xl, high))):
                        last = nc.tensor.matmul(core.ps[:, b, :], x, w[:, n % 2, :],
                                                start=(k == 0 and j == 0), stop=(k == kb - 1 and j == 2))
                    if k == kb - 1:
                        last.then_inc(product, 1)
                        if b == NT - 1:
                            pe.wait_ge(product, (h + 1) * NT)
                            pe.sem_inc(used, 1)
                    elif b == NT - 1:
                        last.then_inc(used, 1)

        @block.scalar
        def _(act):
            for n in range(N):
                k = n % kb
                act.wait_ge(loaded[n % 2], 16 * (n // 2 + 1))
                if n >= 2:
                    act.wait_ge(used, n - 1)
                if whole:
                    nc.scalar.activation(x_high[:, n % 2, :], lhsT[:, k, :], ACT.Copy)
                nc.scalar.activation(high[:, n % 2, :], raw[:, n % 2, :], ACT.Copy).then_inc(rounded, 1)

        @block.vector
        def _(dve):
            def split_step(n):
                dve.wait_ge(rounded, n + 1)
                if whole:
                    nc.vector.tensor_tensor(x_low[:, n % 2, :], lhsT[:, n % kb, :], x_high[:, n % 2, :].bitcast(F32), ALU.subtract)
                nc.vector.tensor_tensor(low[:, n % 2, :], raw[:, n % 2, :], high[:, n % 2, :].bitcast(F32), ALU.subtract)\
                    .then_inc(split, 1)
            done = 0
            for h in range(n_half):
                while done < min(N, (h + 1) * kb + 1):
                    split_step(done)
                    done += 1
                if source is not None:
                    dve.wait_ge(xin[h], 16)
                for b in range(NT):
                    dve.wait_ge(product, h * NT + b + 1)
                    xs = dst[:, b, h * HALF:(h + 1) * HALF]
                    if source is None:
                        nc.vector.tensor_copy(xs, core.ps[:, b, :]).then_inc(added, 1)
                    else:
                        nc.vector.tensor_tensor(xs, xs, core.ps[:, b, :], ALU.add).then_inc(added, 1)
    st.end()


def norm_rows(core, name, x, gain_row, out=None, source=None):
    nc = core.nc
    st = Stage(core, name)
    junk = st.sb("junk", [P, D])
    stat = st.sb("stat", [P, 3, NT])
    gain = st.sb("gain", [P, D])
    x_loaded = [st.sem(f"x_loaded{b}") for b in range(NT)]
    loaded, summed, mean, root, inverse, normed, written = (
        st.sem(n) for n in ("loaded", "summed", "mean", "root", "inverse", "normed", "written"))
    with nc.Block(name) as block:
        @block.sync
        def _(sp):
            if source is not None:
                for b in range(NT):
                    sp.dma_start(x[:, b, :], source[b * P:(b + 1) * P, :]).then_inc(x_loaded[b], 16)
            sp.dma_start(gain[:, :], gain_row.to_broadcast([P, D])).then_inc(loaded, 16)
            if out is not None:
                for b in range(NT):
                    sp.wait_ge(normed, b + 1)
                    sp.dma_start(out[b * P:(b + 1) * P, :], x[:, b, :]).then_inc(written, 16)
                sp.wait_ge(written, 16 * NT)

        @block.scalar
        def _(act):
            for b in range(NT):
                if source is not None:
                    act.wait_ge(x_loaded[b], 16)
                if b:
                    act.wait_ge(summed, b)
                nc.scalar.activation(junk[:, :], x[:, b, :], ACT.Square,
                                     accum_out=stat[:, 0, b:b + 1]).then_inc(summed, 1)
            act.wait_ge(mean, 1)
            nc.scalar.activation(stat[:, 2, :], stat[:, 1, :], ACT.Sqrt).then_inc(root, 1)

        @block.vector
        def _(dve):
            dve.wait_ge(summed, NT)
            nc.vector.tensor_scalar(stat[:, 1, :], stat[:, 0, :], 1.0 / D, 1e-6, ALU.mult, ALU.add).then_inc(mean, 1)
            dve.wait_ge(root, 1)
            nc.vector.reciprocal(stat[:, 0, :], stat[:, 2, :]).then_inc(inverse, 1)
            dve.wait_ge(inverse, 1)
            dve.wait_ge(loaded, 16)
            for b in range(NT):
                nc.vector.scalar_tensor_tensor(x[:, b, :], x[:, b, :], stat[:, 0, b:b + 1], gain[:, :],
                                               ALU.mult, ALU.mult).then_inc(normed, 1)
    st.end()


def rope_tables(core, table):
    nc = core.nc
    st = Stage(core, "rope")
    pos_i = st.sb("pos_i", [P, T], I32)
    ang = st.sb("ang", [P, T])
    turns = st.sb("turns", [P, T])
    loaded, d_link, reduced, sines = (st.sem(x) for x in ("loaded", "d_link", "reduced", "sines"))
    c1, c2 = 6.28125, 4059.0 / 2 ** 21
    c3 = 2 * math.pi - c1 - c2
    magic = 12582912.0
    with nc.Block("rope") as block:
        @block.sync
        def _(sp):
            sp.dma_start(pos_i[:, :], core.dram["positions"].to_broadcast([P, T])).then_inc(loaded, 16)

        @block.vector
        def _(dve):
            link = Links(dve, d_link)
            ts = nc.vector.tensor_scalar
            dve.wait_ge(loaded, 16)
            link(nc.vector.tensor_copy(ang[:, :], pos_i[:, :]))
            link(ts(ang[:, :], ang[:, :], core.v("inv", 0), None, ALU.mult))
            link(ts(turns[0:64, :], ang[0:64, :], 1 / (2 * math.pi), 0.25, ALU.mult, ALU.add))
            link(ts(turns[64:P, :], ang[64:P, :], 1 / (2 * math.pi), None, ALU.mult))
            link(ts(turns[:, :], turns[:, :], magic, None, ALU.add))
            link(ts(turns[:, :], turns[:, :], magic, None, ALU.subtract))
            for c in (c1, c2, c3):
                link(nc.vector.scalar_tensor_tensor(ang[:, :], turns[:, :], -c, ang[:, :], ALU.mult, ALU.add))
            link(ts(ang[0:64, :], ang[0:64, :], math.pi / 2, None, ALU.add))
            ts(ang[:, :], ang[:, :], 3.1415925, -3.1415925, ALU.min, ALU.max).then_inc(reduced, 1)
            dve.wait_ge(sines, 1)
            ts(table[64:96, :], table[64:96, :], -1.0, None, ALU.mult)

        @block.scalar
        def _(act):
            act.wait_ge(reduced, 1)
            nc.scalar.activation(table[:, :], ang[:, :], ACT.Sin).then_inc(sines, 1)
    st.end()


def rotate(core, name, blocks, table, dst):
    nc = core.nc
    st = Stage(core, name)
    scaled, product, free = st.sem("scaled"), st.sem("product"), st.sem("free")
    with nc.Block(name) as block:
        @block.vector
        def _(dve):
            for n, x in enumerate(blocks):
                nc.vector.tensor_tensor(x, x, table[:, :], ALU.mult).then_inc(scaled, 1)

        @block.tensor
        def _(pe):
            for n, x in enumerate(blocks):
                pe.wait_ge(scaled, n + 1)
                if n >= 4:
                    pe.wait_ge(free, n - 3)
                for h in range(2):
                    last = nc.tensor.matmul(core.ps[0:64, 2 * (n % 4) + h, :], core.c("fold"), x[:, h * HALF:(h + 1) * HALF],
                                            start=True, stop=True)
                last.then_inc(product, 1)

        @block.scalar
        def _(act):
            for n, x in enumerate(blocks):
                act.wait_ge(product, n + 1)
                nc.scalar.activation(dst[0:64, n, :], core.ps[0:64, 2 * (n % 4):2 * (n % 4) + 2, :].rearrange("p a n -> p (a n)"),
                                     ACT.Copy).then_inc(free, 1)
    st.end()


def gates_of_layer(core, name, l, qk, z):
    nc = core.nc
    st = Stage(core, name)
    low = st.sb("low", [P, 8, 4])
    small = st.sb("small", [P, 4, T])
    wide = lambda x: x.rearrange("p a n -> p (a n)")
    shifted, exps, sig, ready, logs, d_link = (st.sem(x) for x in ("shifted", "exps", "sigmoids", "ready", "logs", "d_link"))
    tiny = 2.0 ** -60
    with nc.Block(name) as block:
        @block.scalar
        def _(act):
            act.wait_ge(shifted, 2)
            nc.scalar.activation(low[:, 2:4, :], low[:, 0:2, :], ACT.Exp).then_inc(exps, 1)
            nc.scalar.activation(wide(qk[:, 1]), wide(z), ACT.Sigmoid, scale=-1.0).then_inc(sig, 1)
            act.wait_ge(sig, 1)
            nc.scalar.activation(wide(z), wide(z), ACT.Sigmoid).then_inc(sig, 1)
            act.wait_ge(ready, 2)
            nc.scalar.activation(wide(z), wide(z), ACT.Ln).then_inc(logs, 1)
            nc.scalar.activation(wide(small[:, :, :]), wide(small[:, :, :]), ACT.Ln).then_inc(logs, 1)

        @block.vector
        def _(dve):
            link = Links(dve, d_link)
            tt, ts = nc.vector.tensor_tensor, nc.vector.tensor_scalar
            link(tt(low[:, 4, :], core.vs("lb0"), core.vs("lb1"), ALU.max))
            tt(low[:, 0, :], core.vs("lb0"), low[:, 4, :], ALU.subtract).then_inc(shifted, 1)
            tt(low[:, 1, :], core.vs("lb1"), low[:, 4, :], ALU.subtract).then_inc(shifted, 1)
            dve.wait_ge(exps, 1)
            link(tt(low[:, 4, :], low[:, 2, :], low[:, 3, :], ALU.add))
            link(nc.vector.reciprocal(low[:, 5, :], low[:, 4, :]))
            link(tt(low[:, 2, :], low[:, 2, :], low[:, 5, :], ALU.mult))
            link(tt(low[:, 3, :], low[:, 3, :], low[:, 5, :], ALU.mult))
            if l == 1:
                link(tt(low[:, 6, :], low[:, 2, :], low[:, 3, :], ALU.add))
                link(tt(low[:, 6, :], low[:, 6, :], low[:, 2, :], ALU.subtract))
            else:
                link(tt(low[:, 6, :], low[:, 2, :], low[:, 2, :], ALU.subtract))
            link(ts(low[:, 7, :], low[:, 6, :], -1.0, 1.0, ALU.mult, ALU.add))
            dve.wait_ge(sig, 2)
            for j in range(4):
                ts(qk[:, 1, j, :], qk[:, 1, j, :], low[:, 7, j:j + 1], None, ALU.mult)
                last = ts(z[:, j, :], z[:, j, :], low[:, 7, j:j + 1], low[:, 6, j:j + 1], ALU.mult, ALU.add)
            link(last)
            link(ts(wide(z), wide(z), 1e-30, None, ALU.max))
            ts(wide(small[:, :, :]), wide(z), tiny, 1 / tiny, ALU.min, ALU.mult).then_inc(ready, 1)
            dve.wait_ge(ready, 1)
            ts(wide(z), wide(z), tiny, None, ALU.max).then_inc(ready, 1)
            dve.wait_ge(logs, 2)
            tt(wide(z), wide(z), wide(small[:, :, :]), ALU.add)
    st.end()


def gated_chunks(core, name, qk, log_decays, inputs, oT):
    nc = core.nc
    st = Stage(core, name)
    H = 4
    decays = st.sb("decays", [64, 2, HALF])
    value = st.sb("value", [P, 2, HALF])
    span = st.sb("span", [P, 2, H, 8, CH])
    qs = st.sb("qs", [P, 2, H, 8, CH])
    ks = st.sb("ks", [P, 2, H, 8, CH])
    prod = st.sb("prod", [P, 2, 7, CH])
    attn = st.sb("attn", [P, 2, CH])
    kt = st.sb("kt", [P, 2, P])
    state = st.sb("state", [P, H, P])
    names = ("decays_in", "value_in", "state_new", "summed", "span_exp", "q_ready", "k_ready", "raw", "k_end", "products", "masked",
             "attn_ready", "turned", "k_rows", "o_ready", "o_stored")
    s = {x: st.sem(x) for x in names}
    ps = core.ps
    half = lambda h: slice(64 * (h // 2), 64 * (h // 2) + 64)
    o_psum = ps[:, 6, 256:512].rearrange("p (h n) -> p h n", h=H)

    def skewed(eng, ahead, behind):
        def step(n, u, i):
            ahead(n, u, i)
            behind(n - 1, 1 - u, i - (1 - u))
        ahead(0, 0, 0)
        step(1, 1, 0)
        pairs(eng, NCH, step, first=2)
        behind(NCH - 1, 1, NCH // 2 - 1)

    with nc.Block(name) as block:
        @block.gpsimd
        def _(pool):
            nc.gpsimd.memset(state[:, :, :], 0.0).then_inc(s["state_new"], H)
            pool.wait_ge(s["state_new"], H)
            nc.gpsimd.memset(value[:, :, :], 0.0).then_inc(s["value_in"], 1)
            pool.wait_ge(s["value_in"], 1)

            def ahead(n, u, i):
                if not isinstance(n, int) or n >= 2:
                    pool.wait_ge(s["summed"], n - 1)
                    core.settle(pool)
                rows = slice(64 * u, 64 * u + 64)
                nc.gpsimd.tensor_copy(decays[:, u, :], log_decays[rows, bass.ds(i, 1), :].rearrange("p b n -> p (b n)"))\
                    .then_inc(s["decays_in"], 1)
                pool.wait_ge(s["decays_in"], n + 1)
                core.settle(pool)

            def behind(n, u, i):
                pool.wait_ge(s["span_exp"], n + 1)
                if not isinstance(n, int) or n >= 1:
                    pool.wait_ge(s["o_ready"], n)
                core.settle(pool)
                nc.gpsimd.tensor_tensor(ks[:, u, :, 7, :], span[:, u, :, 7, :], qk[:, 1, :, bass.ds(n * CH, CH)], ALU.mult)\
                    .then_inc(s["k_end"], 1)
                pool.wait_ge(s["k_end"], n + 1)
                core.settle(pool)
                rows = slice(64 * u, 64 * u + 64)
                for m in range(2):
                    c = slice(256 * m, 256 * m + 256)
                    nc.gpsimd.tensor_copy(value[64 * m:64 * m + 64, u, c], inputs[rows, bass.ds(i, 1), c].rearrange("p b n -> p (b n)"))\
                        .then_inc(s["value_in"], 1)
                    pool.wait_ge(s["value_in"], 2 * n + m + 2)
                    core.settle(pool)
            skewed(pool, ahead, behind)

        @block.tensor
        def _(pe):
            mm = nc.tensor.matmul
            pe.sem_inc(s["o_ready"], 1)

            def ahead(n, u, i):
                pe.wait_ge(s["decays_in"], n + 1)
                if not isinstance(n, int) or n >= 1:
                    pe.wait_ge(s["span_exp"], n)
                core.settle(pe)
                for h in range(H):
                    last = mm(ps[:, h, :], decays[:, u, h * P:(h + 1) * P], core.c("spans", 0, 64), start=True, stop=True)
                last.then_inc(s["summed"], 1)

            def behind(n, u, i):
                pe.wait_ge(s["q_ready"], n + 1)
                pe.wait_ge(s["k_ready"], n + 1)
                pe.wait_ge(s["raw"], 2 * (n + 1))
                core.settle(pe)
                for h in range(H):
                    for l in range(7):
                        last = mm(ps[half(h), 4 + h % 2, l * CH:(l + 1) * CH], ks[:, u, h, l, :], qs[:, u, h, l if l < 6 else 7, :],
                                  start=True, stop=True)
                last.then_inc(s["products"], 1)
                pe.wait_ge(s["k_end"], n + 1)
                if not isinstance(n, int) or n >= 1:
                    pe.wait_ge(s["o_stored"], n)
                core.settle(pe)
                for h in range(H):
                    last = mm(ps[half(h), 6, (h % 2) * P:(h % 2 + 1) * P], ks[:, u, h, 7, :], core.c("eye"), start=True, stop=True)
                last.then_inc(s["turned"], 1)
                pe.wait_ge(s["k_rows"], n + 1)
                pe.wait_ge(s["value_in"], 2 * (n + 1) + 1)
                pe.wait_ge(s["state_new"], (n + 1) * H)
                core.settle(pe)
                for h in range(H):
                    mm(ps[:, 7, h * P:(h + 1) * P], kt[:, h % 2, :], value[:, u, h * P:(h + 1) * P], start=True, stop=True)
                pe.wait_ge(s["attn_ready"], n + 1)
                core.settle(pe)
                for h in range(H):
                    mm(o_psum[:, h, :], state[:, h, :], qs[:, u, h, 6, :], start=True, stop=False)
                    last = mm(o_psum[:, h, :], value[:, u, h * P:(h + 1) * P], attn[:, h % 2, :], start=False, stop=True)
                last.then_inc(s["o_ready"], 1)
            skewed(pe, ahead, behind)

        @block.scalar
        def _(act):
            def ahead(n, u, i):
                cols = bass.ds(n * CH, CH)
                if not isinstance(n, int) or n >= 2:
                    act.wait_ge(s["o_ready"], n)
                    act.wait_ge(s["state_new"], n * H)
                    act.wait_ge(s["k_end"], n - 1)
                nc.scalar.activation(ks[:, u, :, 6, :], qk[:, 1, :, cols], ACT.Copy).then_inc(s["raw"], 1)
                nc.scalar.activation(qs[:, u, :, 7, :], qk[:, 0, :, cols], ACT.Copy).then_inc(s["raw"], 1)
                act.wait_ge(s["summed"], n + 1)
                nc.scalar.activation(span[:, u, :, :, :].rearrange("p h l n -> p (h l n)"),
                                     ps[:, 0:4, :].rearrange("p a n -> p (a n)"), ACT.Exp).then_inc(s["span_exp"], 1)

            def behind(n, u, i):
                act.wait_ge(s["turned"], n + 1)
                act.wait_ge(s["o_ready"], n + 1)
                nc.scalar.activation(kt[:, :, :], ps[:, 6, 0:256].rearrange("p (h n) -> p h n", h=2), ACT.Copy).then_inc(s["k_rows"], 1)
                act.wait_ge(s["o_ready"], n + 2)
                nc.scalar.activation(oT[:, :, bass.ds(n * CH, CH)], o_psum, ACT.Copy).then_inc(s["o_stored"], 1)
            skewed(act, ahead, behind)

        @block.vector
        def _(dve):
            def scores(n, u, i):
                dve.wait_ge(s["products"], n + 1)
                if not isinstance(n, int) or n >= 1:
                    dve.wait_ge(s["attn_ready"], n)
                nc.vector.tensor_tensor(prod[:, :, :, :], ps[:, 4:6, :].rearrange("p h (l n) -> p h l n", l=8)[:, :, 0:7],
                                        core.c("decaylevel").rearrange("p (l n) -> p l n", l=7).unsqueeze(1)
                                        .to_broadcast([P, 2, 7, CH]), ALU.mult).then_inc(s["masked"], 1)
                dve.wait_ge(s["masked"], n + 1)
                dve.wait_ge(s["o_ready"], n + 1)
                nc.vector.tensor_reduce(attn[:, :, :], prod[:, :, :, :].rearrange("p h l n -> p h n l"), AX, ALU.add)\
                    .then_inc(s["attn_ready"], 1)

            def factors(n, u, i):
                cols = bass.ds(n * CH, CH)
                dve.wait_ge(s["span_exp"], n + 1)
                if not isinstance(n, int) or n >= 2:
                    dve.wait_ge(s["o_ready"], n)
                for h in range(H):
                    q = qk[:, 0, h:h + 1, cols].to_broadcast([P, 7, CH])
                    last = nc.vector.tensor_tensor(qs[:, u, h, 0:7, :], span[:, u, h, 0:7, :], q, ALU.mult)
                last.then_inc(s["q_ready"], 1)
                for h in range(H):
                    k = qk[:, 1, h:h + 1, cols].to_broadcast([P, 6, CH])
                    last = nc.vector.tensor_tensor(ks[:, u, h, 0:6, :], span[:, u, h, 0:6, :], k, ALU.mult)
                last.then_inc(s["k_ready"], 1)

            def advance(n, u, i):
                dve.wait_ge(s["o_ready"], n + 2)
                for h in range(H):
                    nc.vector.scalar_tensor_tensor(state[:, h, :], state[:, h, :], span[:, u, h, 6, CH - 1:CH],
                                                   ps[:, 7, h * P:(h + 1) * P], ALU.mult, ALU.add).then_inc(s["state_new"], 1)

            def step(n, u, i):
                scores(n - 1, 1 - u, i - (1 - u))
                factors(n, u, i)
                advance(n - 1, 1 - u, i - (1 - u))
            factors(0, 0, 0)
            step(1, 1, 0)
            pairs(dve, NCH, step, first=2)
            scores(NCH - 1, 1, NCH // 2 - 1)
            advance(NCH - 1, 1, NCH // 2 - 1)
    st.end()


def head_norm_gate(core, name, oT, gain, dst):
    nc = core.nc
    st = Stage(core, name)
    sq = st.sb("sq", [P, 4, T])
    two = lambda j: core.ps[:, 2 * j:2 * j + 2, :].rearrange("p b n -> p (b n)")
    squared, sums, gated, meansq, rooted, inverse = (st.sem(x) for x in ("squared", "sums", "gated", "meansq", "rooted", "inverse"))
    with nc.Block(name) as block:
        @block.scalar
        def _(act):
            for j in range(4):
                nc.scalar.activation(sq[:, j, :], oT[:, j, :], ACT.Square).then_inc(squared, 1)
            for j in range(4):
                act.wait_ge(meansq, j + 1)
                nc.scalar.activation(sq[:, j, :], sq[:, j, :], ACT.Sqrt).then_inc(rooted, 1)

        @block.tensor
        def _(pe):
            for j in range(4):
                pe.wait_ge(squared, j + 1)
                for h in range(2):
                    last = nc.tensor.matmul(core.ps[:, 2 * j + h, :], core.c("ones"), sq[:, j, h * HALF:(h + 1) * HALF],
                                            start=True, stop=True)
                last.then_inc(sums, 1)

        @block.vector
        def _(dve):
            for j in range(4):
                nc.vector.tensor_tensor(dst[:, j, :], dst[:, j, :], oT[:, j, :], ALU.mult).then_inc(gated, 1)
                dve.wait_ge(sums, j + 1)
                nc.vector.tensor_scalar(sq[:, j, :], two(j), 1.0 / P, 1e-6, ALU.mult, ALU.add).then_inc(meansq, 1)

            def invert(j):
                dve.wait_ge(rooted, j + 1)
                nc.vector.reciprocal(sq[:, j, :], sq[:, j, :]).then_inc(inverse, 1)
            invert(0)
            for j in range(4):
                if j < 3:
                    invert(j + 1)
                dve.wait_ge(gated, j + 1)
                dve.wait_ge(inverse, j + 1)
                nc.vector.scalar_tensor_tensor(dst[:, j, :], dst[:, j, :], gain, sq[:, j, :], ALU.mult, ALU.mult)
    st.end()


def route(core, xT, gates, slots, experts, tiles):
    nc, d = core.nc, core.dram
    st = Stage(core, "route")
    rw = st.sb("rw", [P, KD, NEXP])
    logits = st.sb("logits", [P, NT, NEXP])
    top = st.sb("top", [P, NT, 8])
    which = st.sb("which", [P, NT, 8], U32)
    whichf = st.sb("whichf", [P, NT, 8])
    hot = st.sb("hot", [P, 2, NT, NEXP])
    both = st.sb("both", [P, NT, NEXP])
    g = st.sb("g", [P, 4, NT])
    rank = st.sb("rank", [P, NT, NEXP])
    ex = st.sb("ex", [P, 6, NEXP])
    over = st.sb("over", [P, NPASS + 1, NEXP])
    left = st.sb("left", [P, NPASS + 1, NEXP])
    ef = st.sb("ef", [P, NPASS + 1])
    first = st.sb("first", [P, NPASS + 1])
    slotf = st.sb("slotf", [P, 2, NT])
    token = st.sb("token", [P, NT], U32)
    zero = st.sb("zero", [P, (NPASS + 1) * SLOTS // P], U32)
    loaded, product, d_link, e_done, counted, ready, cleared, scattered, ranked, diffed = (
        st.sem(x) for x in ("loaded", "product", "d_link", "exp", "counted", "ready", "cleared", "scattered", "ranked", "diffed"))
    with nc.Block("route") as block:
        @block.sync
        def _(sp):
            sp.dma_start(rw[:, :, :], d["router"]).then_inc(loaded, 16)

        @block.tensor
        def _(pe):
            pe.wait_ge(loaded, 16)
            for b in range(NT):
                for k in range(KD):
                    last = nc.tensor.matmul(core.ps[:, 0, b * 8:b * 8 + 8], xT[:, k, b * P:(b + 1) * P], rw[:, k, :],
                                            start=(k == 0), stop=(k == KD - 1))
            last.then_inc(product, 1)
            pe.wait_ge(counted, 1)
            for b in range(NT):
                for e in range(b):
                    nc.tensor.matmul(core.ps[:, 1, b * 8:b * 8 + 8], core.c("ones"), both[:, e, :], start=(e == 0), stop=False)
                nc.tensor.matmul(core.ps[:, 1, b * 8:b * 8 + 8], core.c("earlier"), both[:, b, :], start=(b == 0), stop=True)
            for b in range(NT):
                last = nc.tensor.matmul(core.ps[:, 2, 0:8], core.c("ones"), both[:, b, :], start=(b == 0), stop=(b == NT - 1))
            last.then_inc(ranked, 1)

        @block.scalar
        def _(act):
            act.wait_ge(diffed, 1)
            nc.scalar.activation(g[:, 1, :], g[:, 0, :], ACT.Exp).then_inc(e_done, 1)

        @block.vector
        def _(dve):
            link = Links(dve, d_link)
            tt, ts = nc.vector.tensor_tensor, nc.vector.tensor_scalar
            dve.wait_ge(product, 1)
            link(nc.vector.tensor_copy(logits[:, :, :].rearrange("p a n -> p (a n)"), core.ps[:, 0, 0:64]))
            for b in range(NT):
                link(nc.vector.max(top[:, b, :], logits[:, b, :]))
                link(nc.vector.max_index(which[:, b, :], top[:, b, :], logits[:, b, :]))
            link(nc.vector.tensor_copy(whichf[:, :, :], which[:, :, :]))
            for k in range(2):
                link(tt(hot[:, k, :, :], core.c("iota8").unsqueeze(1).to_broadcast([P, NT, NEXP]),
                        whichf[:, :, k:k + 1].to_broadcast([P, NT, NEXP]), ALU.is_equal))
            tt(both[:, :, :], hot[:, 0, :, :], hot[:, 1, :, :], ALU.add).then_inc(counted, 1)
            tt(g[:, 0, :], top[:, :, 1], top[:, :, 0], ALU.subtract).then_inc(diffed, 1)
            dve.wait_ge(e_done, 1)
            link(ts(g[:, 2, :], g[:, 1, :], 1.0, None, ALU.add))
            link(nc.vector.reciprocal(gates[:, 0, :], g[:, 2, :]))
            link(tt(gates[:, 1, :], gates[:, 0, :], g[:, 1, :], ALU.mult))
            dve.wait_ge(ranked, 1)
            link(nc.vector.tensor_copy(ex[:, 0, :], core.ps[:, 2, 0:8]))
            link(ts(ex[:, 1, :], ex[:, 0, :], 0.0, None, ALU.is_gt))
            for j in range(1, T // SLOTS):
                link(ts(ex[:, 2, :], ex[:, 0, :], float(j * SLOTS), None, ALU.is_gt))
                link(tt(ex[:, 1, :], ex[:, 1, :], ex[:, 2, :], ALU.add))
            link(nc.vector.tensor_tensor_scan(ex[:, 3, :], core.c("ones")[:, 0:NEXP], ex[:, 1, :], 0.0, ALU.mult, ALU.add))
            link(tt(ex[:, 4, :], ex[:, 3, :], ex[:, 1, :], ALU.subtract))
            link(ts(ex[:, 4, :], ex[:, 4, :], float(SLOTS), None, ALU.mult))
            link(tt(rank[:, :, :], core.ps[:, 1, 0:64].rearrange("p (b e) -> p b e", b=NT),
                    ex[:, 4, :].unsqueeze(1).to_broadcast([P, NT, NEXP]), ALU.add))
            for k in range(2):
                link(tt(hot[:, k, :, :], hot[:, k, :, :], rank[:, :, :], ALU.mult))
                link(nc.vector.tensor_reduce(slotf[:, k, :], hot[:, k, :, :], AX, ALU.add))
            link(nc.vector.tensor_copy(slots[:, :, :], slotf[:, :, :]))
            each = [P, NPASS + 1, NEXP]
            by_pass, by_expert = (lambda x: x.unsqueeze(2).to_broadcast(each)), (lambda x: x.unsqueeze(1).to_broadcast(each))
            link(tt(over[:, :, :], by_expert(ex[:, 3, :]), by_pass(core.c("pass")), ALU.is_le))
            link(nc.vector.tensor_reduce(ef[:, :], over[:, :, :], AX, ALU.add))
            link(ts(ef[:, :], ef[:, :], float(NEXP - 1), None, ALU.min))
            link(nc.vector.tensor_copy(experts[:, :], ef[:, :]))
            link(ts(first[:, :], core.c("pass"), float(SLOTS), None, ALU.mult))
            link(tt(left[:, :, :], by_expert(ex[:, 4, :]), by_pass(first[:, :]), ALU.is_le))
            link(tt(over[:, :, :], left[:, :, :], over[:, :, :], ALU.subtract))
            link(tt(ex[:, 5, :], ex[:, 4, :], ex[:, 0, :], ALU.add))
            link(tt(left[:, :, :], by_expert(ex[:, 5, :]), by_pass(first[:, :]), ALU.subtract))
            link(tt(left[:, :, :], left[:, :, :], over[:, :, :], ALU.mult))
            link(nc.vector.tensor_reduce(ef[:, :], left[:, :, :], AX, ALU.add))
            link(ts(first[:, :], ef[:, :], float(P), None, ALU.is_gt))
            link(ts(ef[:, :], ef[:, :], 0.0, None, ALU.is_gt))
            link(tt(ef[:, :], ef[:, :], first[:, :], ALU.add))
            link(nc.vector.tensor_copy(tiles[:, :], ef[:, :]))
            nc.vector.tensor_copy(token[:, :], core.c("tok")).then_inc(ready, 1)

        @block.gpsimd
        def _(pool):
            nc.gpsimd.memset(zero[:, :], 0).then_inc(cleared, 1)
            pool.wait_ge(cleared, 1)
            nc.gpsimd.dma_start(d["slot_token"].rearrange("(p n) one -> p (n one)", p=P), zero[:, :]).then_inc(scattered, 16)
            pool.wait_ge(scattered, 16)
            pool.wait_ge(ready, 1)
            for k in range(2):
                for b in range(NT):
                    nc.gpsimd.indirect_dma_start(
                        d["slot_token"], bass.IndirectOffsetOnAxis(ap=slots[:, k, b:b + 1], axis=0),
                        token[:, b:b + 1], None).then_inc(scattered, 16)
            pool.wait_ge(scattered, 16 * (2 * NT + 1))
    st.end()


def swiglu_passes(core, name, NC, weights, out, experts=None, tiles=None, residual=None):
    nc, d = core.nc, core.dram
    st = Stage(core, name)
    NB, AHEAD = 4, 2
    routed = experts is not None
    n_pass = NPASS if routed else T // SLOTS
    assert NC % NB == 0 or (2 * NC % NB == 0 and not routed)
    raw = st.sb("raw", [P, NB, 3, D])
    high = st.sb("high", [P, NB, 3, D], F32R)
    low = st.sb("low", [P, NB, 3, D], F32R)
    index = st.sb("index", [P, 2], U32)
    xs = st.sb("xs", [P, 2, D])
    xs_parts = st.sb("xs_parts", [P, KD, 2, SLOTS], F32R)
    xs_high, xs_low = xs_parts[:, :, 0, :], xs_parts[:, :, 1, :]
    total = st.sb("total", [P, 2, 2, P])
    silu = st.sb("silu", [P, 2, SLOTS])
    hid = st.sb("hid", [P, 2, SLOTS])
    hid_high = st.sb("hid_high", [P, 2, SLOTS], F32R)
    hid_low = st.sb("hid_low", [P, 2, SLOTS], F32R)
    y = st.sb("y", [P, 2, D])
    loaded = [st.sem(f"loaded{i}") for i in range(NB)]
    (summed, y_loaded, indexed, gathered, turned, x_high, x_low, rounded, split, product, silu_done, hid_made, hid_rounded, hid_split, down,
     y_copied_a, y_copied_v, written) = (
        st.sem(x) for x in ("summed", "y_loaded", "indexed", "gathered", "turned", "x_high", "x_low", "rounded", "split", "product", "silu", "hid_made",
                            "hid_rounded", "hid_split", "down", "y_scalar", "y_vector", "written"))
    ps = core.ps
    SPLIT0 = 3 * NB
    bank = lambda u, m, width: ps[:, u % 2, m * SLOTS:m * SLOTS + width]
    rows_psum = ps[:, 2:4, :].rearrange("p b (k n) -> p (b k) n", k=4)

    def chunks(eng, body, shift):
        G = NC // NB
        for f in range(NB):
            body(f, (f + shift) % NB)
        with eng.Fori(1, G - 1, 1) as g:
            for u in range(NB):
                body(g * NB + u, (u + shift) % NB)
        for f in range((G - 1) * NB, NC):
            body(f, (f + shift) % NB)

    def passes(eng, body, otherwise=None):
        if not routed:
            with eng.Fori(0, n_pass // 2, 1) as i:
                for v in range(2):
                    body(2 * i + v, SLOTS, v * NC % NB)
            return
        with eng.Fori(0, n_pass, 1) as j:
            n = eng.value_load(tiles[0:1, bass.ds(j, 1)], min_val=0, max_val=2)
            with eng.If(n > 1):
                body(j, SLOTS, 0)
            with eng.If(n == 1):
                body(j, P, 0)
            if otherwise is not None:
                with eng.If(n == 0):
                    otherwise(j)

    with nc.Block(name) as block:
        @block.sync
        def _(sp):
            def fetch(e, f, v):
                row = f if e is None else e * NC + f
                src = weights[row] if isinstance(row, int) else weights[bass.ds(row, 1)].rearrange("a p n -> p (a n)")
                sp.dma_start(raw[:, v, :, :].rearrange("p a n -> p (a n)"), src).then_inc(loaded[v], 16)

            def one_pass(j, shift, e, e_next):
                def one(f, u):
                    sp.wait_ge(split, 3 * (j * NC + f - 1) + SPLIT0)
                    over = isinstance(f, int) and f + AHEAD >= NC
                    fetch(e_next if over else e, f + AHEAD - NC if over else f + AHEAD, (u + AHEAD) % NB)
                chunks(sp, one, shift)

            if not routed:
                for f in range(AHEAD):
                    fetch(None, f, f)
                with sp.Fori(0, n_pass // 2, 1) as i:
                    for v in range(2):
                        one_pass(2 * i + v, v * NC % NB, None, None)
            else:
                first = sp.value_load(experts[0:1, 0:1], min_val=0, max_val=NEXP - 1)
                for f in range(AHEAD):
                    fetch(first, f, f)
                with sp.Fori(0, n_pass, 1) as j:
                    n = sp.value_load(tiles[0:1, bass.ds(j, 1)], min_val=0, max_val=2)
                    with sp.If(n > 0):
                        e = sp.value_load(experts[0:1, bass.ds(j, 1)], min_val=0, max_val=NEXP - 1)
                        e_next = sp.value_load(experts[0:1, bass.ds(j + 1, 1)], min_val=0, max_val=NEXP - 1)
                        one_pass(j, 0, e, e_next)

        @block.gpsimd
        def _(pool):
            def gather(j):
                for a in range(2):
                    src = d["slot_token"][j * SLOTS + a * P:j * SLOTS + (a + 1) * P, :] if isinstance(j, int) \
                        else d["slot_token"][bass.ds(j * SLOTS + a * P, P), :]
                    nc.gpsimd.dma_start(index[:, a:a + 1], src).then_inc(indexed, 16)
                pool.wait_ge(indexed, 32 * (j + 1))
                core.settle(pool)
                for a in range(2):
                    nc.gpsimd.indirect_dma_start(xs[:, a, :], None, d["h_rows"],
                                                 bass.IndirectOffsetOnAxis(ap=index[:, a:a + 1], axis=0)).then_inc(gathered, 16)
                pool.wait_ge(gathered, 32 * (j + 1))

            def fetch_rows(j):
                rows = slice((j % n_pass) * SLOTS, (j % n_pass + 1) * SLOTS)
                pool.dma_start(xs[:, :, :], d["h_rows"][rows, :].rearrange("(a p) n -> p a n", p=P)).then_inc(gathered, 32)
            if not routed:
                fetch_rows(0)
                for j in range(n_pass):
                    pool.wait_ge(turned, 2 * (j + 1))
                    fetch_rows(j + 1)
                    pool.wait_ge(written, 16 * (j + 1))
                    pool.dma_start(y[:, :, :], residual[j * SLOTS:(j + 1) * SLOTS, :].rearrange("(a p) n -> p a n", p=P)).then_inc(y_loaded, 16)
                return
            gather(0)
            with pool.Fori(0, n_pass, 1) as j:
                n = pool.value_load(tiles[0:1, bass.ds(j, 1)], min_val=0, max_val=2)
                with pool.If(n > 0):
                    pool.wait_ge(turned, 2 * (j + 1))
                    gather(j + 1)

        @block.tensor
        def _(pe):
            pe.sem_inc(down, 2)

            def turn(a):
                for k in range(KD):
                    last = nc.tensor.transpose(rows_psum[:, k, :], xs[:, a, k * P:(k + 1) * P], core.c("eye"))
                last.then_inc(turned, 1)
            pe.wait_ge(gathered, 32)
            turn(0)
            pe.wait_ge(x_low, 1)
            turn(1)

            def one_pass(j, width, shift):
                pe.wait_ge(x_low, 2 * (j + 1))
                core.settle(pe)

                def down_part(f, v, first, last_one):
                    pe.wait_ge(hid_split, j * NC + f + 1)
                    core.settle(pe)
                    for a in range(width // P):
                        for h in range(2):
                            for i, (x, w) in enumerate(((hid_high, high), (hid_high, low), (hid_low, high))):
                                last = nc.tensor.matmul(ps[:, 4 + 2 * a + h, :], x[:, v % 2, a * P:(a + 1) * P],
                                                        w[:, v, 2, h * HALF:(h + 1) * HALF],
                                                        start=first and i == 0, stop=last_one and i == 2)
                    last.then_inc(down, 1)

                def one(f, u):
                    pe.wait_ge(split, 3 * (j * NC + f + 1) + SPLIT0)
                    pe.wait_ge(hid_made, j * NC + f + 1)
                    core.settle(pe)
                    for m in range(2):
                        for k in range(KD):
                            c = slice(k * P, (k + 1) * P)
                            if width > P:
                                for i, (w, x) in enumerate(((high, xs_high), (high, xs_low), (low, xs_high))):
                                    last = nc.tensor.matmul(bank(u, m, SLOTS), w[:, u, m, c], x[:, k, :],
                                                            start=(k == 0 and i == 0), stop=(k == KD - 1 and i == 2))
                            else:
                                nc.tensor.matmul(bank(u, m, SLOTS).rearrange("p (a n) -> p a n", a=2), high[:, u, m, c],
                                                 xs_parts[:, k, :, 0:P], start=(k == 0), stop=False)
                                last = nc.tensor.matmul(bank(u, m, P), low[:, u, m, c], xs_high[:, k, 0:P],
                                                        start=False, stop=(k == KD - 1))
                    last.then_inc(product, 1)
                    is_last = isinstance(f, int) and f == NC - 1
                    if is_last:
                        pe.wait_ge(gathered, 32 * (j + 2))
                        core.settle(pe)
                        turn(0)
                    if isinstance(f, int) and f == 1:
                        if routed:
                            pe.wait_ge(y_copied_a, 2 * j + 2)
                        pe.wait_ge(y_copied_v, 2 * j + 2)
                    if not (isinstance(f, int) and f == 0):
                        down_part(f - 1, (u - 1) % NB, isinstance(f, int) and f == 1, False)
                    if is_last:
                        pe.wait_ge(x_low, 2 * (j + 1) + 1)
                        core.settle(pe)
                        turn(1)
                        down_part(f, u, False, True)
                chunks(pe, one, shift)
            passes(pe, one_pass)

        @block.scalar
        def _(act):
            act.sem_inc(y_copied_a, 2)

            def round_chunk(n, v, parts=(0, 1, 2)):
                if 0 in parts:
                    act.wait_ge(loaded[v], n)
                for t in parts:
                    nc.scalar.activation(high[:, v, t, :], raw[:, v, t, :], ACT.Copy).then_inc(rounded, 1)

            def place(a, n):
                act.wait_ge(turned, n)
                nc.scalar.activation(xs_high[:, :, a * P:(a + 1) * P], rows_psum, ACT.Copy).then_inc(x_high, 1)

            def write(j):
                act.dma_start(out[bass.ds(j * SLOTS, SLOTS), :].rearrange("(a p) n -> p a n", p=P), y[:, :, :]).then_inc(written, 16)
            round_chunk(16, 0)
            for a in range(2):
                place(a, a + 1)
            round_chunk(16, 1)

            def one_pass(j, width, shift):
                def one(f, u):
                    v = (u + AHEAD) % NB
                    loads = (j * NC + f + AHEAD - v) * (16 // NB) + 16
                    act.wait_ge(down, j * NC + f + 1)
                    round_chunk(loads, v, (0,))
                    if width > P:
                        act.wait_ge(product, j * NC + f + 1)
                        gate = bank(u, 0, SLOTS)
                    else:
                        act.wait_ge(summed, 2 * (j * NC + f) + 1)
                        gate = total[:, u % 2, 0, :]
                    nc.scalar.activation(silu[:, u % 2, 0:width], gate, ACT.Silu).then_inc(silu_done, 1)
                    if isinstance(f, int) and f == NC - 1:
                        place(0, 2 * (j + 1) + 1)
                    round_chunk(loads, v, (1,))
                    act.wait_ge(hid_made, j * NC + f + 3)
                    nc.scalar.activation(hid_high[:, u % 2, 0:width], hid[:, u % 2, 0:width], ACT.Copy).then_inc(hid_rounded, 1)
                    round_chunk(loads, v, (2,))
                chunks(act, one, shift)
                place(1, 2 * (j + 1) + 2)
                if routed:
                    act.wait_ge(down, (j + 1) * NC + 2)
                    act.wait_ge(written, 16 * (j + 1))
                    for h in range(2 if width > P else 1):
                        nc.scalar.activation(y[:, 0, h * HALF:(h + 1) * HALF], ps[:, 4 + h, :], ACT.Copy)\
                            .then_inc(y_copied_a, 1 if width > P else 2)
                    act.wait_ge(y_copied_a, 2 * (j + 2))
                act.wait_ge(y_copied_v, 2 * (j + 2))
                write(j)
            passes(act, one_pass, lambda j: write(j))
            act.wait_ge(written, 16 * (n_pass + 1))

        @block.vector
        def _(dve):
            if routed:
                nc.vector.memset(y[:, :, :], 0.0).then_inc(y_copied_v, 2)
                dve.wait_ge(y_copied_v, 2)
            else:
                dve.sem_inc(y_copied_v, 2)
            dve.sem_inc(hid_made, 2)
            dve.sem_inc(written, 16)
            dve.sem_inc(split, SPLIT0)

            def place(a, n):
                dve.wait_ge(x_high, n)
                part = slice(a * P, (a + 1) * P)
                nc.vector.tensor_tensor(xs_low[:, :, part], rows_psum, xs_high[:, :, part].bitcast(F32), ALU.subtract).then_inc(x_low, 1)

            def split_chunk(v, n, parts=(0, 1, 2)):
                for t in parts:
                    dve.wait_ge(rounded, 3 * n + t + 1)
                    nc.vector.tensor_tensor(low[:, v, t, :], raw[:, v, t, :], high[:, v, t, :].bitcast(F32), ALU.subtract).then_inc(split, 1)
            split_chunk(0, 0)
            for a in range(2):
                place(a, a + 1)
            split_chunk(1, 1)

            def one_pass(j, width, shift):
                def one(f, u):
                    h = slice(0, width)
                    up = bank(u, 1, SLOTS)
                    ahead = (u + AHEAD) % NB, j * NC + f + AHEAD
                    if width == P:
                        dve.wait_ge(product, j * NC + f + 1)
                        for m in range(2):
                            nc.vector.tensor_reduce(total[:, u % 2, m, :], bank(u, m, SLOTS).rearrange("p (a n) -> p n a", a=2), AX, ALU.add)\
                                .then_inc(summed, 1)
                        dve.wait_ge(summed, 2 * (j * NC + f) + 2)
                        up = total[:, u % 2, 1, :]
                    split_chunk(*ahead, (0,))
                    dve.wait_ge(silu_done, j * NC + f + 1)
                    nc.vector.tensor_tensor(hid[:, u % 2, h], silu[:, u % 2, h], up, ALU.mult).then_inc(hid_made, 1)
                    if isinstance(f, int) and f == NC - 1:
                        place(0, 2 * (j + 1) + 1)
                    split_chunk(*ahead, (1,))
                    dve.wait_ge(hid_rounded, j * NC + f + 1)
                    nc.vector.tensor_tensor(hid_low[:, u % 2, h], hid[:, u % 2, h], hid_high[:, u % 2, h].bitcast(F32),
                                            ALU.subtract).then_inc(hid_split, 1)
                    split_chunk(*ahead, (2,))
                if routed and width > P:
                    dve.sem_inc(summed, 2 * NC)
                chunks(dve, one, shift)
                place(1, 2 * (j + 1) + 2)
                dve.wait_ge(down, (j + 1) * NC + 2)
                if routed:
                    dve.wait_ge(written, 16 * (j + 1))
                else:
                    dve.wait_ge(y_loaded, 16 * (j + 1))
                if not routed:
                    for n in range(4):
                        part = y[:, n // 2, (n % 2) * HALF:(n % 2 + 1) * HALF]
                        last = nc.vector.tensor_tensor(part, part, ps[:, 4 + n, :], ALU.add)
                    last.then_inc(y_copied_v, 2)
                elif width > P:
                    for h in range(2):
                        nc.vector.tensor_copy(y[:, 1, h * HALF:(h + 1) * HALF], ps[:, 6 + h, :]).then_inc(y_copied_v, 1)
                else:
                    nc.vector.tensor_copy(y[:, 0, HALF:D], ps[:, 5, :]).then_inc(y_copied_v, 2)
            passes(dve, one_pass)
    st.end()


def combine(core, x, source, gates, slots):
    nc, d = core.nc, core.dram
    st = Stage(core, "combine")
    rows = st.sb("rows", [P, 4, D])
    loaded = [st.sem(f"loaded{b}") for b in range(NT)]
    gathered = [st.sem(f"gathered{i}") for i in range(4)]
    added = st.sem("added")
    with nc.Block("combine") as block:
        @block.sync
        def _(sp):
            for b in range(NT):
                sp.dma_start(x[:, b, :], source[b * P:(b + 1) * P, :]).then_inc(loaded[b], 16)

        @block.gpsimd
        def _(pool):
            for n in range(2 * NT):
                b, k = divmod(n, 2)
                if n >= 4:
                    pool.wait_ge(added, n - 3)
                nc.gpsimd.indirect_dma_start(rows[:, n % 4, :], None, d["y_slot"],
                                             bass.IndirectOffsetOnAxis(ap=slots[:, k, b:b + 1], axis=0)).then_inc(gathered[n % 4], 16)

        @block.vector
        def _(dve):
            for n in range(2 * NT):
                b, k = divmod(n, 2)
                if k == 0:
                    dve.wait_ge(loaded[b], 16)
                else:
                    dve.wait_ge(added, n)
                dve.wait_ge(gathered[n % 4], 16 * (n // 4 + 1))
                nc.vector.scalar_tensor_tensor(x[:, b, :], rows[:, n % 4, :], gates[:, k, b:b + 1], x[:, b, :],
                                               ALU.mult, ALU.add).then_inc(added, 1)
    st.end()


def build(nc, dram, dump=None, until=None):
    with ExitStack() as ctx:
        core = Core(nc, dram, ctx)
        load_constants(core)
        first_block(core, dump)
        with nc.sbuf_tensor("rope_table", [P, T], F32) as table:
            rope_tables(core, table)
            source = dram["x_block"]
            for l in range(2):
                mix_layer(core, l, table, source, dram[f"x_mixed{l}"], dump)
                source = dram[f"x_mixed{l}"]
                if l == 0:
                    dense_ffn(core, source, dram["x_ffn"])
                    source = dram["x_ffn"]
            expert_ffn(core, source, dram["out"])


def dense_ffn(core, source, out):
    nc, d = core.nc, core.dram
    with nc.sbuf_tensor("ffn_x", [P, NT, D], F32) as x:
        norm_rows(core, "ffn_norm", x, d["dense_g"], d["h_rows"], source)
    swiglu_passes(core, "dense", DFF // P, d["dense"], out, residual=source)


def expert_ffn(core, source, out):
    nc, d = core.nc, core.dram
    with nc.sbuf_tensor("gates", [P, 2, NT], F32) as gates, nc.sbuf_tensor("slots", [P, 2, NT], U32) as slots, \
            nc.sbuf_tensor("experts_of", [P, NPASS + 1], U32) as experts, nc.sbuf_tensor("tiles", [P, NPASS + 1], U32) as tiles:
        with nc.sbuf_tensor("moe_xT", [P, KD, T], F32) as xT, nc.sbuf_tensor("moe_x", [P, NT, D], F32) as x:
            norm_transpose(core, "moe_norm", x, xT, "ffn1", source)
            norm_rows(core, "moe_rows", x, d["ffn_g"], d["h_rows"])
            route(core, xT, gates, slots, experts, tiles)
        swiglu_passes(core, "experts", EFF // P, d["experts"], d["y_slot"], experts, tiles)
        with nc.sbuf_tensor("moe_y", [P, NT, D], F32) as x:
            combine(core, x, source, gates, slots)
            norm_rows(core, "final_norm", x, d["final_norm"], out)


def split_tensors(core, stack, name, shape):
    return tuple(stack.enter_context(core.nc.sbuf_tensor(f"{name}_{part}", shape, F32R)) for part in ("high", "low"))


def mix_layer(core, l, table, source, out, dump):
    nc, d = core.nc, core.dram
    with ExitStack() as s1:
        sb = lambda name, shape: s1.enter_context(nc.sbuf_tensor(f"{name}{l}", shape, F32))
        mixT = sb("mixT", [P, 8, T])
        with ExitStack() as s2:
            sb2 = lambda name, shape: s2.enter_context(nc.sbuf_tensor(f"{name}{l}", shape, F32))
            z = sb2("z", [P, 4, T])
            qk = sb2("qk", [P, 2, 4, T])
            inputs = as_rows(mixT[:, 0:4, :])
            with ExitStack() as s3:
                xT = split_tensors(core, s3, f"xT{l}", [P, KD, T])
                norm_transpose(core, f"mix_norm{l}", as_rows(qk[:, :, :, :].rearrange("p a j n -> p (a j) n")), xT, f"mix{l}", source)
                projections(core, f"proj{l}", d[f"w_in{l}"], xT,
                            [(6, ACT.Copy, None, d["spill_down"]), (4, ACT.Silu, lambda n: at(qk[:, 0], n), None),
                             (4, ACT.Copy, lambda n: at(z, n), None), (4, ACT.Silu, lambda n: at(mixT[:, 4:8], n), None)])
                product_rows(core, f"inputs{l}", xT, KD, d[f"w_hi{l}"], 1, inputs)
            gates_of_layer(core, f"gates{l}", l, qk, z)
            log_decays = sb2("log_decays", [P, NT, HALF])
            transposed_blocks(core, f"decay_rows{l}", [(log_decays[:, b, j * P:(j + 1) * P], z[:, j, b * P:(b + 1) * P])
                                                       for b in range(NT) for j in range(4)])
            gated_chunks(core, f"gated{l}", qk, log_decays, inputs, z)
            head_norm_gate(core, f"gated_norm{l}", z[:, :, :], core.v(f"hgn{l}", 0), mixT[:, 4:8, :])
        with ExitStack() as s2:
            sb2 = lambda name, shape: s2.enter_context(nc.sbuf_tensor(f"{name}{l}", shape, F32))
            turned = sb2("turned", [64, 5, T])
            down = sb2("down", [P, 6, T])
            values = sb2("values", [P, NT, HALF])
            queries = sb2("queries", [P, 8, T])
            nope = queries[:, 0:4, :]
            keys = sb2("keys", [P, 4, T])
            load(core, f"load_down{l}", [(down[:, :, :], d["spill_down"])])
            channel_norms(core, f"mla_norms{l}", down, [((0, 1, 2), 384, 1e-6, f"qa{l}", None),
                                                        ((3, 4), 256, 1e-6, f"kva{l}", None)])
            gemm_t(core, f"up_q{l}", d[f"w_q{l}"], 8, 3, down, lambda n: at(queries, n))
            rotate(core, f"rotate{l}", [queries[:, 4 + j, :] for j in range(4)] + [down[:, 5, :]], table, turned)
            gemm_t(core, f"up_k{l}", d[f"w_k{l}"], 4, 2, down[:, 3:5], lambda n: at(keys, n))
            product_rows(core, f"up_v{l}", down[:, 3:5, :], 2, d[f"w_v{l}"], 1, values)
            qbuf = down[:, 0:2, :]
            vbuf = down[:, 2:4, :].rearrange("p u (b n) -> p u b n", b=NT)
            rbuf = down[0:64, 4:6, :]
            attention(core, f"mla{l}", 4,
                      lambda n, u: [(qbuf[:, u, :], at(nope, n)), (rbuf[:, u, :], at(turned, n)),
                                    (vbuf[:, u, :, :], values[:, :, bass.ds(n * P, P)])],
                      lambda u, b, n: [(qbuf[:, u, b * P:(b + 1) * P], at(keys, n)),
                                       (rbuf[:, u, b * P:(b + 1) * P], turned[:, 4, :])],
                      lambda u, j: vbuf[:, u, j, :],
                      lambda b: core.c("causal")[:, T - (b + 1) * P:T], 192 ** -0.5, mixT[:, 0:4, :])
        if dump:
            dump(core, f"mix{l}", mixT[:, :, :].rearrange("p a n -> p (a n)"))
        x = sb("x_out", [P, NT, D])
        product_rows(core, f"out_proj{l}", mixT, 8, d[f"w_out{l}"], 2, x, source, out)


def as_rows(x):
    return x.rearrange("p a n -> p (a n)").rearrange("p (b n) -> p b n", b=NT)


def first_block(core, dump):
    nc, d = core.nc, core.dram
    with nc.sbuf_tensor("index_weight", [P, NT, IDX_HEADS], F32) as weight:
        with nc.sbuf_tensor("big", [P, 5, 4, T], F32) as big, nc.sbuf_tensor("small", [P, T], F32) as small:
            flat = big[:, :, :, :].rearrange("p a j n -> p (a j) n")
            with ExitStack() as s2:
                xT = split_tensors(core, s2, "xT", [P, KD, T])
                norm_transpose(core, "norm_in", as_rows(flat[:, 0:8, :]), xT, "norm_g", d["x"])
                projections(core, "proj", d["w_in"], xT,
                            [(4, ACT.Copy, lambda n: at(flat, n + 4), None), (8, ACT.Copy, lambda n: at(flat, n + 12), None),
                             (4, ACT.Silu, None, d["spill_gate"]), (4, ACT.Copy, None, d["spill_down"]),
                             (4, ACT.Silu, None, d["spill_gate2"]), (1, ACT.Copy, lambda n: small[:, :], None)])
            index_weights(core, small, weight)
            shift_tokens(core, big, small)
            with nc.sbuf_tensor("space", [P, 8, T], F32) as space, nc.sbuf_tensor("bonus", [P, 4, T], F32) as bonus,                     nc.sbuf_tensor("decay_end", [P, 4, NCH], F32) as decay_end:
                rwkv_operands(core, big, small, decay_end, bonus, space[:, 0:4], space[:, 4:8])
                rwkv_chunks(core, big, decay_end, space)
                gate = big[:, 0]
                load(core, "load_gate", [(gate, d["spill_gate"])])
                rwkv_output(core, big, gate, bonus, space)
                load(core, "store_rwkv", [(d["spill_rwkv"], space[:, 0:4, :])])
        with nc.sbuf_tensor("mixT", [P, 8, T], F32) as mixT:
            index_attention(core, weight, mixT)
            if dump:
                dump(core, "mixT", mixT[:, :, :].rearrange("p a n -> p (a n)"))
            with nc.sbuf_tensor("x_res", [P, NT, D], F32) as x:
                product_rows(core, "out_proj", mixT, 8, d["w_out"], 2, x, d["x"])
                norm_rows(core, "block_norm", x, d["final_g"], d["x_block"])
                if dump:
                    dump(core, "x1", x[:, :, :].rearrange("p a n -> p (a n)"))


def index_attention(core, weight, mixT):
    nc, d = core.nc, core.dram
    with ExitStack() as s:
        sb = lambda name, shape: s.enter_context(nc.sbuf_tensor(name, shape, F32))
        down = sb("down", [P, 4, T])
        gate = mixT[:, 4:8, :]
        load(core, "load_down", [(down[:, :, :], d["spill_down"][:, 0:4, :]), (mixT[:, 0:4, :], d["spill_rwkv"]),
                                 (gate, d["spill_gate2"])])
        channel_norms(core, "latent_norms", down, [((0, 1), 256, 1e-6, "q_norm_g", None),
                                                   ((2,), 128, 1e-6, "kv_norm_g", None),
                                                   ((3,), 64, 1e-5, "kidx_g", "kidx_b")])
        queries = sb("queries", [P, 6, T])
        gemm_t(core, "up_q", d["w_uq"], 6, 2, down, lambda n: at(queries, n))
        latent = sb("latent", [P, NT, P])
        blk = lambda x, b: x[:, b * P:(b + 1) * P]
        transposed_blocks(core, "latent_rows", [(latent[:, b, :], blk(down[:, 2, :], b)) for b in range(NT)])
        masks = sb("masks", [P, offset(NT)])
        index_masks(core, queries[:, 4:6, :], down[:, 3, :], weight, masks)
        w_uk = sb("uk", [P, 4, P])
        w_uv = sb("uv", [P, 8, P])
        load(core, "absorb_w", [(w_uk[:, :, :], d["w_uk"]), (w_uv[:, :, :], d["w_uv"])])
        q_abs = sb("q_abs", [P, 8, T])
        half = lambda x, h: x[64 * (h % 2):64 * (h % 2) + 64, h // 2, :]
        pair_products(core, "absorb", lambda n: q_abs[:, n, :], [[(half(w_uk, h), half(queries, h))] for h in range(8)],
                      scale=0.125)
        o_lat = sb("o_lat", [P, 8, T])
        qbuf = queries[:, 0:2, :]
        attention(core, "dsa", 8, lambda n, u: [(qbuf[:, u, :], at(q_abs, n))],
                  lambda u, b, n: [(qbuf[:, u, b * P:(b + 1) * P], down[:, 2, :])],
                  lambda u, j: latent[:, j, :],
                  lambda b: masks[:, offset(b):offset(b + 1)] if b * P >= TOPK else core.c("causal")[:, T - (b + 1) * P:T],
                  1.0, o_lat)
        pair_products(core, "values_up", lambda n: mixT[:, 4 + n, :],
                      [[(w_uv[:, 2 * r, :], o_lat[:, 2 * r, :]), (w_uv[:, 2 * r + 1, :], o_lat[:, 2 * r + 1, :])]
                       for r in range(4)], gate=lambda n: gate[:, n, :])


def index_weights(core, small, weight):
    nc = core.nc
    st = Stage(core, "index_w")
    turned = st.sem("turned")
    with nc.Block("index_w") as block:
        @block.tensor
        def _(pe):
            for b in range(NT):
                last = nc.tensor.transpose(core.ps[:, b // 4, (b % 4) * P:(b % 4 + 1) * P], small[:, b * P:(b + 1) * P], core.c("eye"))
            last.then_inc(turned, 1)

        @block.scalar
        def _(act):
            act.wait_ge(turned, 1)
            for b in range(NT):
                o = (b % 4) * P + 64
                nc.scalar.activation(weight[:, b, :], core.ps[:, b // 4, o:o + IDX_HEADS], ACT.Copy, scale=IDX_HEADS ** -0.5)
    st.end()


def blocks_of(w, cols=P):
    k, n = w.shape
    return np.ascontiguousarray(w.reshape(k // P, P, n // cols, cols).transpose(2, 1, 0, 3).reshape(n // cols, P, (k // P) * cols))


def rows_of(w):
    k, n = w.shape
    return np.ascontiguousarray(w.reshape(k // P, P, n).transpose(1, 0, 2))


def padded(w):
    return np.concatenate([w, np.zeros((w.shape[0], -w.shape[1] % P), w.dtype)], 1)


def constants():
    c = np.zeros((P, NCST), np.float32)
    p = np.arange(P)[:, None]
    q = np.arange(64)[:, None]

    def put(name, value):
        o, w = CST[name]
        value = np.asarray(value, np.float32)
        c[:value.shape[0], o:o + w] = value
    put("eye", np.eye(P))
    put("ones", np.ones((P, P)))
    put("heads", (p // 64) == (np.arange(P)[None] // 64))
    n = np.arange(64)[None]
    put("upto", p % 64 <= n)
    put("before", p % 64 < n)
    lev = [((q >> (l + 1)) == (n >> (l + 1))) & (((q >> l) & 1) == 1) & (((n >> l) & 1) == 0) for l in range(LEVELS)]
    put("restart", np.broadcast_to((np.arange(T) % CH != 0), (P, T)))
    put("causal", np.where(np.arange(T)[None] - (T - P) <= p, 0.0, NEG))
    put("decaylevel", np.tile(np.concatenate([x.T for x in lev] + [q == n], 1), (2, 1)))
    put("earlier", p < np.arange(P)[None])
    put("iota8", np.broadcast_to(np.arange(8), (P, 8)))
    put("tok", p + P * np.arange(8)[None])
    put("fold", (p % 64) == n)
    u, t = np.arange(64)[:, None], np.arange(64)[None]
    groups = []
    for l in range(LEVELS):
        mid = (t >> (l + 1) << (l + 1)) + (1 << l) - 1
        groups.append(((u > mid) & (u <= t)) | ((u > t) & (u <= mid)))
    put("spans", np.concatenate(groups + [u <= t, u > t], 1))
    put("pass", np.broadcast_to(np.arange(NPASS + 1), (P, NPASS + 1)))
    return c


def laid_out(a):
    out = {"x": a["x"][0], "constants": constants()}
    w = a["w_in"][0]
    s, g = 1600, 2112
    w_in = np.concatenate([w[:, 0:1536], w[:, 1600:2112], w[:, 2112:2368], w[:, 2368:2496], w[:, 2496:2560], w[:, 2496:2560],
                           w[:, 2564:3076], padded(np.concatenate([w[:, 1536:1600], w[:, 2560:2564]], 1))], 1)
    out["w_in"] = blocks_of(w_in)
    z = np.zeros((32, 512), np.float32)
    out["w_up"] = np.concatenate([a["w_up"][0], z], 0)
    out["a_up"] = np.concatenate([z, a["a_up"][0]], 0)
    vec = np.zeros((P, NVEC), np.float32)

    def put(name, value):
        o, wd = VEC[name]
        value = np.asarray(value).reshape(-1)
        value = np.concatenate([value, np.zeros(wd * P - value.size, value.dtype)])
        vec[:, o:o + wd] = value.reshape(wd, P).T
    for name in ("norm_g", "w0", "a0", "k_k", "k_a", "r_k", "gn_g", "gn_b", "q_norm_g", "kv_norm_g"):
        put(name, a[name][0])
    put("mu", a["mu_shift"][0])
    put("kidx_g", np.concatenate([a["kidx_g"][0]] * 2))
    put("kidx_b", np.concatenate([a["kidx_b"][0]] * 2))
    for l in range(2):
        put(f"mix{l}", a["mix_norm_2"][l])
        put(f"ffn{l}", a["ffn_norm_2"][l])
        put(f"qa{l}", a["q_a_norm_2"][l])
        put(f"kva{l}", a["kv_a_norm_2"][l])
        put(f"hgn{l}", a["hg_out_norm_2"][l])
        put(f"lb{l}", a["hg_lower_bounds_2"][l])
    inv = (10000.0 ** (-np.arange(0, 64, 2) / 64.0)).astype(np.float32)
    put("inv", np.concatenate([inv] * 4))
    out["vectors"] = vec
    out["positions"] = a["positions_2"]
    for l in range(2):
        w = a["w_in_2"][l]
        pe = w[:, 640:704]
        swap = lambda x: np.concatenate([x[:, 32:], x[:, :32]], 1)
        out[f"w_in{l}"] = blocks_of(np.concatenate([w[:, 0:640], pe, swap(pe), w[:, 704:1728], w[:, 2240:2752]], 1))
        out[f"w_hi{l}"] = np.ascontiguousarray(w[:, 1728:2240])
        wq = a["w_q_b_2"][l].reshape(384, 4, 192)
        out[f"w_q{l}"] = blocks_of(np.concatenate([wq[:, h, 0:128] for h in range(4)] +
                                                  [x for h in range(4) for x in (wq[:, h, 128:], swap(wq[:, h, 128:]))], 1))
        wkv = a["w_kv_b_2"][l].reshape(256, 4, 2, 128)
        out[f"w_k{l}"] = blocks_of(np.ascontiguousarray(wkv[:, :, 0]).reshape(256, 512))
        out[f"w_v{l}"] = np.ascontiguousarray(wkv[:, :, 1]).reshape(256, 512)
        out[f"w_out{l}"] = a["w_out_2"][l]
    out["w_uq"] = blocks_of(np.concatenate([a["w_uq"][0], a["w_qidx"][0]], 1))
    out["w_uk"] = np.ascontiguousarray(a["w_uk"][0].transpose(2, 0, 1).reshape(64, 4, 2, P).transpose(2, 0, 1, 3).reshape(P, 4, P))
    uv = np.zeros((P, 8, P), np.float32)
    for h in range(8):
        uv[:, h, 64 * (h % 2):64 * (h % 2) + 64] = a["w_uv"][0][h]
    out["w_uv"] = uv
    out["w_out"] = a["w_out"][0]
    out["final_g"] = a["final_g"][None]
    out["final_norm"] = a["final_norm_2"][None]
    out["ffn_g"] = a["ffn_norm_2"][1:2]
    out["dense_g"] = a["ffn_norm_2"][0:1]
    out["router"] = rows_of(a["moe_router_2"][0])
    chunks = lambda gate, up, down: np.concatenate([blocks_of(gate), blocks_of(up), down.reshape(-1, P, D)], 2)
    out["dense"] = chunks(a["dense_w_gate_2"][0], a["dense_w_up_2"][0], a["dense_w_down_2"][0])
    out["experts"] = np.concatenate([chunks(*(a[f"moe_w_{x}_2"][0, e] for x in ("gate", "up", "down"))) for e in range(NEXP)])
    return out


def kernel(**inputs):
    import concourse.bacc as bacc
    from concourse.bass_utils import run_bass_kernel_spmd

    arrays = laid_out({name: np.asarray(value) for name, value in inputs.items()})
    nc = bacc.Bacc("TRN2", target_bir_lowering=False, num_devices=1)
    dram = {name: nc.dram_tensor(name, a.shape, mybir.dt.from_np(a.dtype), kind="ExternalInput").ap()
            for name, a in arrays.items()}
    for name in ("x_block", "x_mixed0", "x_ffn", "x_mixed1", "h_rows"):
        dram[name] = nc.dram_tensor(name, (T, D), F32).ap()
    for name, blocks in (("spill_down", 6), ("spill_gate", 4), ("spill_gate2", 4), ("spill_rwkv", 4)):
        dram[name] = nc.dram_tensor(name, (P, blocks, T), F32).ap()
    dram["y_slot"] = nc.dram_tensor("y_slot", (NPASS * SLOTS, D), F32).ap()
    dram["slot_token"] = nc.dram_tensor("slot_token", ((NPASS + 1) * SLOTS, 1), U32).ap()
    dram["out"] = nc.dram_tensor("out", (T, D), F32, kind="ExternalOutput").ap()
    build(nc, dram)
    result = run_bass_kernel_spmd(nc, [arrays], core_ids=[0])
    return result.results[0]["out"].reshape(1, T, D)
```
